# Optimizing a Trainium2 kernel written in Bass

```python
import math
import jax
import jax.numpy as jnp
from jax import lax
import numpy as np

D_MODEL = 2048
BATCH = 1
SEQ = 256
DEPTH = 1

HEAD_DIM = 128
D_MIX = D_MODEL
N_MIX_HEADS = D_MIX // HEAD_DIM
RET_HEADS = N_MIX_HEADS // 4
GDN_HEADS = (N_MIX_HEADS - RET_HEADS) // 2
MOBA_HEADS = N_MIX_HEADS - RET_HEADS - GDN_HEADS
RET_W = RET_HEADS * HEAD_DIM
GDN_W = GDN_HEADS * HEAD_DIM
MOBA_W = MOBA_HEADS * HEAD_DIM
IN_WIDTH = 4 * RET_W + 4 * GDN_W + 2 * GDN_HEADS + 4 * MOBA_W
RET_CHUNK = 128
GDN_CHUNK = 64
GDN_CONV = 4
MOBA_BLOCK = 256
MOBA_TOP_K = 3
MOBA_Q_BLOCK = 64
RMS_EPS = 1e-6

kernel_name = 'hymba_style_retention_gdn_moba_block'

def rms_norm(x, w):
    x32 = x.astype(jnp.float32)
    y = x32 * lax.rsqrt(jnp.mean(x32 * x32, axis=-1, keepdims=True) + RMS_EPS)
    return (y * w).astype(x.dtype)

def l2_norm(x):
    x32 = x.astype(jnp.float32)
    return (x32 * lax.rsqrt(jnp.sum(x32 * x32, axis=-1, keepdims=True) + RMS_EPS)).astype(x.dtype)

def to_heads(t, n_heads):
    b, s, _ = t.shape
    return t.reshape(b, s, n_heads, -1).transpose(0, 2, 1, 3)

def from_heads(t):
    b, h, s, d = t.shape
    return t.transpose(0, 2, 1, 3).reshape(b, s, h * d)

def causal_depthwise_conv(x, w):
    k, c = w.shape
    return lax.conv_general_dilated(x, w[:, None, :].astype(x.dtype), window_strides=(1,),
                                    padding=[(k - 1, 0)], dimension_numbers=('NWC', 'WIO', 'NWC'),
                                    feature_group_count=c)

def retention(q, k, v):
    in_dtype = v.dtype
    q, k, v = (t.astype(jnp.float32) for t in (q, k, v))
    b, h, s, d = q.shape
    c = RET_CHUNK
    n = s // c
    q = q.reshape(b, h, n, c, d)
    k = k.reshape(b, h, n, c, d)
    v = v.reshape(b, h, n, c, d)
    log_gamma = jnp.log1p(-jnp.exp2(-5.0 - jnp.arange(h, dtype=jnp.float32)))[:, None]
    pos = jnp.arange(c, dtype=jnp.float32)
    diff = pos[:, None] - pos[None, :]
    decay_mat = jnp.where(diff >= 0, jnp.exp(jnp.maximum(diff, 0.0) * log_gamma[:, :, None]), 0.0)
    scores = jnp.einsum('bhncd,bhnsd->bhncs', q, k) * decay_mat[None, :, None]
    intra = jnp.einsum('bhncs,bhnse->bhnce', scores, v)
    k_w = k * jnp.exp((c - 1 - pos) * log_gamma)[None, :, None, :, None]
    kv = jnp.einsum('bhncd,bhnce->nbhde', k_w, v)
    chunk_decay = jnp.exp(c * log_gamma)[:, :, None]

    def step(state, kv_n):
        return state * chunk_decay + kv_n, state

    _, s_prev = lax.scan(step, jnp.zeros((b, h, d, d), jnp.float32), kv)
    q_w = q * jnp.exp((pos + 1.0) * log_gamma)[None, :, None, :, None]
    cross = jnp.einsum('bhncd,nbhde->bhnce', q_w, s_prev)
    return (intra + cross).reshape(b, h, s, d).astype(in_dtype)

def gated_delta_rule(q, k, v, g, beta):
    in_dtype = v.dtype
    q, k, v, g, beta = (t.astype(jnp.float32) for t in (q, k, v, g, beta))
    b, h, s, d = q.shape
    c = GDN_CHUNK
    n = s // c
    q = q.reshape(b, h, n, c, d)
    k = k.reshape(b, h, n, c, d)
    v = v.reshape(b, h, n, c, d)
    g_cum = jnp.cumsum(g.reshape(b, h, n, c), axis=-1)
    beta = beta.reshape(b, h, n, c)
    causal = jnp.tril(jnp.ones((c, c), dtype=bool))
    strict = jnp.tril(jnp.ones((c, c), dtype=bool), -1)
    decay = jnp.exp(jnp.where(causal, g_cum[..., :, None] - g_cum[..., None, :], -jnp.inf))
    k_beta = k * beta[..., None]
    m = jnp.where(strict, jnp.einsum('bhncd,bhnsd->bhncs', k_beta, k) * decay, 0.0)
    rhs = jnp.concatenate([k_beta * jnp.exp(g_cum)[..., None], v * beta[..., None]], axis=-1)
    wu = lax.linalg.triangular_solve(m + jnp.eye(c, dtype=jnp.float32), rhs, left_side=True,
                                     lower=True, unit_diagonal=True)
    w, u = wu[..., :d], wu[..., d:]
    qk = jnp.einsum('bhncd,bhnsd->bhncs', q, k) * decay
    q_g = q * jnp.exp(g_cum)[..., None]
    g_last = g_cum[..., -1]
    k_g = k * jnp.exp(g_last[..., None] - g_cum)[..., None]

    def step(state, inp):
        q_n, k_n, w_n, u_n, qk_n, gl_n = inp
        v_new = u_n - jnp.einsum('bhcd,bhde->bhce', w_n, state)
        o = jnp.einsum('bhcd,bhde->bhce', q_n, state) + jnp.einsum('bhcs,bhse->bhce', qk_n, v_new)
        state = state * jnp.exp(gl_n)[..., None, None] + jnp.einsum('bhcd,bhce->bhde', k_n, v_new)
        return state, o

    xs = tuple(jnp.moveaxis(t, 2, 0) for t in (q_g, k_g, w, u, qk, g_last))
    _, o = lax.scan(step, jnp.zeros((b, h, d, d), jnp.float32), xs)
    return jnp.moveaxis(o, 0, 2).reshape(b, h, s, d).astype(in_dtype)

def moba_attention(q, k, v):
    b, h, s, d = q.shape
    n_blocks = -(-s // MOBA_BLOCK)
    s_pad = n_blocks * MOBA_BLOCK
    pad = ((0, 0), (0, 0), (0, s_pad - s), (0, 0))
    q, k, v = jnp.pad(q, pad), jnp.pad(k, pad), jnp.pad(v, pad)
    k_blocks = k.reshape(b, h, n_blocks, MOBA_BLOCK, d)
    v_blocks = v.reshape(b, h, n_blocks, MOBA_BLOCK, d)
    k_mean = jnp.mean(k_blocks.astype(jnp.float32), axis=3)
    k_sel = min(MOBA_TOP_K, n_blocks)
    scale = d ** -0.5
    slopes = jnp.exp2(-8.0 * jnp.arange(1, h + 1, dtype=jnp.float32) / h)
    bi = jnp.arange(b)[:, None, None, None]
    hi = jnp.arange(h)[None, :, None, None]
    blk_off = jnp.arange(MOBA_BLOCK)

    def one_query_block(i):
        start = i * MOBA_Q_BLOCK
        own = start // MOBA_BLOCK
        qc = lax.dynamic_slice_in_dim(q, start, MOBA_Q_BLOCK, axis=2)
        qpos = start + jnp.arange(MOBA_Q_BLOCK)
        gate = jnp.einsum('bhqd,bhnd->bhqn', qc.astype(jnp.float32), k_mean)
        gate = jnp.where(jnp.arange(n_blocks) < own, gate, -jnp.inf)
        gval, gidx = lax.top_k(gate, k_sel)
        sel_ok = jnp.isfinite(gval)
        k_g = k_blocks[bi, hi, gidx]
        kpos = gidx[..., None] * MOBA_BLOCK + blk_off
        dist_sel = (qpos[None, None, :, None, None] - kpos).astype(jnp.float32)
        s_sel = (jnp.einsum('bhqd,bhqjsd->bhqjs', qc, k_g).astype(jnp.float32) * scale
                 - slopes[None, :, None, None, None] * dist_sel)
        s_sel = jnp.where(sel_ok[..., None], s_sel, -jnp.inf)
        own_k = lax.dynamic_slice_in_dim(k, own * MOBA_BLOCK, MOBA_BLOCK, axis=2)
        own_v = lax.dynamic_slice_in_dim(v, own * MOBA_BLOCK, MOBA_BLOCK, axis=2)
        own_pos = own * MOBA_BLOCK + blk_off
        dist_own = (qpos[:, None] - own_pos[None, :]).astype(jnp.float32)
        s_own = (jnp.einsum('bhqd,bhsd->bhqs', qc, own_k).astype(jnp.float32) * scale
                 - slopes[:, None, None] * dist_own)
        s_own = jnp.where(own_pos[None, :] <= qpos[:, None], s_own, -jnp.inf)
        logits = jnp.concatenate([s_sel.reshape(b, h, MOBA_Q_BLOCK, k_sel * MOBA_BLOCK), s_own], axis=-1)
        p = jax.nn.softmax(logits, axis=-1)
        p_sel = p[..., :k_sel * MOBA_BLOCK].reshape(b, h, MOBA_Q_BLOCK, k_sel, MOBA_BLOCK)
        p_own = p[..., k_sel * MOBA_BLOCK:]
        v_g = v_blocks[bi, hi, gidx]
        o = jnp.einsum('bhqjs,bhqjsd->bhqd', p_sel, v_g) + jnp.einsum('bhqs,bhsd->bhqd', p_own, own_v)
        return o.astype(q.dtype)

    out = lax.map(one_query_block, jnp.arange(s_pad // MOBA_Q_BLOCK))
    out = jnp.moveaxis(out, 0, 2).reshape(b, h, s_pad, d)
    return out[:, :, :s]

def hybrid_layer(x, norm_w, w_in, conv_w, a_log, dt_bias, ret_norm_w, gdn_norm_w, q_norm_w, k_norm_w, w_out):
    h = rms_norm(x, norm_w)
    proj = jnp.einsum('btd,de->bte', h, w_in)
    sizes = (RET_W,) * 4 + (3 * GDN_W, GDN_W, GDN_HEADS, GDN_HEADS) + (MOBA_W,) * 4
    offsets = [int(o) for o in np.cumsum(sizes)[:-1]]
    rq, rk, rv, rg, gqkv, gz, ga, gb, mq, mk, mv, mz = jnp.split(proj, offsets, axis=-1)

    o_ret = retention(to_heads(rq, RET_HEADS), to_heads(rk, RET_HEADS) * HEAD_DIM ** -0.5,
                      to_heads(rv, RET_HEADS))
    y_ret = from_heads(rms_norm(o_ret, ret_norm_w[:, None, :])) * jax.nn.silu(rg)

    qkv = jax.nn.silu(causal_depthwise_conv(gqkv, conv_w))
    gq, gk, gv = jnp.split(qkv, 3, axis=-1)
    gq = l2_norm(to_heads(gq, GDN_HEADS)) * HEAD_DIM ** -0.5
    gk = l2_norm(to_heads(gk, GDN_HEADS))
    gv = to_heads(gv, GDN_HEADS)
    beta = jax.nn.sigmoid(gb.astype(jnp.float32)).transpose(0, 2, 1)
    g = (-jnp.exp(a_log.astype(jnp.float32))
         * jax.nn.softplus(ga.astype(jnp.float32) + dt_bias.astype(jnp.float32))).transpose(0, 2, 1)
    o_gdn = gated_delta_rule(gq, gk, gv, g, beta)
    y_gdn = from_heads(rms_norm(o_gdn, gdn_norm_w)) * jax.nn.silu(gz)

    mq = rms_norm(to_heads(mq, MOBA_HEADS), q_norm_w)
    mk = rms_norm(to_heads(mk, MOBA_HEADS), k_norm_w)
    o_moba = moba_attention(mq, mk, to_heads(mv, MOBA_HEADS))
    y_moba = from_heads(o_moba) * jax.nn.silu(mz)

    y = jnp.concatenate([y_ret, y_gdn, y_moba], axis=-1)
    return x + jnp.einsum('bte,ed->btd', y, w_out).astype(x.dtype)

def setup_inputs(seed: int = 0) -> dict:
    key = jax.random.key(seed)
    ks = jax.random.split(key, 12)
    f32 = jnp.float32
    x = jax.random.normal(ks[0], (BATCH, SEQ, D_MODEL), f32)
    norm_w = 1.0 + 0.02 * jax.random.normal(ks[1], (DEPTH, D_MODEL), f32)
    w_in = jax.random.normal(ks[2], (DEPTH, D_MODEL, IN_WIDTH), f32) * D_MODEL ** -0.5
    conv_w = jax.random.normal(ks[3], (DEPTH, GDN_CONV, 3 * GDN_W), f32) * GDN_CONV ** -0.5
    a_log = jnp.log(jax.random.uniform(ks[4], (DEPTH, GDN_HEADS), f32, minval=1.0, maxval=16.0))
    dt = jnp.exp(jax.random.uniform(ks[5], (DEPTH, GDN_HEADS), f32,
                                    minval=math.log(1e-3), maxval=math.log(0.1)))
    dt_bias = dt + jnp.log(-jnp.expm1(-dt))
    ret_norm_w = 1.0 + 0.02 * jax.random.normal(ks[6], (DEPTH, RET_HEADS, HEAD_DIM), f32)
    gdn_norm_w = 1.0 + 0.02 * jax.random.normal(ks[7], (DEPTH, HEAD_DIM), f32)
    q_norm_w = 1.0 + 0.02 * jax.random.normal(ks[8], (DEPTH, HEAD_DIM), f32)
    k_norm_w = 1.0 + 0.02 * jax.random.normal(ks[9], (DEPTH, HEAD_DIM), f32)
    w_out = jax.random.normal(ks[10], (DEPTH, D_MIX, D_MODEL), f32) * D_MIX ** -0.5
    return {'x': x, 'norm_w': norm_w, 'w_in': w_in, 'conv_w': conv_w, 'a_log': a_log,
            'dt_bias': dt_bias, 'ret_norm_w': ret_norm_w, 'gdn_norm_w': gdn_norm_w,
            'q_norm_w': q_norm_w, 'k_norm_w': k_norm_w, 'w_out': w_out}

def reference(x, norm_w, w_in, conv_w, a_log, dt_bias, ret_norm_w, gdn_norm_w, q_norm_w, k_norm_w, w_out):
    for layer in range(DEPTH):
        x = hybrid_layer(x, norm_w[layer], w_in[layer], conv_w[layer], a_log[layer], dt_bias[layer],
                         ret_norm_w[layer], gdn_norm_w[layer], q_norm_w[layer], k_norm_w[layer],
                         w_out[layer])
    return x


_drawn_inputs = setup_inputs


def setup_inputs(seed=0):
    import zlib

    import numpy as np

    out = dict(_drawn_inputs(seed))
    spreads = {}
    factors = {'norm_w': 3.392, 'ret_norm_w': 8.0, 'gdn_norm_w': 8.0, 'q_norm_w': 8.0, 'k_norm_w': 8.0}
    for name, (base, spread) in spreads.items():
        noise = np.random.default_rng([zlib.crc32(name.encode()), seed]).standard_normal(out[name].shape)
        drawn = base * np.exp(spread * noise) if base else spread * noise
        out[name] = jnp.asarray(drawn.astype(out[name].dtype))
    for name, factor in factors.items():
        out[name] = (out[name] * factor).astype(out[name].dtype)
    return out
```

```python
from contextlib import ExitStack

import numpy as np

import concourse.bass as bass
from concourse import mybir

F32 = mybir.dt.float32
F32R = mybir.dt.float32r
ALU = mybir.AluOpType
ACT = mybir.ActivationFunctionType
AX = mybir.AxisListType

P = 128
D = 2048
T = 256
C = T // P
KC = D // P
RET, GDN, MOBA = 4, 6, 6
RET_COL = 0
GDN_COL = 4 * RET * P
AB_COL = GDN_COL + 4 * GDN * P
MOBA_COL = AB_COL + 2 * GDN
AB = 2 * GDN
EPS = 1e-6
SCALE = float(P) ** -0.5
CONV = 4
PAD = CONV - 1

TK = 2
TPH = KC // TK
UPT = 4 * TK
HEADS = RET + GDN + MOBA
GROUPS = HEADS + D // 512
NRAW, NSPLIT, LEAD = 8, 4, 3
TILES = GROUPS * TPH

PAIRS = [("gdn", 0), ("gdn", 1), ("gdn", 2), ("ret", 0), ("ret", 1), ("moba", 0), ("moba", 1), ("moba", 2)]
Y_BLOCK = {"ret": 0, "gdn": RET, "moba": RET + GDN}
VEC_LO = (3, 7)

LEVELS = 7

K_ID, K_UP, K_ONE = 0, P, 2 * P
K_POW = 3 * P
K_FIRST = K_POW + 8
K_LEVEL = K_FIRST
K_DECAY = K_LEVEL + LEVELS * P
K_DIST = K_DECAY + RET * P
K_KDEC = K_DIST + 3 * P
K_QDEC = K_KDEC + RET
K_COLS = K_QDEC + RET

R_CONV = 0
R_NORM = R_CONV + CONV * 3 * GDN
R_RET = R_NORM + KC
R_GDN = R_RET + RET
R_Q = R_GDN + 1
R_K = R_Q + 1
R_ROWS = R_K + 1

U_GDN = {"gram": 30, "vtok": 34}
for _l in range(LEVELS):
    U_GDN[f"x{_l}"] = 38 + 10 * _l
    U_GDN[f"y{_l}"] = 41 + 10 * _l
    U_GDN[f"t{_l}"] = 44 + 10 * _l
U_GDN.update(v0=105, s1=108, ks=111, v1=115, o=119, tr=124)
U_RET = {"gram": 6, "s1": 12, "qs": 18, "o": 18, "tr": 36}
U_MOBA = {"nrm": 6, "bc": 14, "score": 22, "pt": 40, "o": 48}


def constants():
    t = np.zeros((P, K_COLS), np.float64)
    p, c = np.arange(P)[:, None], np.arange(P)[None, :]
    t[:, K_ID:K_ID + P] = p == c
    t[:, K_UP:K_UP + P] = p <= c
    t[:, K_ONE:K_ONE + P] = 1
    for l in range(LEVELS):
        b = 2 ** l
        t[:, K_LEVEL + l * P:K_LEVEL + (l + 1) * P] = ((p // b) % 2 == 1) & (c // b == p // b - 1)
    for h in range(RET):
        lg = np.log1p(-2.0 ** (-5.0 - h))
        t[:, K_DECAY + h * P:K_DECAY + (h + 1) * P] = np.where(c >= p, np.exp(np.maximum(c - p, 0) * lg), 0) * SCALE
        t[:, K_KDEC + h] = np.exp((P - 1 - np.arange(P)) * lg) * SCALE
        t[:, K_QDEC + h] = np.exp((np.arange(P) + 1) * lg)
    s = np.arange(2 * P)[None, :]
    t[:, K_DIST:K_DIST + P] = np.where(c <= p, c - p, -1e30)
    t[:, K_DIST + P:K_DIST + 3 * P] = np.where(s <= p + P, s - p - P, -1e30)
    t[:, K_POW:K_POW + 8] = -0.5
    return t.astype(np.float32)


def layer(nc, x, norm_w, w_in, conv_w, a_log, dt_bias, ret_norm_w, gdn_norm_w, q_norm_w, k_norm_w, w_out,
          table, out):
    ctx = ExitStack()
    with ctx:
        def sb(name, shape, dt=F32):
            return ctx.enter_context(nc.sbuf_tensor(name, shape, dt))

        sems = {}

        def S(name):
            if name not in sems:
                sems[name] = ctx.enter_context(nc.semaphore(name))
            return sems[name]

        w_raw = sb("w_raw", [P, NRAW, TK * 512])
        w_hi = sb("w_hi", [P, NSPLIT, TK * 512], F32R)
        w_lo = sb("w_lo", [P, NSPLIT, TK * 512], F32R)
        hT = sb("hT", [P, KC, 2, T], F32R)
        yT = sb("yT", [P, KC, 2, T], F32R)
        cst = sb("cst", [P, K_COLS])
        prow = sb("prow", [R_ROWS, P])
        pcol = sb("pcol", [P, R_ROWS])
        raw = sb("raw", [P, 2, 4, PAD + T])
        ev_lo = sb("ev_lo", [P, 4, T])
        cv = sb("cv", [P, 2 * 3 * T])
        th = sb("th", [P, 2 * 3 * T])
        kq = sb("kq", [P, 2, C, 2, P])
        sq = sb("sq", [P, 2, C, 2, P])
        vT = sb("vT", [P, 2, T])
        zg = sb("zg", [P, 2, T])
        dd = sb("dd", [P, 4, P])
        ee = sb("ee", [P, 4, P])
        er = sb("er", [P, 4, P])
        mT = sb("mT", [P, 4, P])
        aT = sb("aT", [P, 4, P])
        vr = sb("vr", [P, 4, P])
        ktok = sb("ktok", [P, 2, P])
        gm = sb("gm", [P, 4, P])
        gt = sb("gt", [P, 4, P])
        xs = sb("xs", [P, 4, P])
        v0 = sb("v0", [P, 2, P])
        v0s = sb("v0s", [P, 2, P])
        v1 = sb("v1", [P, 2, P])
        st = sb("st", [P, 2, P])
        os_ = sb("os", [P, 2, C, P])
        on = sb("on", [P, 2, C, P])
        yf = sb("yf", [P, 2, T])
        ab = sb("ab", [P, 24, C, GDN])
        wab = sb("wab", [P, KC, AB])
        wab_hi = sb("wab_hi", [P, KC, AB], F32R)
        wab_lo = sb("wab_lo", [P, KC, AB], F32R)
        bias = sb("bias", [P, 2, GDN])
        sm = sb("sm", [P, 128])

        pj = [ctx.enter_context(nc.psum_tensor(f"pj{s}", [P, 512], F32)) for s in range(4)]
        mx = [ctx.enter_context(nc.psum_tensor(f"mx{s}", [P, 512], F32)) for s in range(4)]

        ident = cst[:, K_ID:K_ID + P]
        upper = cst[:, K_UP:K_UP + P]
        ones = cst[:, K_ONE:K_ONE + P]
        x_sb = w_raw[:, NRAW // 2:, :].rearrange("p a n -> p (a n)").rearrange("p (c n) -> p c n", c=C)
        xn = cv[:, :], th[:, :]

        def four(ap):
            return ap.rearrange("p (n c) -> p n c", c=P)

        A_G, A_BETA, A_GC, A_NGC, A_EGC, A_NEGC, A_GL, A_Z, A_E, A_U, A_L, A_T1, A_T2, A_T3, A_ELAST, A_TB = range(16)

        def chunk_in(h, s, c):
            return raw[:, h, s, PAD + c * P:PAD + (c + 1) * P]

        def lo_count(n, vec):
            v = n // TPH * len(VEC_LO) + sum(q < n % TPH for q in VEC_LO)
            return v if vec else n - v

        def wait_lo(eng, n):
            if n % TPH in VEC_LO:
                eng.wait_ge(S("lo_vec"), lo_count(n + 1, True))
            else:
                eng.wait_ge(S("lo_pool"), lo_count(n + 1, False))

        def wait_used(eng, n):
            g, q = n // TPH, n % TPH
            if q < TPH - 1:
                eng.wait_ge(S("tile_used"), (TPH - 1) * g + q + 1)
            elif g < HEADS:
                eng.wait_ge(S("proj_done"), 4 * (g + 1))
            else:
                eng.wait_ge(S("out_psum"), 2 * (g + 1 - HEADS))

        def evacuated(v):
            head, rest = divmod(v + 6, 64)
            return (head - 1, rest // 2) if 0 < head <= HEADS and rest < 8 and rest % 2 == 0 else None

        def low_part(eng, n, name):
            eng.wait_ge(S("hi_done"), n + 1)
            eng.tensor_tensor(w_lo[:, n % NSPLIT, :], w_raw[:, n % NRAW, :],
                              w_hi[:, n % NSPLIT, :].bitcast(F32), ALU.subtract).then_inc(S(name), 1)

        block = ctx.enter_context(nc.Block())

        @block.sync
        def _(sp):
            sp.dma_start(x_sb[:, 0, :], x[0, 0:P, :]).then_inc(S("x0_in"), 16)
            sp.dma_start(prow[R_NORM:R_RET, :], norm_w[0].rearrange("(k p) -> k p", p=P)).then_inc(S("norm_in"), 16)
            sp.dma_start(cst[:, 0:K_FIRST], table[:, 0:K_FIRST]).then_inc(S("cst_in"), 16)
            sp.dma_start(x_sb[:, 1, :], x[0, P:T, :]).then_inc(S("x1_in"), 16)

            def load(n):
                group, q = n // TPH, n % TPH
                rows = slice(q * TK * P, (q + 1) * TK * P)
                if n >= NRAW:
                    wait_lo(sp, n - NRAW)
                elif n >= NRAW // 2:
                    sp.wait_ge(S("hT_psum"), KC)
                dst = w_raw[:, n % NRAW, :].rearrange("p (k n) -> p k n", k=TK)
                if group < HEADS:
                    kind, j = PAIRS[group // 2]
                    heads = {"gdn": GDN, "ret": RET, "moba": MOBA}[kind]
                    col = {"gdn": GDN_COL, "ret": RET_COL, "moba": MOBA_COL}[kind]
                    h = 2 * j + group % 2
                    src = w_in[0, rows, col:col + 4 * heads * P].rearrange(
                        "(k p) (s c) -> p k s c", p=P, s=4)[:, :, :, h * P:(h + 1) * P]
                    dst = dst.rearrange("p k (s c) -> p k s c", s=4)
                    for k in range(TK):
                        sp.dma_start(dst[:, k], src[:, k]).then_inc(S(f"w_in{n % NRAW}"), 16)
                else:
                    g = group - HEADS
                    src = w_out[0, rows, g * 512:(g + 1) * 512].rearrange("(k p) c -> p k c", p=P)
                    for k in range(TK):
                        sp.dma_start(dst[:, k], src[:, k]).then_inc(S(f"w_in{n % NRAW}"), 16)

            def load_x(n):
                g, c = n // 2, n % 2
                if n >= 3:
                    sp.wait_ge(S("out_ready"), n - 2)
                sp.dma_start(cv[:, (n % 3) * 512:(n % 3 + 1) * 512],
                             x[0, c * P:(c + 1) * P, g * 512:(g + 1) * 512]).then_inc(S(f"xr_in{n % 3}"), 16)

            for n in range(TILES):
                load(n)
                group = n // TPH - 1 - HEADS
                if group >= 0 and n % TPH == 3:
                    load_x(2 * group)
                    load_x(2 * group + 1)
                if n == NRAW // 2 - 1:
                    sp.dma_start(cst[:, K_FIRST:], table[:, K_FIRST:]).then_inc(S("cst_in2"), 16)
            load_x(6)
            load_x(7)

        @block.scalar
        def _(act):
            act.dma_start(prow[R_CONV:R_NORM, :], conv_w[0].rearrange("j (t c) -> (j t) c", c=P)).then_inc(S("param_in"), 16)
            act.dma_start(prow[R_RET:R_GDN, :], ret_norm_w[0]).then_inc(S("param_in1"), 16)
            act.dma_start(prow[R_GDN:R_Q, :], gdn_norm_w).then_inc(S("param_in2"), 16)
            act.dma_start(prow[R_Q:R_K, :], q_norm_w).then_inc(S("param_in3"), 16)
            act.dma_start(prow[R_K:R_ROWS, :], k_norm_w).then_inc(S("param_in4"), 16)
            act.dma_start(wab[:, :, :], w_in[0, :, AB_COL:AB_COL + AB].rearrange("(k p) c -> p k c", p=P)).then_inc(S("wab_in"), 16)
            act.dma_start(bias[:, 0, :], a_log[0:1, :].broadcast_to([P, GDN])).then_inc(S("bias_in"), 16)
            act.dma_start(bias[:, 1, :], dt_bias[0:1, :].broadcast_to([P, GDN])).then_inc(S("bias_in1"), 16)

            def high_part(n):
                act.wait_ge(S(f"w_in{n % NRAW}"), 16 * TK * (n // NRAW + 1))
                if n >= NSPLIT:
                    wait_used(act, n - NSPLIT)
                act.activation(w_hi[:, n % NSPLIT, :], w_raw[:, n % NRAW, :], ACT.Copy).then_inc(S("hi_done"), 1)

            def evacuate_low(g, s):
                act.wait_ge(S("proj_done"), 4 * g + s + 1)
                act.activation(ev_lo[:, s, :], pj[s][:, T:2 * T], ACT.Copy).then_inc(S("ev_lo_done"), 1)

            def send(n):
                g, c = n // 2, n % 2
                act.wait_ge(S("out_ready"), n + 1)
                act.dma_start(out[0, c * P:(c + 1) * P, g * 512:(g + 1) * 512],
                              sq[:, n % 2].rearrange("p c k t -> p (c k t)")).then_inc(S(f"out_sent{n % 2}"), 16)

            pos = [0]

            def advance(u):
                for v in range(pos[0], min(u, 64 * GROUPS)):
                    if evacuated(v):
                        evacuate_low(*evacuated(v))
                    if v % UPT == 0 and v // UPT + LEAD < TILES:
                        high_part(v // UPT + LEAD)
                    if v > 64 * HEADS and v % 64 == 0:
                        send(2 * (v // 64 - HEADS) - 2)
                        send(2 * (v // 64 - HEADS) - 1)
                pos[0] = max(pos[0], u)

            act.wait_ge(S("x0_in"), 16)
            act.activation(xn[0][:, 0:1024], x_sb[:, 0, 0:1024], ACT.Square, accum_out=sm[:, 0:1]).then_inc(S("ss_done"), 1)
            act.activation(xn[1][:, 0:1024], x_sb[:, 0, 1024:], ACT.Square, accum_out=sm[:, 1:2]).then_inc(S("ss_done"), 1)
            act.wait_ge(S("x1_in"), 16)
            act.wait_ge(S("ss_done"), 2)
            act.activation(xn[0][:, 0:1024], x_sb[:, 1, 0:1024], ACT.Square, accum_out=sm[:, 2:3]).then_inc(S("ss_done"), 1)
            act.activation(xn[1][:, 0:1024], x_sb[:, 1, 1024:], ACT.Square, accum_out=sm[:, 3:4]).then_inc(S("ss_done"), 1)
            for n in range(LEAD):
                high_part(n)
            act.wait_ge(S("wab_in"), 16)
            act.activation(wab_hi[:, :, :], wab[:, :, :], ACT.Copy).then_inc(S("wab_hi_done"), 1)
            act.wait_ge(S("pcol_done"), 1)
            for k in range(KC):
                act.wait_ge(S("hT_psum"), k + 1)
                act.activation(hT[:, k, 0, :], (pj + mx)[k % 8][:, 0:T], ACT.Copy,
                               scale=pcol[:, R_NORM + k:R_NORM + k + 1]).then_inc(S("h_hi"), 1)

            act.wait_ge(S("bias_in"), 16)
            act.activation(sm[:, 16:16 + GDN], bias[:, 0, :], ACT.Exp).then_inc(S("expa_done"), 1)
            act.wait_ge(S("ab_psum"), 1)
            act.activation(ab[:, A_TB], mx[0][:, 0:2 * AB].rearrange("p (c h) -> p c h", c=C)[:, :, GDN:], ACT.Tanh,
                           scale=0.5).then_inc(S("tanh_b"), 1)
            act.wait_ge(S("negabs_z"), 1)
            act.activation(ab[:, A_E], ab[:, A_T1], ACT.Exp).then_inc(S("exp_z"), 1)
            act.wait_ge(S("one_plus"), 1)
            act.activation(ab[:, A_L], ab[:, A_U], ACT.Ln).then_inc(S("ln_u"), 1)
            act.wait_ge(S("gc_done"), 1)
            act.activation(ab[:, A_EGC], ab[:, A_GC], ACT.Exp).then_inc(S("egc_done"), 1)
            act.activation(ab[:, A_ELAST, 0, :], ab[:, A_T2, 0, :], ACT.Exp).then_inc(S("egc_done"), 1)

            def gate_tanh(p):
                act.wait_ge(S("evac"), 8 * (p + 1))
                if p:
                    act.wait_ge(S("yf_done"), p)
                act.activation(zg[:, :, :], raw[:, :, 3, PAD:], ACT.Tanh, scale=0.5).then_inc(S("tanh_z"), 1)

            def split_y(p, y0):
                act.wait_ge(S("yf_done"), p + 1)
                act.activation(yT[:, y0:y0 + 2, 0, :], yf[:, :, :], ACT.Copy).then_inc(S("y_hi"), 1)

            def mix_gdn(p, j, base):
                U = {k: base + v for k, v in U_GDN.items()}
                advance(base + 12)
                th3, cv3 = (b[:, :].rearrange("p (h s t) -> p h s t", h=2, s=3) for b in (th, cv))
                for h in range(2):
                    advance(base + 12 + 6 * h)
                    act.wait_ge(S("conv_kq"), 2 * j + h + 1)
                    act.activation(th3[:, h, 0:2], cv3[:, h, 0:2], ACT.Tanh, scale=0.5).then_inc(S("tanh_kq"), 1)
                gate_tanh(p)
                act.wait_ge(S("clip_done"), 4 * (j + 1))
                act.activation(ee[:, :, :], dd[:, :, :], ACT.Exp).then_inc(S("exp_decay"), 1)
                act.wait_ge(S("conv_v"), 2 * j + 2)
                act.activation(th3[:, :, 2], cv3[:, :, 2], ACT.Tanh, scale=0.5).then_inc(S("tanh_v"), 1)
                advance(U["gram"])
                act.wait_ge(S("g_norm"), j + 1)
                act.activation(ktok[:, :, :], mx[3][:, 0:2 * P].rearrange("p (h c) -> p h c", h=2), ACT.Copy).then_inc(S("ktok"), 1)
                advance(U["vtok"])
                act.wait_ge(S("vtok"), j + 1)
                act.wait_ge(S("g_scalars"), j + 1)
                for n in range(4):
                    act.activation(vr[:, n, :], mx[2][:, n * P:(n + 1) * P], ACT.Copy,
                                   scale=sm[:, 40 + n:41 + n]).then_inc(S("vr"), 1)
                for l in range(LEVELS - 1):
                    advance(U[f"t{l}"])
                    act.wait_ge(S("gtr"), (LEVELS - 1) * j + l + 1)
                    act.activation(gm[:, :, :], four(mx[2][:, :]), ACT.Copy).then_inc(S("gm"), 1)
                advance(U["v0"])
                act.wait_ge(S("v0s"), 2 * j + 2)
                act.activation(v0[:, :, :], mx[3][:, 0:2 * P].rearrange("p (h c) -> p h c", h=2), ACT.Copy).then_inc(S("v0"), 1)
                advance(U["s1"])
                act.wait_ge(S("s1_psum"), j + 1)
                act.activation(st[:, :, :], mx[1][:, 0:2 * P].rearrange("p (h c) -> p h c", h=2), ACT.Copy).then_inc(S("st"), 1)
                advance(U["v1"])
                act.wait_ge(S("v1_psum"), j + 1)
                act.activation(v1[:, :, :], mx[1][:, 2 * P:4 * P].rearrange("p (h c) -> p h c", h=2), ACT.Copy).then_inc(S("v1"), 1)
                advance(U["o"])
                act.wait_ge(S("o_psum"), p + 1)
                act.activation(os_[:, :, :, :], mx[2][:, :].rearrange("p (h c e) -> p h c e", h=2, c=C), ACT.Copy).then_inc(S("os"), 1)
                squares(p)
                advance(U["tr"])
                split_y(p, Y_BLOCK["gdn"] + 2 * j)

            def squares(p):
                act.wait_ge(S("os_full"), p + 1)
                for n in range(4):
                    act.wait_ge(S("os_sq"), 4 * p + n) if 4 * p + n else None
                    act.activation(xs[:, 0, :], os_[:, n // 2, n % 2, :], ACT.Square,
                                   accum_out=sm[:, 48 + n:49 + n]).then_inc(S("os_sq"), 1)

            def mix_ret(p, j, base):
                U = {k: base + v for k, v in U_RET.items()}
                advance(base + 1)
                gate_tanh(p)
                advance(U["gram"])
                act.wait_ge(S("r_vtok"), j + 1)
                act.activation(vr[:, :, :], four(mx[1][:, :]), ACT.Copy).then_inc(S("r_vr"), 1)
                for h in range(2):
                    act.activation(ktok[:, h, :], mx[2][:, h * P:(h + 1) * P], ACT.Copy,
                                   scale=cst[:, K_KDEC + 2 * j + h:K_KDEC + 2 * j + h + 1]).then_inc(S("r_ktok"), 1)
                advance(U["s1"])
                act.wait_ge(S("r_s1_psum"), j + 1)
                act.activation(st[:, :, :], mx[3][:, 0:2 * P].rearrange("p (h c) -> p h c", h=2), ACT.Copy).then_inc(S("r_st"), 1)
                advance(U["o"])
                act.wait_ge(S("o_psum"), p + 1)
                act.activation(os_[:, :, :, :], mx[2][:, :].rearrange("p (h c e) -> p h c e", h=2, c=C), ACT.Copy).then_inc(S("os"), 1)
                squares(p)
                advance(U["tr"])
                split_y(p, Y_BLOCK["ret"] + 2 * j)

            def mix_moba(p, j, base):
                U = {k: base + v for k, v in U_MOBA.items()}
                lg = th[:, 0:6 * P].rearrange("p (h c) -> p h c", h=2)
                pr = th[:, 6 * P:12 * P].rearrange("p (h c) -> p h c", h=2)
                advance(base + 1)
                gate_tanh(p)
                advance(U["nrm"])
                act.wait_ge(S("m_vtok"), j + 1)
                act.activation(vr[:, :, :], four(mx[1][:, :]), ACT.Copy).then_inc(S("m_vr"), 1)
                advance(U["score"])
                act.wait_ge(S("score"), j + 1)
                for h in range(2):
                    for c in range(C):
                        a, b = (0, P) if c == 0 else (P, 3 * P)
                        act.activation(lg[:, h, a:b], mx[(0, 3)[h]][:, a:b], ACT.Copy,
                                       scale=sm[:, 64 + 4 * h + c:65 + 4 * h + c]).then_inc(S("m_lg"), 1)
                for n in range(4):
                    h, c = n // 2, n % 2
                    a, b = (0, P) if c == 0 else (P, 3 * P)
                    act.wait_ge(S("m_max"), 4 * j + n + 1)
                    act.activation(pr[:, h, a:b], lg[:, h, a:b], ACT.Exp, bias=sm[:, 72 + n:73 + n],
                                   accum_out=sm[:, 76 + n:77 + n]).then_inc(S("m_exp"), 1)
                advance(U["pt"])
                act.wait_ge(S("pt_psum"), 2 * j + 1)
                act.activation(kq[:, 0].rearrange("p c k t -> p (c k t)")[:, 0:3 * P], mx[2][:, 0:3 * P], ACT.Copy).then_inc(S("pt_a"), 1)
                advance(U["o"])
                split_y(p, Y_BLOCK["moba"] + 2 * j)

            advance(128)
            for p, (kind, j) in enumerate(PAIRS):
                {"gdn": mix_gdn, "ret": mix_ret, "moba": mix_moba}[kind](p, j, 128 * (p + 1))
                advance(128 * (p + 2))
            advance(64 * GROUPS)

            send(6)
            send(7)
            act.wait_ge(S("out_sent0"), 64)
            act.wait_ge(S("out_sent1"), 64)

        @block.gpsimd
        def _(pool):
            pos = [0]

            def advance(u):
                for v in range(pos[0], min(u, 64 * GROUPS)):
                    n = v // UPT + LEAD
                    if v % UPT == 0 and n < TILES and n % TPH not in VEC_LO:
                        low_part(pool, n, "lo_pool")
                pos[0] = max(pos[0], u)

            def power(dst, src, n):
                return pool.tensor_tensor(sm[:, dst:dst + n], sm[:, src:src + n], cst[:, K_POW:K_POW + n], ALU.pow)

            pool.memset(raw[:, :, :, 0:PAD], 0.0).then_inc(S("pad_zero"), 1)
            pool.wait_ge(S("cst_in"), 16)
            pool.wait_ge(S("ms_done"), 1)
            power(6, 4, 2).then_inc(S("rstd_done"), 1)
            for n in range(LEAD):
                if n not in VEC_LO:
                    low_part(pool, n, "lo_pool")
            pool.wait_ge(S("wab_hi_done"), 1)
            pool.tensor_tensor(wab_lo[:, :, :], wab[:, :, :], wab_hi[:, :, :].bitcast(F32), ALU.subtract).then_inc(S("wab_lo_done"), 1)

            def split_y(p, y0):
                pool.wait_ge(S("y_hi"), p + 1)
                pool.tensor_tensor(yT[:, y0:y0 + 2, 1, :], yf[:, :, :], yT[:, y0:y0 + 2, 0, :].bitcast(F32),
                                   ALU.subtract).then_inc(S("y_lo"), 1)

            def rms_power(p):
                pool.wait_ge(S("o_ms"), p + 1)
                power(56, 52, 4).then_inc(S("o_pow"), 1)

            def mix_gdn(p, j, base):
                U = {k: base + v for k, v in U_GDN.items()}
                advance(base + 12)
                for h in range(2):
                    pool.wait_ge(S("silu_kq"), 4 * j + 2 * h + 2)
                    pool.tensor_tensor(sq[:, h], kq[:, h], kq[:, h], ALU.mult).then_inc(S("sq"), 1)
                advance(U["gram"])
                pool.wait_ge(S("g_norm"), j + 1)
                power(32, 24, 8).then_inc(S("g_pow"), 1)
                pool.wait_ge(S("exp_decay"), j + 1)
                pool.tensor_tensor(er[:, :, :], ee[:, :, :], upper.unsqueeze(1).broadcast_to([P, 4, P]), ALU.mult).then_inc(S("er1"), 1)
                pool.wait_ge(S("er1"), j + 1)
                pool.wait_ge(S("g_pow"), j + 1)
                pool.tensor_tensor(ee[:, :, :], er[:, :, :],
                                   sm[:, 32:40].rearrange("p (n k) -> p n k", k=2)[:, :, 0:1].broadcast_to([P, 4, P]),
                                   ALU.mult).then_inc(S("er2"), 1)
                for l in range(LEVELS):
                    advance(U[f"x{l}"])
                advance(U["o"])
                rms_power(p)
                pool.wait_ge(S("o_fac"), p + 1)
                pool.tensor_tensor(on[:, :, :, :].rearrange("p h c e -> p (h c) e"), os_[:, :, :, :].rearrange("p h c e -> p (h c) e"),
                                   sm[:, 60:64].unsqueeze(2).broadcast_to([P, 4, P]), ALU.mult).then_inc(S("on"), 1)
                advance(U["tr"])
                split_y(p, Y_BLOCK["gdn"] + 2 * j)

            def mix_ret(p, j, base):
                U = {k: base + v for k, v in U_RET.items()}
                advance(U["o"])
                rms_power(p)
                pool.wait_ge(S("o_fac"), p + 1)
                pool.tensor_tensor(on[:, :, :, :].rearrange("p h c e -> p (h c) e"), os_[:, :, :, :].rearrange("p h c e -> p (h c) e"),
                                   sm[:, 60:64].unsqueeze(2).broadcast_to([P, 4, P]), ALU.mult).then_inc(S("on"), 1)
                advance(U["tr"])
                split_y(p, Y_BLOCK["ret"] + 2 * j)

            def mix_moba(p, j, base):
                U = {k: base + v for k, v in U_MOBA.items()}
                for h in range(2):
                    pool.wait_ge(S("evac"), 8 * p + 4 * h + 2)
                    pool.tensor_tensor(sq[:, h].rearrange("p c k t -> p (c k t)").rearrange("p (s t) -> p s t", s=2),
                                       raw[:, h, 0:2, PAD:], raw[:, h, 0:2, PAD:], ALU.mult).then_inc(S("m_sq"), 1)
                advance(U["nrm"])
                pool.wait_ge(S("m_norm"), j + 1)
                power(64, 80, 8).then_inc(S("m_pow"), 1)
                advance(U["score"])
                for n in range(4):
                    h, c = n // 2, n % 2
                    a, b = (0, P) if c == 0 else (P, 3 * P)
                    pr = th[:, 6 * P:12 * P].rearrange("p (h c) -> p h c", h=2)
                    pool.wait_ge(S("m_rec"), j + 1)
                    pool.tensor_scalar(pr[:, h, a:b], pr[:, h, a:b], sm[:, 88 + n:89 + n], None, ALU.mult).then_inc(S("m_prob"), 1)
                advance(U["o"])
                split_y(p, Y_BLOCK["moba"] + 2 * j)

            advance(128)
            for p, (kind, j) in enumerate(PAIRS):
                {"gdn": mix_gdn, "ret": mix_ret, "moba": mix_moba}[kind](p, j, 128 * (p + 1))
                advance(128 * (p + 2))
            advance(64 * GROUPS)

        @block.vector
        def _(dve):
            pos = [0]

            def evacuate(g, s):
                dve.wait_ge(S("ev_lo_done"), 4 * g + s + 1)
                if g == 0 and s == 0:
                    dve.wait_ge(S("pad_zero"), 1)
                dve.tensor_tensor(raw[:, g % 2, s, PAD:], pj[s][:, 0:T], ev_lo[:, s, :], ALU.add).then_inc(S("evac"), 1)

            def residual(n):
                g, c = n // 2, n % 2
                dve.wait_ge(S("out_psum"), n + 1)
                dve.wait_ge(S(f"xr_in{n % 3}"), 16 * (n // 3 + 1))
                if n >= 2:
                    dve.wait_ge(S(f"out_sent{n % 2}"), 16 * (n // 2))
                dve.tensor_tensor(sq[:, n % 2].rearrange("p c k t -> p (c k t)"), pj[n % 4][:, :],
                                  cv[:, (n % 3) * 512:(n % 3 + 1) * 512], ALU.add).then_inc(S("out_ready"), 1)

            def advance(u):
                for v in range(pos[0], min(u, 64 * GROUPS)):
                    if evacuated(v):
                        evacuate(*evacuated(v))
                    n = v // UPT + LEAD
                    if v % UPT == 0 and n < TILES and n % TPH in VEC_LO:
                        low_part(dve, n, "lo_vec")
                    if v > 64 * HEADS and v % 64 == 0:
                        residual(2 * (v // 64 - HEADS) - 2)
                        residual(2 * (v // 64 - HEADS) - 1)
                pos[0] = max(pos[0], u)

            dve.wait_ge(S("cst_in"), 16)
            dve.wait_ge(S("cst_in2"), 16)
            dve.wait_ge(S("ss_done"), 4)
            dve.tensor_tensor(sm[:, 8:10], sm[:, 0:4].rearrange("p (c h) -> p c h", h=2)[:, :, 0],
                              sm[:, 0:4].rearrange("p (c h) -> p c h", h=2)[:, :, 1], ALU.add).then_inc(S("ss2"), 1)
            dve.wait_ge(S("ss2"), 1)
            dve.tensor_scalar(sm[:, 4:6], sm[:, 8:10], 1.0 / D, EPS, ALU.mult, ALU.add).then_inc(S("ms_done"), 1)
            dve.wait_ge(S("params_psum"), 1)
            dve.tensor_copy(pcol[:, :], mx[3][:, 0:R_ROWS]).then_inc(S("pcol_done"), 1)
            dve.wait_ge(S("rstd_done"), 1)
            for c in range(C):
                dve.tensor_scalar(x_sb[:, c, :], x_sb[:, c, :], sm[:, 6 + c:7 + c], None, ALU.mult).then_inc(S("xn_done"), 1)
            for k in range(KC):
                dve.wait_ge(S("h_hi"), k + 1)
                if k == 0:
                    dve.wait_ge(S("pcol_done"), 1)
                dve.scalar_tensor_tensor(hT[:, k, 1, :], (pj + mx)[k % 8][:, 0:T], pcol[:, R_NORM + k:R_NORM + k + 1],
                                         hT[:, k, 0, :].bitcast(F32), ALU.mult, ALU.subtract).then_inc(S("h_lo"), 1)

            steps = [0]

            def link(ins):
                steps[0] += 1
                ins.then_inc(S("ab_step"), 1)
                dve.wait_ge(S("ab_step"), steps[0])

            def over_chunks(ap):
                return ap.unsqueeze(1).broadcast_to([P, C, GDN])

            dve.wait_ge(S("bias_in1"), 16)
            dve.wait_ge(S("tanh_b"), 1)
            link(dve.tensor_tensor(ab[:, A_Z], mx[0][:, 0:2 * AB].rearrange("p (c h) -> p c h", c=C)[:, :, 0:GDN],
                                   over_chunks(bias[:, 1, :]), ALU.add))
            link(dve.tensor_scalar(ab[:, A_T1], ab[:, A_Z], -1.0, None, ALU.mult))
            dve.tensor_tensor(ab[:, A_T1], ab[:, A_Z], ab[:, A_T1], ALU.min).then_inc(S("negabs_z"), 1)
            dve.wait_ge(S("exp_z"), 1)
            dve.tensor_scalar(ab[:, A_U], ab[:, A_E], 1.0, None, ALU.add).then_inc(S("one_plus"), 1)
            dve.wait_ge(S("one_plus"), 1)
            link(dve.tensor_scalar(ab[:, A_T2], ab[:, A_U], 1.0, None, ALU.subtract))
            link(dve.tensor_tensor(ab[:, A_T2], ab[:, A_E], ab[:, A_T2], ALU.subtract))
            link(dve.reciprocal(ab[:, A_T3], ab[:, A_U]))
            link(dve.tensor_tensor(ab[:, A_T2], ab[:, A_T2], ab[:, A_T3], ALU.mult))
            dve.wait_ge(S("ln_u"), 1)
            link(dve.tensor_tensor(ab[:, A_T2], ab[:, A_T2], ab[:, A_L], ALU.add))
            link(dve.scalar_tensor_tensor(ab[:, A_T2], ab[:, A_Z], 0.0, ab[:, A_T2], ALU.max, ALU.add))
            dve.wait_ge(S("expa_done"), 1)
            link(dve.tensor_tensor(ab[:, A_T2], ab[:, A_T2], over_chunks(sm[:, 16:16 + GDN]), ALU.mult))
            dve.tensor_scalar(ab[:, A_G], ab[:, A_T2], -1.0, None, ALU.mult).then_inc(S("g_done"), 1)
            dve.wait_ge(S("tanh_b"), 1)
            dve.tensor_scalar(ab[:, A_BETA], ab[:, A_TB], 0.5, 0.5, ALU.mult, ALU.add).then_inc(S("beta_done"), 1)
            dve.wait_ge(S("cum_psum"), 1)
            link(dve.tensor_copy(ab[:, A_GC], mx[1][:, 0:C * GDN].rearrange("p (c h) -> p c h", c=C)))
            link(dve.tensor_scalar(ab[:, A_NGC], ab[:, A_GC], -1.0, None, ALU.mult))
            dve.tensor_tensor(ab[:, A_T2, 0, :], mx[1][:, C * GDN:(C + 1) * GDN], ab[:, A_GC, 0, :], ALU.subtract).then_inc(S("gc_done"), 1)
            dve.wait_ge(S("egc_done"), 2)
            link(dve.tensor_scalar(ab[:, A_NEGC], ab[:, A_EGC], -1.0, None, ALU.mult))
            dve.tensor_tensor(sm[:, 22:23], pcol[:, R_Q:R_Q + 1], pcol[:, R_K:R_K + 1], ALU.mult).then_inc(S("wqk0"), 1)
            dve.wait_ge(S("wqk0"), 1)
            dve.tensor_scalar(sm[:, 23:24], sm[:, 22:23], SCALE, None, ALU.mult).then_inc(S("wqk"), 1)
            dve.tensor_scalar(sm[:, 96:96 + RET + 1], pcol[:, R_RET:R_GDN + 1], 0.5, None, ALU.mult).then_inc(S("halfw"), 1)

            def gate(p):
                dve.wait_ge(S("tanh_z"), p + 1)
                dve.scalar_tensor_tensor(zg[:, :, :], zg[:, :, :], 1.0, raw[:, :, 3, PAD:], ALU.add, ALU.mult).then_inc(S("zg"), 1)

            def rms_factor(p, gdn):
                dve.wait_ge(S("os_sq"), 4 * p + 4)
                if gdn:
                    dve.tensor_tensor(sm[:, 104:108], sm[:, 48:52], sm[:, 112:116], ALU.mult).then_inc(S("o_ms0"), 1)
                    dve.wait_ge(S("o_ms0"), p + 1)
                    dve.tensor_scalar(sm[:, 52:56], sm[:, 104:108], EPS, None, ALU.add).then_inc(S("o_ms"), 1)
                    dve.wait_ge(S("o_pow"), p + 1)
                    dve.tensor_tensor(sm[:, 60:64], sm[:, 56:60], sm[:, 108:112], ALU.mult).then_inc(S("o_fac"), 1)
                else:
                    dve.tensor_scalar(sm[:, 52:56], sm[:, 48:52], 1.0 / P, EPS, ALU.mult, ALU.add).then_inc(S("o_ms"), 1)
                    dve.wait_ge(S("o_pow"), p + 1)
                    dve.tensor_copy(sm[:, 60:64], sm[:, 56:60]).then_inc(S("o_fac"), 1)

            def mix_gdn(p, j, base):
                U = {k: base + v for k, v in U_GDN.items()}
                th3, cv3 = (b[:, :].rearrange("p (h s t) -> p h s t", h=2, s=3) for b in (th, cv))

                def tap(h, s, k):
                    return pcol[:, R_CONV + k * 3 * GDN + s * GDN + 2 * j + h:][:, 0:1]

                def conv(h, s, name):
                    at = {0: 1, 1: 0, 2: 2}[s]
                    dst = cv3[:, h, at]
                    dve.wait_ge(S("evac"), 8 * p + 4 * h + s + 1)
                    ins = dve.tensor_scalar(dst, raw[:, h, s, 0:T], tap(h, s, 0), None, ALU.mult)
                    for k in range(1, CONV):
                        conv_step[0] += 1
                        ins.then_inc(S("conv_step"), 1)
                        dve.wait_ge(S("conv_step"), conv_step[0])
                        ins = dve.scalar_tensor_tensor(dst, raw[:, h, s, k:k + T], tap(h, s, k), dst, ALU.mult, ALU.add)
                    return ins

                advance(base + 1)
                dve.wait_ge(S("gcb"), j + 1)
                for n in range(4):
                    h, c = n // 2, n % 2
                    dve.tensor_scalar(dd[:, n, :], mx[2][:, n * P:(n + 1) * P], ab[:, A_NGC, c, 2 * j + h:2 * j + h + 1], 0.0,
                                      ALU.add, ALU.min).then_inc(S("clip_done"), 1)
                for h in range(2):
                    conv(h, 1, "k").then_inc(S("conv_one"), 1)
                    conv(h, 0, "q").then_inc(S("conv_kq"), 1)
                    advance(base + 6 + 6 * h)
                for h in range(2):
                    dve.wait_ge(S("tanh_kq"), 2 * j + h + 1)
                    dve.wait_ge(S("conv_kq"), 2 * j + h + 1)
                    for i in range(2):
                        dve.scalar_tensor_tensor(kq[:, h, :, i, :], th3[:, h, i].rearrange("p (c t) -> p c t", c=C), 1.0,
                                                 cv3[:, h, i].rearrange("p (c t) -> p c t", c=C), ALU.add, ALU.mult).then_inc(S("silu_kq"), 1)
                for h in range(2):
                    conv(h, 2, "v").then_inc(S("conv_v"), 1)
                gate(p)
                dve.wait_ge(S("tanh_v"), j + 1)
                dve.wait_ge(S("conv_v"), 2 * j + 2)
                dve.scalar_tensor_tensor(vT[:, :, :], th3[:, :, 2], 1.0, cv3[:, :, 2], ALU.add, ALU.mult).then_inc(S("silu_v"), 1)
                advance(U["gram"])
                dve.wait_ge(S("gram"), j + 1)
                dve.tensor_scalar(sm[:, 24:32], mx[3][:, 2 * P:2 * P + 8], 4 * EPS, None, ALU.add).then_inc(S("g_norm"), 1)
                dve.wait_ge(S("g_pow"), j + 1)
                rk = sm[:, 32:40].rearrange("p (n k) -> p n k", k=2)[:, :, 0]
                rq = sm[:, 32:40].rearrange("p (n k) -> p n k", k=2)[:, :, 1]
                nk = sm[:, 24:32].rearrange("p (n k) -> p n k", k=2)[:, :, 0]
                dve.scalar_tensor_tensor(sm[:, 40:44], nk, 0.5, rk, ALU.mult, ALU.mult).then_inc(S("g_scalars"), 1)
                dve.tensor_scalar(sm[:, 108:112], rq, SCALE, None, ALU.mult).then_inc(S("g_q"), 1)
                dve.wait_ge(S("g_q"), j + 1)
                dve.scalar_tensor_tensor(sm[:, 112:116], sm[:, 108:112], 1.0 / P, sm[:, 108:112], ALU.mult, ALU.mult).then_inc(S("g_q2"), 1)
                for h in range(2):
                    dve.tensor_tensor(sm[:, 44 + 2 * h:46 + 2 * h], rk[:, 2 * h:2 * h + 2], ab[:, A_BETA, :, 2 * j + h], ALU.mult).then_inc(S("g_b"), 1)
                    dve.tensor_tensor(sm[:, 116 + h:117 + h], rk[:, 2 * h:2 * h + 1], ab[:, A_ELAST, 0, 2 * j + h:2 * j + h + 1], ALU.mult).then_inc(S("g_el"), 1)
                dve.wait_ge(S("g_b"), 2 * j + 2)
                dve.tensor_tensor(gt[:, :, :], ident.unsqueeze(1).broadcast_to([P, 4, P]),
                                  sm[:, 44:48].unsqueeze(2).broadcast_to([P, 4, P]), ALU.mult).then_inc(S("gt"), 1)
                dve.wait_ge(S("er2"), j + 1)
                for i, dst in enumerate((mT, aT)):
                    for h in range(2):
                        dve.tensor_tensor(dst[:, 2 * h:2 * h + 2, :], mx[h][:, :].rearrange("p (c k t) -> p c k t", c=C, k=2)[:, :, i],
                                          ee[:, 2 * h:2 * h + 2, :], ALU.mult).then_inc(S("mt_at"), 1)
                for l in range(LEVELS):
                    advance(U[f"x{l}"])
                    dve.wait_ge(S("x_psum"), LEVELS * j + l + 1)
                    mask = cst[:, K_LEVEL + l * P:K_LEVEL + (l + 1) * P].unsqueeze(1).broadcast_to([P, 4, P])
                    dve.tensor_tensor(xs[:, :, :], four(mx[0][:, :]), mask, ALU.mult).then_inc(S("xs"), 1)
                    advance(U[f"y{l}"])
                    dve.wait_ge(S("y_psum"), LEVELS * j + l + 1)
                    dve.wait_ge(S("gt"), (LEVELS + 1) * j + l + 1)
                    dve.tensor_tensor(gt[:, :, :], gt[:, :, :], four(mx[1][:, :]), ALU.subtract).then_inc(S("gt"), 1)
                advance(U["v0"])
                dve.wait_ge(S("v0_psum"), j + 1)
                dve.wait_ge(S("g_el"), 2 * j + 2)
                for h in range(2):
                    dve.tensor_scalar(v0s[:, h, :], mx[3][:, h * P:(h + 1) * P], sm[:, 116 + h:117 + h], None, ALU.mult).then_inc(S("v0s"), 1)
                advance(U["ks"])
                dve.wait_ge(S("ks_psum"), j + 1)
                dve.wait_ge(S("vr"), 4 * j + 4)
                for h in range(2):
                    dve.scalar_tensor_tensor(vr[:, 2 * h + 1, :], mx[0][:, h * P:(h + 1) * P], ab[:, A_NEGC, 1, 2 * j + h:2 * j + h + 1],
                                             vr[:, 2 * h + 1, :], ALU.mult, ALU.add).then_inc(S("vr1"), 1)
                advance(U["o"])
                dve.wait_ge(S("os"), p + 1)
                for h in range(2):
                    ins = dve.scalar_tensor_tensor(os_[:, h, 1, :], mx[0][:, (2 + h) * P:(3 + h) * P], ab[:, A_EGC, 1, 2 * j + h:2 * j + h + 1],
                                                   os_[:, h, 1, :], ALU.mult, ALU.add)
                ins.then_inc(S("os_full"), 1)
                rms_factor(p, True)
                advance(U["tr"])
                gated_pair(p, mx[3], [sm[:, 96 + RET:97 + RET]] * 2)

            def gated_pair(p, psum, weights):
                dve.wait_ge(S("otr"), p + 1)
                dve.wait_ge(S("zg"), p + 1)
                for h in range(2):
                    ins = dve.scalar_tensor_tensor(yf[:, h, :], psum[:, h * T:(h + 1) * T], weights[h], zg[:, h, :], ALU.mult, ALU.mult)
                    if h == 1:
                        ins.then_inc(S("yf_done"), 1)

            def mix_ret(p, j, base):
                U = {k: base + v for k, v in U_RET.items()}
                advance(base + 1)
                gate(p)
                advance(U["gram"])
                dve.wait_ge(S("r_gram"), j + 1)
                for h in range(2):
                    dec = cst[:, K_DECAY + (2 * j + h) * P:K_DECAY + (2 * j + h + 1) * P].unsqueeze(1).broadcast_to([P, C, P])
                    dve.tensor_tensor(aT[:, 2 * h:2 * h + 2, :], mx[0][:, h * T:(h + 1) * T].rearrange("p (c t) -> p c t", c=C), dec,
                                      ALU.mult).then_inc(S("r_at"), 1)
                advance(U["o"])
                dve.wait_ge(S("os"), p + 1)
                for h in range(2):
                    ins = dve.scalar_tensor_tensor(os_[:, h, 1, :], mx[3][:, (2 + h) * P:(3 + h) * P],
                                                   cst[:, K_QDEC + 2 * j + h:K_QDEC + 2 * j + h + 1],
                                                   os_[:, h, 1, :], ALU.mult, ALU.add)
                ins.then_inc(S("os_full"), 1)
                rms_factor(p, False)
                advance(U["tr"])
                gated_pair(p, mx[0], [sm[:, 96 + 2 * j + h:97 + 2 * j + h] for h in range(2)])

            def mix_moba(p, j, base):
                U = {k: base + v for k, v in U_MOBA.items()}
                lg = th[:, 0:6 * P].rearrange("p (h c) -> p h c", h=2)
                advance(base + 1)
                gate(p)
                advance(U["nrm"])
                dve.wait_ge(S("m_nrm"), j + 1)
                dve.tensor_scalar(sm[:, 80:88], mx[3][:, 0:8], 1.0 / P, EPS, ALU.mult, ALU.add).then_inc(S("m_norm"), 1)
                advance(U["bc"])
                dve.wait_ge(S("m_bc"), j + 1)
                for h in range(2):
                    dve.scalar_tensor_tensor(vT[:, h, :], raw[:, h, 1, PAD:], sm[:, 23:24], mx[2][:, h * T:(h + 1) * T], ALU.mult, ALU.mult).then_inc(S("knT"), 1)
                advance(U["score"])
                for h in range(2):
                    head = 2 * j + h
                    slope = 2.0 ** (-8.0 * (head + 1) / MOBA)
                    dve.wait_ge(S("m_lg"), 4 * j + 2 * h + 2)
                    dve.scalar_tensor_tensor(lg[:, h, :], cst[:, K_DIST:K_DIST + 3 * P], slope, lg[:, h, :], ALU.mult, ALU.add).then_inc(S("m_alibi"), 1)
                    dve.wait_ge(S("m_alibi"), 2 * j + h + 1)
                    for c in range(C):
                        a, b = (0, P) if c == 0 else (P, 3 * P)
                        n = 2 * h + c
                        dve.tensor_reduce(sm[:, 72 + n:73 + n], lg[:, h, a:b], AX.X, ALU.max, negate=True).then_inc(S("m_max"), 1)
                dve.wait_ge(S("m_exp"), 4 * j + 4)
                dve.reciprocal(sm[:, 88:92], sm[:, 76:80]).then_inc(S("m_rec"), 1)
                advance(U["pt"])
                dve.wait_ge(S("pt_psum"), 2 * j + 2)
                dve.tensor_copy(kq[:, 1].rearrange("p c k t -> p (c k t)")[:, 0:3 * P], mx[0][:, 0:3 * P]).then_inc(S("pt_v"), 1)
                advance(U["o"])
                dve.wait_ge(S("otr"), p + 1)
                dve.wait_ge(S("zg"), p + 1)
                dve.scalar_tensor_tensor(yf[:, :, :], mx[1][:, :].rearrange("p (h t) -> p h t", h=2), 0.5, zg[:, :, :],
                                         ALU.mult, ALU.mult).then_inc(S("yf_done"), 1)

            conv_step = [0]
            advance(128)
            for p, (kind, j) in enumerate(PAIRS):
                {"gdn": mix_gdn, "ret": mix_ret, "moba": mix_moba}[kind](p, j, 128 * (p + 1))
                advance(128 * (p + 2))
            advance(64 * GROUPS)
            residual(6)
            residual(7)

        @block.tensor
        def _(pe):
            pos = [0]

            def unit(v):
                g, t = v // 64, v // UPT
                n, r = t, v % UPT
                if r == 0:
                    wait_lo(pe, n)
                hi = w_hi[:, n % NSPLIT, :].rearrange("p (k c) -> p k c", k=TK)
                lo = w_lo[:, n % NSPLIT, :].rearrange("p (k c) -> p k c", k=TK)
                if g < HEADS:
                    s, k = r // TK, r % TK
                    kc = (t % TPH) * TK + k
                    first, last = kc == 0, kc == KC - 1
                    if first and g:
                        pe.wait_ge(S("evac"), 4 * (g - 1) + s + 1)
                    cols = slice(s * P, (s + 1) * P)

                    def low(**kw):
                        return pe.matmul(pj[s][:, 0:T], lo[:, k, cols], hT[:, kc, 0, :], **kw)

                    def high(**kw):
                        return pe.matmul(pj[s][:, :], hi[:, k, cols], hT[:, kc].rearrange("p a t -> p (a t)"), **kw)

                    if last:
                        low(start=False, stop=False)
                        ins = high(start=False, stop=True)
                        ins.then_inc(S("proj_done"), 1)
                    else:
                        high(start=first, stop=False)
                        ins = low(start=False, stop=False)
                else:
                    k, c, half = r // 4, r // 2 % 2, r % 2
                    kc = (t % TPH) * TK + k
                    first, last = kc == 0, kc == KC - 1
                    bank = pj[(2 * (g - HEADS) + c) % 4]
                    if first and half == 0:
                        if g == HEADS:
                            pe.wait_ge(S("evac"), 4 * HEADS)
                        elif g >= HEADS + 2:
                            pe.wait_ge(S("out_ready"), 2 * (g - HEADS - 2) + c + 1)
                    if kc % 2 == 0 and half == 0 and c == 0 and g == HEADS:
                        block_ready(kc // 2)
                    tok = slice(c * P, (c + 1) * P)
                    if half == 0:
                        ins = pe.matmul(bank[:, :], yT[:, kc, 0, tok], hi[:, k, :], start=first, stop=False)
                    else:
                        pe.matmul(bank[:, :], yT[:, kc, 1, tok], hi[:, k, :], start=False, stop=False)
                        ins = pe.matmul(bank[:, :], yT[:, kc, 0, tok], lo[:, k, :], start=False, stop=last)
                        if last:
                            ins.then_inc(S("out_psum"), 1)
                if r == UPT - 1 and not last:
                    ins.then_inc(S("tile_used"), 1)

            def block_ready(b):
                order = {"ret": 3, "gdn": 0, "moba": 5}
                kind = "ret" if b < 2 else "gdn" if b < 5 else "moba"
                p = order[kind] + b - {"ret": 0, "gdn": 2, "moba": 5}[kind]
                pe.wait_ge(S("y_lo"), p + 1)

            def stream(u):
                for v in range(pos[0], min(u, 64 * GROUPS)):
                    unit(v)
                pos[0] = max(pos[0], u)

            pe.wait_ge(S("cst_in"), 16)
            for name in ("param_in", "norm_in", "param_in1", "param_in2", "param_in3", "param_in4"):
                pe.wait_ge(S(name), 16)
            pe.transpose(mx[3][:, 0:R_ROWS], prow[:, :], ident[0:R_ROWS, 0:R_ROWS]).then_inc(S("params_psum"), 1)
            for k in range(KC):
                if k == 0:
                    pe.wait_ge(S("xn_done"), 2)
                if k == 7:
                    pe.wait_ge(S("pcol_done"), 1)
                if k >= 8:
                    pe.wait_ge(S("h_lo"), k - 7)
                for c in range(C):
                    ins = pe.transpose((pj + mx)[k % 8][:, c * P:(c + 1) * P], x_sb[:, c, k * P:(k + 1) * P], ident)
                ins.then_inc(S("hT_psum"), 1)

            pe.wait_ge(S("h_lo"), KC)
            pe.wait_ge(S("wab_lo_done"), 1)
            for c in range(C):
                tok = slice(c * P, (c + 1) * P)
                for k in range(KC):
                    for i, (a, w) in enumerate(((0, wab_hi), (1, wab_hi), (0, wab_lo))):
                        ins = pe.matmul(mx[0][:, c * AB:(c + 1) * AB], hT[:, k, a, tok], w[:, k, :],
                                        start=k == 0 and i == 0, stop=k == KC - 1 and i == 2)
            ins.then_inc(S("ab_psum"), 1)
            stream(24)
            pe.wait_ge(S("g_done"), 1)
            for c in range(C):
                pe.matmul(mx[1][:, c * GDN:(c + 1) * GDN], upper, ab[:, A_G, c, :], start=True, stop=True)
            pe.matmul(mx[1][:, C * GDN:(C + 1) * GDN], ones, ab[:, A_G, 0, :], start=True, stop=True).then_inc(S("cum_psum"), 1)

            def mix_gdn(p, j, base):
                U = {k: base + v for k, v in U_GDN.items()}
                stream(base + 1)
                pe.wait_ge(S("egc_done"), 2)
                for n in range(4):
                    h, c = n // 2, n % 2
                    ins = pe.matmul(mx[2][:, n * P:(n + 1) * P], ab[:, A_GC, c, 2 * j + h:2 * j + h + 1].broadcast_to([P, P]), ident,
                                    start=True, stop=True)
                ins.then_inc(S("gcb"), 1)
                stream(U["gram"])
                if p:
                    pe.wait_ge(S("yf_done"), p)
                pe.wait_ge(S("silu_kq"), 4 * j + 4)
                for h in range(2):
                    for c in range(C):
                        pe.matmul(mx[h][:, c * T:(c + 1) * T], kq[:, h, c, 0, :], kq[:, h, c].rearrange("p k t -> p (k t)"),
                                  start=True, stop=True)
                    pe.transpose(mx[3][:, h * P:(h + 1) * P], kq[:, h, 0, 0, :], ident)
                pe.wait_ge(S("sq"), 2 * j + 2)
                for h in range(2):
                    for c in range(C):
                        for i in range(2):
                            at = 2 * P + 4 * h + 2 * c + i
                            ins = pe.matmul(mx[3][:, at:at + 1], sq[:, h, c, i, :], ones[:, 0:1], start=True, stop=True)
                ins.then_inc(S("gram"), 1)
                stream(U["vtok"])
                pe.wait_ge(S("silu_v"), j + 1)
                pe.wait_ge(S("clip_done"), 4 * j + 4)
                for n in range(4):
                    ins = pe.transpose(mx[2][:, n * P:(n + 1) * P], vT[:, n // 2, (n % 2) * P:(n % 2 + 1) * P], ident)
                ins.then_inc(S("vtok"), 1)
                for l in range(LEVELS):
                    stream(U[f"x{l}"])
                    if l == 0:
                        pe.wait_ge(S("mt_at"), 4 * j + 4)
                        pe.wait_ge(S("gt"), (LEVELS + 1) * j + 1)
                    else:
                        pe.wait_ge(S("gm"), (LEVELS - 1) * j + l)
                    g_in = gt if l == 0 else gm
                    for n in range(4):
                        ins = pe.matmul(mx[0][:, n * P:(n + 1) * P], mT[:, n, :], g_in[:, n, :], start=True, stop=True)
                    ins.then_inc(S("x_psum"), 1)
                    stream(U[f"y{l}"])
                    pe.wait_ge(S("xs"), LEVELS * j + l + 1)
                    for n in range(4):
                        ins = pe.matmul(mx[1][:, n * P:(n + 1) * P], xs[:, n, :], gt[:, n, :], start=True, stop=True)
                    ins.then_inc(S("y_psum"), 1)
                    if l < LEVELS - 1:
                        stream(U[f"t{l}"])
                        pe.wait_ge(S("gt"), (LEVELS + 1) * j + l + 2)
                        if l == 0:
                            pe.wait_ge(S("vr"), 4 * j + 4)
                        for n in range(4):
                            ins = pe.transpose(mx[2][:, n * P:(n + 1) * P], gt[:, n, :], ident)
                        ins.then_inc(S("gtr"), 1)
                stream(U["v0"])
                pe.wait_ge(S("gt"), (LEVELS + 1) * (j + 1))
                pe.wait_ge(S("ktok"), j + 1)
                for h in range(2):
                    ins = pe.matmul(mx[3][:, h * P:(h + 1) * P], gt[:, 2 * h, :], vr[:, 2 * h, :], start=True, stop=True)
                ins.then_inc(S("v0_psum"), 1)
                stream(U["s1"])
                pe.wait_ge(S("v0s"), 2 * j + 2)
                for h in range(2):
                    ins = pe.matmul(mx[1][:, h * P:(h + 1) * P], ktok[:, h, :], v0s[:, h, :], start=True, stop=True)
                ins.then_inc(S("s1_psum"), 1)
                stream(U["ks"])
                pe.wait_ge(S("st"), j + 1)
                for h in range(2):
                    pe.matmul(mx[0][:, h * P:(h + 1) * P], kq[:, h, 1, 0, :], st[:, h, :], start=True, stop=True)
                    ins = pe.matmul(mx[0][:, (2 + h) * P:(3 + h) * P], kq[:, h, 1, 1, :], st[:, h, :], start=True, stop=True)
                ins.then_inc(S("ks_psum"), 1)
                stream(U["v1"])
                pe.wait_ge(S("vr1"), 2 * j + 2)
                for h in range(2):
                    ins = pe.matmul(mx[1][:, (2 + h) * P:(3 + h) * P], gt[:, 2 * h + 1, :], vr[:, 2 * h + 1, :], start=True, stop=True)
                ins.then_inc(S("v1_psum"), 1)
                stream(U["o"])
                pe.wait_ge(S("v0"), j + 1)
                pe.wait_ge(S("v1"), j + 1)
                for h in range(2):
                    for c, v in enumerate((v0, v1)):
                        ins = pe.matmul(mx[2][:, (2 * h + c) * P:(2 * h + c + 1) * P], aT[:, 2 * h + c, :], v[:, h, :], start=True, stop=True)
                ins.then_inc(S("o_psum"), 1)
                stream(U["tr"])
                out_transposes(p, mx[3])

            def out_transposes(p, bank):
                pe.wait_ge(S("on"), p + 1)
                for n in range(4):
                    ins = pe.transpose(bank[:, n * P:(n + 1) * P], on[:, n // 2, n % 2, :], ident)
                ins.then_inc(S("otr"), 1)

            def mix_ret(p, j, base):
                U = {k: base + v for k, v in U_RET.items()}
                stream(U["gram"])
                pe.wait_ge(S("evac"), 8 * p + 8)
                pe.wait_ge(S("yf_done"), p)
                for h in range(2):
                    for c in range(C):
                        n = 2 * h + c
                        ins = pe.matmul(mx[0][:, n * P:(n + 1) * P], chunk_in(h, 1, c), chunk_in(h, 0, c), start=True, stop=True)
                ins.then_inc(S("r_gram"), 1)
                for h in range(2):
                    for c in range(C):
                        n = 2 * h + c
                        pe.transpose(mx[1][:, n * P:(n + 1) * P], chunk_in(h, 2, c), ident)
                    ins = pe.transpose(mx[2][:, h * P:(h + 1) * P], chunk_in(h, 1, 0), ident)
                ins.then_inc(S("r_vtok"), 1)
                stream(U["s1"])
                pe.wait_ge(S("r_vr"), j + 1)
                pe.wait_ge(S("r_ktok"), 2 * j + 2)
                for h in range(2):
                    ins = pe.matmul(mx[3][:, h * P:(h + 1) * P], ktok[:, h, :], vr[:, 2 * h, :], start=True, stop=True)
                ins.then_inc(S("r_s1_psum"), 1)
                stream(U["qs"])
                pe.wait_ge(S("r_st"), j + 1)
                for h in range(2):
                    pe.matmul(mx[3][:, (2 + h) * P:(3 + h) * P], chunk_in(h, 0, 1), st[:, h, :], start=True, stop=True)
                pe.wait_ge(S("r_at"), 2 * j + 2)
                for n in range(4):
                    ins = pe.matmul(mx[2][:, n * P:(n + 1) * P], aT[:, n, :], vr[:, n, :], start=True, stop=True)
                ins.then_inc(S("o_psum"), 1)
                stream(U["tr"])
                out_transposes(p, mx[0])

            def mix_moba(p, j, base):
                U = {k: base + v for k, v in U_MOBA.items()}
                pr = th[:, 6 * P:12 * P].rearrange("p (h c) -> p h c", h=2)
                pt = [kq[:, h].rearrange("p c k t -> p (c k t)") for h in range(2)]
                stream(U["nrm"])
                pe.wait_ge(S("evac"), 8 * p + 8)
                pe.wait_ge(S("yf_done"), p)
                pe.wait_ge(S("m_sq"), 2 * j + 2)
                sqv = sq[:, :, :, :, :].rearrange("p h c k t -> p (h c k) t")
                for n in range(8):
                    ins = pe.matmul(mx[3][:, n:n + 1], sqv[:, n, :], ones[:, 0:1], start=True, stop=True)
                ins.then_inc(S("m_nrm"), 1)
                for n in range(4):
                    ins = pe.transpose(mx[1][:, n * P:(n + 1) * P], chunk_in(n // 2, 2, n % 2), ident)
                ins.then_inc(S("m_vtok"), 1)
                stream(U["bc"])
                pe.wait_ge(S("m_pow"), j + 1)
                for n in range(4):
                    at = 64 + 4 * (n // 2) + 2 + n % 2
                    ins = pe.matmul(mx[2][:, n * P:(n + 1) * P], sm[:, at:at + 1].broadcast_to([P, P]), ident, start=True, stop=True)
                ins.then_inc(S("m_bc"), 1)
                stream(U["score"])
                pe.wait_ge(S("knT"), 2 * j + 2)
                for h in range(2):
                    bank = mx[(0, 3)[h]]
                    pe.matmul(bank[:, 0:P], chunk_in(h, 0, 0), vT[:, h, 0:P], start=True, stop=True)
                    ins = pe.matmul(bank[:, P:3 * P], chunk_in(h, 0, 1), vT[:, h, :], start=True, stop=True)
                ins.then_inc(S("score"), 1)
                stream(U["pt"])
                for h in range(2):
                    pe.wait_ge(S("m_prob"), 4 * j + 2 * h + 2)
                    for i in range(3):
                        ins = pe.transpose(mx[(2, 0)[h]][:, i * P:(i + 1) * P], pr[:, h, i * P:(i + 1) * P], ident)
                    ins.then_inc(S("pt_psum"), 1)
                stream(U["o"])
                pe.wait_ge(S("m_vr"), j + 1)
                pe.wait_ge(S("pt_a"), j + 1)
                pe.wait_ge(S("pt_v"), j + 1)
                for h in range(2):
                    pe.matmul(mx[1][:, h * T:(h + 1) * T], vr[:, 2 * h, :], pt[h][:, 0:T], start=True, stop=False)
                    ins = pe.matmul(mx[1][:, h * T + P:(h + 1) * T], vr[:, 2 * h + 1, :], pt[h][:, T:T + P], start=False, stop=True)
                ins.then_inc(S("otr"), 1)

            stream(128)
            for p, (kind, j) in enumerate(PAIRS):
                {"gdn": mix_gdn, "ret": mix_ret, "moba": mix_moba}[kind](p, j, 128 * (p + 1))
                stream(128 * (p + 2))
            stream(64 * GROUPS)


_INS = ['x', 'norm_w', 'w_in', 'conv_w', 'a_log', 'dt_bias', 'ret_norm_w', 'gdn_norm_w', 'q_norm_w', 'k_norm_w',
        'w_out']


def kernel(**inputs):
    import numpy as _np
    import concourse.bacc as _bacc
    from concourse import mybir as _mybir
    from concourse.bass_utils import run_bass_kernel_spmd as _run

    nc = _bacc.Bacc("TRN2", target_bir_lowering=False, num_devices=1)
    arrays, args = {}, []
    for name in _INS:
        a = _np.ascontiguousarray(inputs[name])
        arrays[f"in_{name}_dram"] = a
        args.append(nc.dram_tensor(f"in_{name}_dram", a.shape, _mybir.dt.from_np(a.dtype), kind="ExternalInput").ap())
    arrays["table_dram"] = constants()
    args.append(nc.dram_tensor("table_dram", (P, K_COLS), F32, kind="ExternalInput").ap())
    args.append(nc.dram_tensor("out_0_dram", (1, T, D), F32, kind="ExternalOutput").ap())
    layer(nc, *args)
    r = _run(nc, [arrays], core_ids=[0])
    return r.results[0]["out_0_dram"]
```

```python
from contextlib import ExitStack

import numpy as np

import concourse.bass as bass
from concourse import mybir

F32 = mybir.dt.float32
F32R = mybir.dt.float32r
ALU = mybir.AluOpType
ACT = mybir.ActivationFunctionType
AX = mybir.AxisListType

P = 128
D = 2048
T = 256
C = T // P
KC = D // P
RET, GDN, MOBA = 4, 6, 6
RET_COL = 0
GDN_COL = 4 * RET * P
AB_COL = GDN_COL + 4 * GDN * P
MOBA_COL = AB_COL + 2 * GDN
AB = 2 * GDN
EPS = 1e-6
SCALE = float(P) ** -0.5
CONV = 4
PAD = CONV - 1

TK = 2
TPH = KC // TK
UPT = 4 * TK
HEADS = RET + GDN + MOBA
GROUPS = HEADS + D // 512
NRAW, NSPLIT, LEAD = 8, 4, 3
TILES = GROUPS * TPH

PAIRS = [("gdn", 0), ("gdn", 1), ("gdn", 2), ("ret", 0), ("ret", 1), ("moba", 0), ("moba", 1), ("moba", 2)]
Y_BLOCK = {"ret": 0, "gdn": RET, "moba": RET + GDN}
VEC_LO = (1, 3, 5, 7)

LEVELS = 7

K_ID, K_UP, K_ONE = 0, P, 2 * P
K_POW = 3 * P
K_FIRST = K_POW + 8
K_LEVEL = K_FIRST
K_DECAY = K_LEVEL + LEVELS * P
K_DIST = K_DECAY + RET * P
K_KDEC = K_DIST + 3 * P
K_QDEC = K_KDEC + RET
K_COLS = K_QDEC + RET

R_CONV = 0
R_NORM = R_CONV + CONV * 3 * GDN
R_RET = R_NORM + KC
R_GDN = R_RET + RET
R_Q = R_GDN + 1
R_K = R_Q + 1
R_ROWS = R_K + 1

U_GDN = {"gram": 30, "vtok": 33}
for _l in range(LEVELS):
    U_GDN[f"x{_l}"] = 40 + 10 * _l
    U_GDN[f"y{_l}"] = 43 + 10 * _l
    U_GDN[f"t{_l}"] = 47 + 10 * _l
U_GDN.update(v0=107, s1=111, ks=115, v1=119, o=123)
U_TAIL = 4
U_RET = {"gram": 8, "s1": 14, "qs": 20, "o": 20, "tr": 38}
U_MOBA = {"nrm": 8, "bc": 16, "score": 22, "pt": 40, "o": 48}


def constants():
    t = np.zeros((P, K_COLS), np.float64)
    p, c = np.arange(P)[:, None], np.arange(P)[None, :]
    t[:, K_ID:K_ID + P] = p == c
    t[:, K_UP:K_UP + P] = p <= c
    t[:, K_ONE:K_ONE + P] = 1
    for l in range(LEVELS):
        b = 2 ** l
        t[:, K_LEVEL + l * P:K_LEVEL + (l + 1) * P] = ((p // b) % 2 == 1) & (c // b == p // b - 1)
    for h in range(RET):
        lg = np.log1p(-2.0 ** (-5.0 - h))
        t[:, K_DECAY + h * P:K_DECAY + (h + 1) * P] = np.where(c >= p, np.exp(np.maximum(c - p, 0) * lg), 0) * SCALE
        t[:, K_KDEC + h] = np.exp((P - 1 - np.arange(P)) * lg) * SCALE
        t[:, K_QDEC + h] = np.exp((np.arange(P) + 1) * lg)
    s = np.arange(2 * P)[None, :]
    t[:, K_DIST:K_DIST + P] = np.where(c <= p, c - p, -1e30)
    t[:, K_DIST + P:K_DIST + 3 * P] = np.where(s <= p + P, s - p - P, -1e30)
    t[:, K_POW:K_POW + 8] = -0.5
    return t.astype(np.float32)


def layer(nc, x, norm_w, w_in, conv_w, a_log, dt_bias, ret_norm_w, gdn_norm_w, q_norm_w, k_norm_w, w_out,
          table, out):
    ctx = ExitStack()
    with ctx:
        def sb(name, shape, dt=F32):
            return ctx.enter_context(nc.sbuf_tensor(name, shape, dt))

        sems = {}

        def S(name):
            if name not in sems:
                sems[name] = ctx.enter_context(nc.semaphore(name))
            return sems[name]

        w_raw = sb("w_raw", [P, NRAW, TK * 512])
        w_hi = sb("w_hi", [P, NSPLIT, TK * 512], F32R)
        w_lo = sb("w_lo", [P, NSPLIT, TK * 512], F32R)
        hT = sb("hT", [P, KC, 2, T], F32R)
        yT = sb("yT", [P, KC, 2, T], F32R)
        cst = sb("cst", [P, K_COLS])
        prow = sb("prow", [R_ROWS, P])
        pcol = sb("pcol", [P, R_ROWS])
        raw = sb("raw", [P, 2, 4, PAD + T])
        ev_lo = sb("ev_lo", [P, 4, T])
        cv = sb("cv", [P, 2 * 3 * T])
        th = sb("th", [P, 2 * 3 * T])
        kq = sb("kq", [P, 2, C, 2, P])
        sq = sb("sq", [P, 2, C, 2, P])
        vT = sb("vT", [P, 2, T])
        zg = sb("zg", [P, 2, T])
        dd = sb("dd", [P, 4, P])
        ee = sb("ee", [P, 4, P])
        er = sb("er", [P, 4, P])
        mT = sb("mT", [P, 4, P])
        aT = sb("aT", [P, 4, P])
        vr = sb("vr", [P, 4, P])
        ktok = sb("ktok", [P, 2, P])
        gm = sb("gm", [P, 4, P])
        gt = sb("gt", [P, 4, P])
        xs = sb("xs", [P, 4, P])
        v0 = sb("v0", [P, 2, P])
        v0s = sb("v0s", [P, 2, P])
        v1 = sb("v1", [P, 2, P])
        st = sb("st", [P, 2, P])
        os_ = sb("os", [P, 2, C, P])
        on = sb("on", [P, 2, C, P])
        yf = sb("yf", [P, 2, T])
        ab = sb("ab", [P, 24, C, GDN])
        wab = sb("wab", [P, KC, AB])
        wab_hi = sb("wab_hi", [P, KC, AB], F32R)
        wab_lo = sb("wab_lo", [P, KC, AB], F32R)
        bias = sb("bias", [P, 2, GDN])
        sm = sb("sm", [P, 128])

        pj = [ctx.enter_context(nc.psum_tensor(f"pj{s}", [P, 512], F32)) for s in range(4)]
        mx = [ctx.enter_context(nc.psum_tensor(f"mx{s}", [P, 512], F32)) for s in range(4)]

        ident = cst[:, K_ID:K_ID + P]
        upper = cst[:, K_UP:K_UP + P]
        ones = cst[:, K_ONE:K_ONE + P]
        x_sb = w_raw[:, NRAW // 2:, :].rearrange("p a n -> p (a n)").rearrange("p (c n) -> p c n", c=C)

        junk_a, junk_v = kq[:, :].rearrange("p h c k t -> p (h c k t)"), sq[:, :].rearrange("p h c k t -> p (h c k t)")
        rstd_row = yf[:, 0, :]

        def h_tmp(k, n=1):
            buf = (cv, th)[k // 2 % 6 // 3]
            at = k // 2 % 3 * 512 + k % 2 * T
            return buf[:, at:at + n * T]

        def four(ap):
            return ap.rearrange("p (n c) -> p n c", c=P)

        A_G, A_BETA, A_GC, A_NGC, A_EGC, A_NEGC, A_GL, A_Z, A_E, A_U, A_L, A_T1, A_T2, A_T3, A_ELAST, A_TB = range(16)

        def chunk_in(h, s, c):
            return raw[:, h, s, PAD + c * P:PAD + (c + 1) * P]

        def lo_count(n, vec):
            v = n // TPH * len(VEC_LO) + sum(q < n % TPH for q in VEC_LO)
            return v if vec else n - v

        def wait_lo(eng, n):
            if n % TPH in VEC_LO:
                eng.wait_ge(S("lo_vec"), lo_count(n + 1, True))
            else:
                eng.wait_ge(S("lo_pool"), lo_count(n + 1, False))

        def wait_used(eng, n):
            g, q = n // TPH, n % TPH
            if q < TPH - 1:
                eng.wait_ge(S("tile_used"), (TPH - 1) * g + q + 1)
            elif g < HEADS:
                eng.wait_ge(S("proj_done"), 4 * (g + 1))
            else:
                eng.wait_ge(S("out_psum"), 2 * (g + 1 - HEADS))

        def evacuated(v):
            head, rest = divmod(v + 6, 64)
            return (head - 1, rest // 2) if 0 < head <= HEADS and rest < 8 and rest % 2 == 0 else None

        def low_part(eng, n, name):
            eng.wait_ge(S("hi_done"), n + 1)
            eng.tensor_tensor(w_lo[:, n % NSPLIT, :], w_raw[:, n % NRAW, :],
                              w_hi[:, n % NSPLIT, :].bitcast(F32), ALU.subtract).then_inc(S(name), 1)

        block = ctx.enter_context(nc.Block())

        @block.sync
        def _(sp):
            sp.dma_start(cst[:, 0:K_FIRST], table[:, 0:K_FIRST]).then_inc(S("cst_in"), 16)
            sp.dma_start(x_sb[:, 0, :], x[0, 0:P, :]).then_inc(S("x0_in"), 16)
            sp.dma_start(x_sb[:, 1, :], x[0, P:T, :]).then_inc(S("x1_in"), 16)

            def load(n):
                group, q = n // TPH, n % TPH
                rows = slice(q * TK * P, (q + 1) * TK * P)
                if n >= NRAW:
                    wait_lo(sp, n - NRAW)
                elif n >= NRAW // 2:
                    sp.wait_ge(S("hT_psum"), 8)
                dst = w_raw[:, n % NRAW, :].rearrange("p (k n) -> p k n", k=TK)
                if group < HEADS:
                    kind, j = PAIRS[group // 2]
                    heads = {"gdn": GDN, "ret": RET, "moba": MOBA}[kind]
                    col = {"gdn": GDN_COL, "ret": RET_COL, "moba": MOBA_COL}[kind]
                    h = 2 * j + group % 2
                    src = w_in[0, rows, col:col + 4 * heads * P].rearrange(
                        "(k p) (s c) -> p k s c", p=P, s=4)[:, :, :, h * P:(h + 1) * P]
                    dst = dst.rearrange("p k (s c) -> p k s c", s=4)
                    for k in range(TK):
                        sp.dma_start(dst[:, k], src[:, k]).then_inc(S(f"w_in{n % NRAW}"), 16)
                else:
                    g = group - HEADS
                    src = w_out[0, rows, g * 512:(g + 1) * 512].rearrange("(k p) c -> p k c", p=P)
                    for k in range(TK):
                        sp.dma_start(dst[:, k], src[:, k]).then_inc(S(f"w_in{n % NRAW}"), 16)

            def load_x(n):
                g, c = n // 2, n % 2
                if n >= 3:
                    sp.wait_ge(S("out_ready"), n - 2)
                sp.dma_start(cv[:, (n % 3) * 512:(n % 3 + 1) * 512],
                             x[0, c * P:(c + 1) * P, g * 512:(g + 1) * 512]).then_inc(S(f"xr_in{n % 3}"), 16)

            for n in range(TILES):
                load(n)
                group = n // TPH - 1 - HEADS
                if group >= 0 and n % TPH == 3:
                    load_x(2 * group)
                    load_x(2 * group + 1)
                if n == NRAW // 2 - 1:
                    sp.dma_start(cst[:, K_FIRST:], table[:, K_FIRST:]).then_inc(S("cst_in2"), 16)
            load_x(6)
            load_x(7)

        @block.scalar
        def _(act):
            act.dma_start(prow[R_NORM:R_RET, :], norm_w[0].rearrange("(k p) -> k p", p=P)).then_inc(S("norm_in"), 16)
            act.dma_start(prow[R_CONV:R_NORM, :], conv_w[0].rearrange("j (t c) -> (j t) c", c=P)).then_inc(S("param_in"), 16)
            act.dma_start(prow[R_RET:R_GDN, :], ret_norm_w[0]).then_inc(S("param_in1"), 16)
            act.dma_start(prow[R_GDN:R_Q, :], gdn_norm_w).then_inc(S("param_in2"), 16)
            act.dma_start(prow[R_Q:R_K, :], q_norm_w).then_inc(S("param_in3"), 16)
            act.dma_start(prow[R_K:R_ROWS, :], k_norm_w).then_inc(S("param_in4"), 16)
            act.dma_start(wab[:, :, :], w_in[0, :, AB_COL:AB_COL + AB].rearrange("(k p) c -> p k c", p=P)).then_inc(S("wab_in"), 16)
            act.dma_start(bias[:, 0, :], a_log[0:1, :].broadcast_to([P, GDN])).then_inc(S("bias_in"), 16)
            act.dma_start(bias[:, 1, :], dt_bias[0:1, :].broadcast_to([P, GDN])).then_inc(S("bias_in1"), 16)

            def high_part(n):
                act.wait_ge(S(f"w_in{n % NRAW}"), 16 * TK * (n // NRAW + 1))
                if n >= NSPLIT:
                    wait_used(act, n - NSPLIT)
                act.activation(w_hi[:, n % NSPLIT, :], w_raw[:, n % NRAW, :], ACT.Copy).then_inc(S("hi_done"), 1)

            def evacuate_low(g, s):
                act.wait_ge(S("proj_done"), 4 * g + s + 1)
                act.activation(ev_lo[:, s, :], pj[s][:, T:2 * T], ACT.Copy).then_inc(S("ev_lo_done"), 1)

            def send(n):
                g, c = n // 2, n % 2
                act.wait_ge(S("out_ready"), n + 1)
                act.dma_start(out[0, c * P:(c + 1) * P, g * 512:(g + 1) * 512],
                              sq[:, n % 2].rearrange("p c k t -> p (c k t)")).then_inc(S(f"out_sent{n % 2}"), 16)

            pos = [0]

            def advance(u):
                for v in range(pos[0], min(u, 64 * GROUPS)):
                    if evacuated(v):
                        evacuate_low(*evacuated(v))
                    if v % UPT == 0 and v // UPT + LEAD < TILES:
                        high_part(v // UPT + LEAD)
                    if v > 64 * HEADS and v % 64 == 0:
                        send(2 * (v // 64 - HEADS) - 2)
                        send(2 * (v // 64 - HEADS) - 1)
                pos[0] = max(pos[0], u)

            act.wait_ge(S("x0_in"), 16)
            act.activation(junk_a,
                           x_sb[:, 0, 0:1024], ACT.Square, accum_out=sm[:, 0:1]).then_inc(S("ss_act"), 1)
            act.wait_ge(S("x1_in"), 16)
            act.wait_ge(S("ss_act"), 1)
            act.activation(junk_a, x_sb[:, 1, 0:1024], ACT.Square, accum_out=sm[:, 2:3]).then_inc(S("ss_act"), 1)
            high_part(0)
            for k in range(KC):
                act.wait_ge(S("h_tmp"), k // 2 + 1)
                act.activation(hT[:, k, 0, :], h_tmp(k), ACT.Copy,
                               scale=pcol[:, R_NORM + k:R_NORM + k + 1]).then_inc(S("h_hi"), 1)
                if k == 1 or k == 3:
                    high_part(k // 2 + 1)
                if k % 2 and k >= 5:
                    advance(UPT * (k // 2 - 1))
            act.wait_ge(S("wab_in"), 16)
            act.activation(wab_hi[:, :, :], wab[:, :, :], ACT.Copy).then_inc(S("wab_hi_done"), 1)
            advance(64)

            act.wait_ge(S("bias_in"), 16)
            act.activation(sm[:, 16:16 + GDN], bias[:, 0, :], ACT.Exp).then_inc(S("expa_done"), 1)
            advance(65)
            act.wait_ge(S("ab_psum"), 1)
            act.activation(ab[:, A_TB], mx[0][:, 0:2 * AB].rearrange("p (c h) -> p c h", c=C)[:, :, GDN:], ACT.Tanh,
                           scale=0.5).then_inc(S("tanh_b"), 1)
            act.wait_ge(S("negabs_z"), 1)
            act.activation(ab[:, A_E], ab[:, A_T1], ACT.Exp).then_inc(S("exp_z"), 1)
            act.wait_ge(S("one_plus"), 1)
            act.activation(ab[:, A_L], ab[:, A_U], ACT.Ln).then_inc(S("ln_u"), 1)
            advance(90)
            act.wait_ge(S("gc_done"), 1)
            act.activation(ab[:, A_EGC], ab[:, A_GC], ACT.Exp).then_inc(S("egc_done"), 1)
            act.activation(ab[:, A_ELAST, 0, :], ab[:, A_T2, 0, :], ACT.Exp).then_inc(S("egc_done"), 1)

            def gate_tanh(p):
                act.wait_ge(S("evac"), 8 * (p + 1))
                if p:
                    act.wait_ge(S("yf_done"), p)
                act.activation(zg[:, :, :], raw[:, :, 3, PAD:], ACT.Tanh, scale=0.5).then_inc(S("tanh_z"), 1)

            def split_y(p, y0):
                act.wait_ge(S("yf_done"), p + 1)
                act.activation(yT[:, y0:y0 + 2, 0, :], yf[:, :, :], ACT.Copy).then_inc(S("y_hi"), 1)

            def tail(p):
                if p and PAIRS[p - 1][0] == "gdn":
                    split_y(p - 1, Y_BLOCK["gdn"] + 2 * PAIRS[p - 1][1])

            def mix_gdn(p, j, base):
                U = {k: base + v for k, v in U_GDN.items()}
                advance(base + 1)
                tail(p)
                th3, cv3 = (b[:, :].rearrange("p (h s t) -> p h s t", h=2, s=3) for b in (th, cv))
                for h in range(2):
                    advance(base + 10 + 8 * h)
                    act.wait_ge(S("conv_kq"), 2 * j + h + 1)
                    act.activation(th3[:, h, 0:2], cv3[:, h, 0:2], ACT.Tanh, scale=0.5).then_inc(S("tanh_kq"), 1)
                for h in range(2):
                    act.wait_ge(S("silu_kq"), 4 * j + 2 * h + 2)
                    act.activation(sq[:, h], kq[:, h], ACT.Square).then_inc(S("sq"), 1)
                gate_tanh(p)
                act.wait_ge(S("clip_done"), 4 * (j + 1))
                act.activation(ee[:, :, :], dd[:, :, :], ACT.Exp).then_inc(S("exp_decay"), 1)
                act.wait_ge(S("conv_v"), 2 * j + 2)
                act.activation(th3[:, :, 2], cv3[:, :, 2], ACT.Tanh, scale=0.5).then_inc(S("tanh_v"), 1)
                advance(U["gram"])
                act.wait_ge(S("g_norm"), j + 1)
                act.activation(ktok[:, :, :], mx[3][:, 0:2 * P].rearrange("p (h c) -> p h c", h=2), ACT.Copy).then_inc(S("ktok"), 1)
                advance(U["vtok"])
                act.wait_ge(S("vtok"), j + 1)
                act.wait_ge(S("g_scalars"), j + 1)
                for n in range(4):
                    act.activation(vr[:, n, :], mx[2][:, n * P:(n + 1) * P], ACT.Copy,
                                   scale=sm[:, 40 + n:41 + n]).then_inc(S("vr"), 1)
                for l in range(LEVELS - 1):
                    advance(U[f"t{l}"])
                    act.wait_ge(S("gtr"), (LEVELS - 1) * j + l + 1)
                    act.activation(gm[:, :, :], four(mx[2][:, :]), ACT.Copy).then_inc(S("gm"), 1)
                advance(U["v0"])
                act.wait_ge(S("v0s"), 2 * j + 2)
                act.activation(v0[:, :, :], mx[3][:, 0:2 * P].rearrange("p (h c) -> p h c", h=2), ACT.Copy).then_inc(S("v0"), 1)
                advance(U["s1"])
                act.wait_ge(S("s1_psum"), j + 1)
                act.activation(st[:, :, :], mx[1][:, 0:2 * P].rearrange("p (h c) -> p h c", h=2), ACT.Copy).then_inc(S("st"), 1)
                advance(U["v1"])
                act.wait_ge(S("v1_psum"), j + 1)
                act.activation(v1[:, :, :], mx[1][:, 2 * P:4 * P].rearrange("p (h c) -> p h c", h=2), ACT.Copy).then_inc(S("v1"), 1)
                advance(U["o"])
                act.wait_ge(S("o_psum"), p + 1)
                act.activation(os_[:, :, :, :], mx[2][:, :].rearrange("p (h c e) -> p h c e", h=2, c=C), ACT.Copy).then_inc(S("os"), 1)
                squares(p)

            def squares(p):
                act.wait_ge(S("os_full"), p + 1)
                for n in range(4):
                    act.wait_ge(S("os_sq"), 4 * p + n) if 4 * p + n else None
                    act.activation(xs[:, 0, :], os_[:, n // 2, n % 2, :], ACT.Square,
                                   accum_out=sm[:, 48 + n:49 + n]).then_inc(S("os_sq"), 1)

            def mix_ret(p, j, base):
                U = {k: base + v for k, v in U_RET.items()}
                advance(base + 1)
                tail(p)
                gate_tanh(p)
                advance(U["gram"])
                act.wait_ge(S("r_vtok"), j + 1)
                act.activation(vr[:, :, :], four(mx[1][:, :]), ACT.Copy).then_inc(S("r_vr"), 1)
                for h in range(2):
                    act.activation(ktok[:, h, :], mx[2][:, h * P:(h + 1) * P], ACT.Copy,
                                   scale=cst[:, K_KDEC + 2 * j + h:K_KDEC + 2 * j + h + 1]).then_inc(S("r_ktok"), 1)
                advance(U["s1"])
                act.wait_ge(S("r_s1_psum"), j + 1)
                act.activation(st[:, :, :], mx[3][:, 0:2 * P].rearrange("p (h c) -> p h c", h=2), ACT.Copy).then_inc(S("r_st"), 1)
                advance(U["o"])
                act.wait_ge(S("o_psum"), p + 1)
                act.activation(os_[:, :, :, :], mx[2][:, :].rearrange("p (h c e) -> p h c e", h=2, c=C), ACT.Copy).then_inc(S("os"), 1)
                squares(p)
                advance(U["tr"])
                split_y(p, Y_BLOCK["ret"] + 2 * j)

            def mix_moba(p, j, base):
                U = {k: base + v for k, v in U_MOBA.items()}
                lg = th[:, 0:6 * P].rearrange("p (h c) -> p h c", h=2)
                pr = th[:, 6 * P:12 * P].rearrange("p (h c) -> p h c", h=2)
                advance(base + 1)
                for h in range(2):
                    act.wait_ge(S("evac"), 8 * p + 4 * h + 2)
                    act.activation(sq[:, h].rearrange("p c k t -> p (c k t)").rearrange("p (s t) -> p s t", s=2),
                                   raw[:, h, 0:2, PAD:], ACT.Square).then_inc(S("m_sq"), 1)
                gate_tanh(p)
                advance(U["nrm"])
                act.wait_ge(S("m_vtok"), j + 1)
                act.activation(vr[:, :, :], four(mx[1][:, :]), ACT.Copy).then_inc(S("m_vr"), 1)
                advance(U["score"])
                act.wait_ge(S("score"), j + 1)
                for h in range(2):
                    for c in range(C):
                        a, b = (0, P) if c == 0 else (P, 3 * P)
                        act.activation(lg[:, h, a:b], mx[(0, 3)[h]][:, a:b], ACT.Copy,
                                       scale=sm[:, 64 + 4 * h + c:65 + 4 * h + c]).then_inc(S("m_lg"), 1)
                for n in range(4):
                    h, c = n // 2, n % 2
                    a, b = (0, P) if c == 0 else (P, 3 * P)
                    act.wait_ge(S("m_max"), 4 * j + n + 1)
                    act.activation(pr[:, h, a:b], lg[:, h, a:b], ACT.Exp, bias=sm[:, 72 + n:73 + n],
                                   accum_out=sm[:, 76 + n:77 + n]).then_inc(S("m_exp"), 1)
                advance(U["pt"])
                act.wait_ge(S("pt_psum"), 2 * j + 1)
                act.activation(kq[:, 0].rearrange("p c k t -> p (c k t)")[:, 0:3 * P], mx[2][:, 0:3 * P], ACT.Copy).then_inc(S("pt_a"), 1)
                advance(U["o"])
                split_y(p, Y_BLOCK["moba"] + 2 * j)

            advance(128)
            for p, (kind, j) in enumerate(PAIRS):
                {"gdn": mix_gdn, "ret": mix_ret, "moba": mix_moba}[kind](p, j, 128 * (p + 1))
                advance(128 * (p + 2))
            advance(64 * GROUPS)

            send(6)
            send(7)
            act.wait_ge(S("out_sent0"), 64)
            act.wait_ge(S("out_sent1"), 64)

        @block.gpsimd
        def _(pool):
            pos = [0]

            def advance(u):
                for v in range(pos[0], min(u, 64 * GROUPS)):
                    n = v // UPT + LEAD
                    if v % UPT == 0 and n < TILES and n % TPH not in VEC_LO:
                        low_part(pool, n, "lo_pool")
                pos[0] = max(pos[0], u)

            def power(dst, src, n):
                return pool.tensor_tensor(sm[:, dst:dst + n], sm[:, src:src + n], cst[:, K_POW:K_POW + n], ALU.pow)

            pool.memset(raw[:, :, :, 0:PAD], 0.0).then_inc(S("pad_zero"), 1)
            pool.wait_ge(S("cst_in"), 16)
            pool.wait_ge(S("ms_done"), 1)
            power(6, 4, 2).then_inc(S("rstd_done"), 1)
            for n in range(LEAD):
                if n not in VEC_LO:
                    low_part(pool, n, "lo_pool")
            advance(56)
            pool.wait_ge(S("wab_hi_done"), 1)
            pool.tensor_tensor(wab_lo[:, :, :], wab[:, :, :], wab_hi[:, :, :].bitcast(F32), ALU.subtract).then_inc(S("wab_lo_done"), 1)

            def split_y(p, y0):
                pool.wait_ge(S("y_hi"), p + 1)
                pool.tensor_tensor(yT[:, y0:y0 + 2, 1, :], yf[:, :, :], yT[:, y0:y0 + 2, 0, :].bitcast(F32),
                                   ALU.subtract).then_inc(S("y_lo"), 1)

            def tail(p):
                if p and PAIRS[p - 1][0] == "gdn":
                    split_y(p - 1, Y_BLOCK["gdn"] + 2 * PAIRS[p - 1][1])

            def rms_power(p):
                pool.wait_ge(S("o_ms"), p + 1)
                power(56, 52, 4).then_inc(S("o_pow"), 1)

            def mix_gdn(p, j, base):
                U = {k: base + v for k, v in U_GDN.items()}
                advance(base + 1)
                tail(p)
                advance(U["gram"])
                pool.wait_ge(S("g_norm"), j + 1)
                power(32, 24, 8).then_inc(S("g_pow"), 1)
                for l in range(LEVELS):
                    advance(U[f"x{l}"])
                advance(U["o"])
                rms_power(p)

            def mix_ret(p, j, base):
                U = {k: base + v for k, v in U_RET.items()}
                advance(base + 1)
                tail(p)
                advance(U["o"])
                rms_power(p)
                advance(U["tr"])
                split_y(p, Y_BLOCK["ret"] + 2 * j)

            def mix_moba(p, j, base):
                U = {k: base + v for k, v in U_MOBA.items()}
                advance(U["nrm"])
                pool.wait_ge(S("m_norm"), j + 1)
                power(64, 80, 8).then_inc(S("m_pow"), 1)
                advance(U["o"])
                split_y(p, Y_BLOCK["moba"] + 2 * j)

            advance(128)
            for p, (kind, j) in enumerate(PAIRS):
                {"gdn": mix_gdn, "ret": mix_ret, "moba": mix_moba}[kind](p, j, 128 * (p + 1))
                advance(128 * (p + 2))
            advance(64 * GROUPS)

        @block.vector
        def _(dve):
            pos = [0]

            def evacuate(g, s):
                dve.wait_ge(S("ev_lo_done"), 4 * g + s + 1)
                if g == 0 and s == 0:
                    dve.wait_ge(S("pad_zero"), 1)
                dve.tensor_tensor(raw[:, g % 2, s, PAD:], pj[s][:, 0:T], ev_lo[:, s, :], ALU.add).then_inc(S("evac"), 1)

            def residual(n):
                g, c = n // 2, n % 2
                dve.wait_ge(S("out_psum"), n + 1)
                dve.wait_ge(S(f"xr_in{n % 3}"), 16 * (n // 3 + 1))
                if n >= 2:
                    dve.wait_ge(S(f"out_sent{n % 2}"), 16 * (n // 2))
                dve.tensor_tensor(sq[:, n % 2].rearrange("p c k t -> p (c k t)"), pj[n % 4][:, :],
                                  cv[:, (n % 3) * 512:(n % 3 + 1) * 512], ALU.add).then_inc(S("out_ready"), 1)

            def advance(u):
                for v in range(pos[0], min(u, 64 * GROUPS)):
                    if evacuated(v):
                        evacuate(*evacuated(v))
                    n = v // UPT + LEAD
                    if v % UPT == 0 and n < TILES and n % TPH in VEC_LO:
                        low_part(dve, n, "lo_vec")
                    if v > 64 * HEADS and v % 64 == 0:
                        residual(2 * (v // 64 - HEADS) - 2)
                        residual(2 * (v // 64 - HEADS) - 1)
                pos[0] = max(pos[0], u)

            for c in range(C):
                dve.wait_ge(S(f"x{c}_in"), 16)
                if c:
                    dve.wait_ge(S("ss_vec"), c)
                dve.scalar_tensor_tensor(junk_v, x_sb[:, c, 1024:], 1.0, x_sb[:, c, 1024:], ALU.mult, ALU.mult,
                                         accum_out=sm[:, 2 * c + 1:2 * c + 2]).then_inc(S("ss_vec"), 1)
            dve.wait_ge(S("params_psum"), 1)
            dve.tensor_copy(pcol[:, :], mx[3][:, 0:R_ROWS]).then_inc(S("pcol_done"), 1)
            dve.wait_ge(S("ss_vec"), C)
            dve.wait_ge(S("ss_act"), C)
            halves = sm[:, 0:4].rearrange("p (c h) -> p c h", h=2)
            dve.tensor_tensor(sm[:, 8:10], halves[:, :, 0], halves[:, :, 1], ALU.add).then_inc(S("ss2"), 1)
            dve.wait_ge(S("ss2"), 1)
            dve.tensor_scalar(sm[:, 4:6], sm[:, 8:10], 1.0 / D, EPS, ALU.mult, ALU.add).then_inc(S("ms_done"), 1)
            dve.wait_ge(S("rstd_psum"), 1)
            dve.tensor_copy(rstd_row, mx[3][:, 0:T]).then_inc(S("rstd_row"), 1)
            dve.wait_ge(S("rstd_row"), 1)

            def norm_two(b):
                dve.wait_ge(S("hT_psum"), b + 1)
                if b >= 6:
                    dve.wait_ge(S("h_hi"), 2 * (b - 6) + 2)
                    dve.wait_ge(S("h_lo"), 2 * (b - 6) + 2)
                dve.tensor_tensor(h_tmp(2 * b, 2).rearrange("p (k t) -> p k t", k=2),
                                  (pj + mx)[b][:, :].rearrange("p (k t) -> p k t", k=2),
                                  rstd_row.unsqueeze(1).broadcast_to([P, 2, T]), ALU.mult).then_inc(S("h_tmp"), 1)

            for b in range(4):
                norm_two(b)
            for k in range(KC):
                dve.wait_ge(S("h_hi"), k + 1)
                dve.scalar_tensor_tensor(hT[:, k, 1, :], h_tmp(k), pcol[:, R_NORM + k:R_NORM + k + 1],
                                         hT[:, k, 0, :].bitcast(F32), ALU.mult, ALU.subtract).then_inc(S("h_lo"), 1)
                if k == 1:
                    low_part(dve, 1, "lo_vec")
                if k % 2 and k // 2 + 4 < 8:
                    norm_two(k // 2 + 4)
                if k % 2:
                    advance(UPT * (k // 2))
            advance(66)

            dve.wait_ge(S("cst_in"), 16)
            dve.wait_ge(S("cst_in2"), 16)
            steps = [0]

            def link(ins):
                steps[0] += 1
                ins.then_inc(S("ab_step"), 1)
                dve.wait_ge(S("ab_step"), steps[0])

            def over_chunks(ap):
                return ap.unsqueeze(1).broadcast_to([P, C, GDN])

            dve.wait_ge(S("bias_in1"), 16)
            dve.wait_ge(S("tanh_b"), 1)
            link(dve.tensor_tensor(ab[:, A_Z], mx[0][:, 0:2 * AB].rearrange("p (c h) -> p c h", c=C)[:, :, 0:GDN],
                                   over_chunks(bias[:, 1, :]), ALU.add))
            link(dve.tensor_scalar(ab[:, A_T1], ab[:, A_Z], -1.0, None, ALU.mult))
            dve.tensor_tensor(ab[:, A_T1], ab[:, A_Z], ab[:, A_T1], ALU.min).then_inc(S("negabs_z"), 1)
            dve.wait_ge(S("exp_z"), 1)
            dve.tensor_scalar(ab[:, A_U], ab[:, A_E], 1.0, None, ALU.add).then_inc(S("one_plus"), 1)
            dve.wait_ge(S("one_plus"), 1)
            link(dve.tensor_scalar(ab[:, A_T2], ab[:, A_U], 1.0, None, ALU.subtract))
            link(dve.tensor_tensor(ab[:, A_T2], ab[:, A_E], ab[:, A_T2], ALU.subtract))
            link(dve.reciprocal(ab[:, A_T3], ab[:, A_U]))
            link(dve.tensor_tensor(ab[:, A_T2], ab[:, A_T2], ab[:, A_T3], ALU.mult))
            dve.wait_ge(S("ln_u"), 1)
            link(dve.tensor_tensor(ab[:, A_T2], ab[:, A_T2], ab[:, A_L], ALU.add))
            link(dve.scalar_tensor_tensor(ab[:, A_T2], ab[:, A_Z], 0.0, ab[:, A_T2], ALU.max, ALU.add))
            dve.wait_ge(S("expa_done"), 1)
            link(dve.tensor_tensor(ab[:, A_T2], ab[:, A_T2], over_chunks(sm[:, 16:16 + GDN]), ALU.mult))
            dve.tensor_scalar(ab[:, A_G], ab[:, A_T2], -1.0, None, ALU.mult).then_inc(S("g_done"), 1)
            dve.wait_ge(S("tanh_b"), 1)
            dve.tensor_scalar(ab[:, A_BETA], ab[:, A_TB], 0.5, 0.5, ALU.mult, ALU.add).then_inc(S("beta_done"), 1)
            advance(90)
            dve.wait_ge(S("cum_psum"), 1)
            link(dve.tensor_copy(ab[:, A_GC], mx[1][:, 0:C * GDN].rearrange("p (c h) -> p c h", c=C)))
            link(dve.tensor_scalar(ab[:, A_NGC], ab[:, A_GC], -1.0, None, ALU.mult))
            dve.tensor_tensor(ab[:, A_T2, 0, :], mx[1][:, C * GDN:(C + 1) * GDN], ab[:, A_GC, 0, :], ALU.subtract).then_inc(S("gc_done"), 1)
            dve.wait_ge(S("egc_done"), 2)
            link(dve.tensor_scalar(ab[:, A_NEGC], ab[:, A_EGC], -1.0, None, ALU.mult))
            dve.tensor_tensor(sm[:, 22:23], pcol[:, R_Q:R_Q + 1], pcol[:, R_K:R_K + 1], ALU.mult).then_inc(S("wqk0"), 1)
            dve.wait_ge(S("wqk0"), 1)
            dve.tensor_scalar(sm[:, 23:24], sm[:, 22:23], SCALE, None, ALU.mult).then_inc(S("wqk"), 1)
            dve.tensor_scalar(sm[:, 96:96 + RET + 1], pcol[:, R_RET:R_GDN + 1], 0.5, None, ALU.mult).then_inc(S("halfw"), 1)

            def gate(p):
                dve.wait_ge(S("tanh_z"), p + 1)
                dve.scalar_tensor_tensor(zg[:, :, :], zg[:, :, :], 1.0, raw[:, :, 3, PAD:], ALU.add, ALU.mult).then_inc(S("zg"), 1)

            def rms_factor(p, gdn):
                dve.wait_ge(S("os_sq"), 4 * p + 4)
                if gdn:
                    dve.tensor_tensor(sm[:, 104:108], sm[:, 48:52], sm[:, 112:116], ALU.mult).then_inc(S("o_ms0"), 1)
                    dve.wait_ge(S("o_ms0"), p + 1)
                    dve.tensor_scalar(sm[:, 52:56], sm[:, 104:108], EPS, None, ALU.add).then_inc(S("o_ms"), 1)
                    dve.wait_ge(S("o_pow"), p + 1)
                    dve.tensor_tensor(sm[:, 60:64], sm[:, 56:60], sm[:, 108:112], ALU.mult).then_inc(S("o_fac"), 1)
                else:
                    dve.tensor_scalar(sm[:, 52:56], sm[:, 48:52], 1.0 / P, EPS, ALU.mult, ALU.add).then_inc(S("o_ms"), 1)
                    dve.wait_ge(S("o_pow"), p + 1)
                    dve.tensor_copy(sm[:, 60:64], sm[:, 56:60]).then_inc(S("o_fac"), 1)
                dve.wait_ge(S("o_fac"), p + 1)
                dve.tensor_tensor(on[:, :, :, :].rearrange("p h c e -> p (h c) e"), os_[:, :, :, :].rearrange("p h c e -> p (h c) e"),
                                  sm[:, 60:64].unsqueeze(2).broadcast_to([P, 4, P]), ALU.mult).then_inc(S("on"), 1)

            def tail(p):
                if p and PAIRS[p - 1][0] == "gdn":
                    gated_pair(p - 1, mx[3], [sm[:, 96 + RET:97 + RET]] * 2)

            def mix_gdn(p, j, base):
                U = {k: base + v for k, v in U_GDN.items()}
                th3, cv3 = (b[:, :].rearrange("p (h s t) -> p h s t", h=2, s=3) for b in (th, cv))

                def tap(h, s, k):
                    return pcol[:, R_CONV + k * 3 * GDN + s * GDN + 2 * j + h:][:, 0:1]

                def conv(h, s, name):
                    at = {0: 1, 1: 0, 2: 2}[s]
                    dst = cv3[:, h, at]
                    dve.wait_ge(S("evac"), 8 * p + 4 * h + s + 1)
                    ins = dve.tensor_scalar(dst, raw[:, h, s, 0:T], tap(h, s, 0), None, ALU.mult)
                    for k in range(1, CONV):
                        conv_step[0] += 1
                        ins.then_inc(S("conv_step"), 1)
                        dve.wait_ge(S("conv_step"), conv_step[0])
                        ins = dve.scalar_tensor_tensor(dst, raw[:, h, s, k:k + T], tap(h, s, k), dst, ALU.mult, ALU.add)
                    return ins

                advance(base + 1)
                tail(p)
                dve.wait_ge(S("gcb"), j + 1)
                for n in range(4):
                    h, c = n // 2, n % 2
                    dve.tensor_scalar(dd[:, n, :], mx[2][:, n * P:(n + 1) * P], ab[:, A_NGC, c, 2 * j + h:2 * j + h + 1], 0.0,
                                      ALU.add, ALU.min).then_inc(S("clip_done"), 1)
                for h in range(2):
                    conv(h, 1, "k").then_inc(S("conv_one"), 1)
                    conv(h, 0, "q").then_inc(S("conv_kq"), 1)
                    advance(base + 6 + 6 * h)
                for h in range(2):
                    dve.wait_ge(S("tanh_kq"), 2 * j + h + 1)
                    dve.wait_ge(S("conv_kq"), 2 * j + h + 1)
                    for i in range(2):
                        dve.scalar_tensor_tensor(kq[:, h, :, i, :], th3[:, h, i].rearrange("p (c t) -> p c t", c=C), 1.0,
                                                 cv3[:, h, i].rearrange("p (c t) -> p c t", c=C), ALU.add, ALU.mult).then_inc(S("silu_kq"), 1)
                for h in range(2):
                    conv(h, 2, "v").then_inc(S("conv_v"), 1)
                gate(p)
                dve.wait_ge(S("exp_decay"), j + 1)
                dve.tensor_tensor(er[:, :, :], ee[:, :, :], upper.unsqueeze(1).broadcast_to([P, 4, P]), ALU.mult).then_inc(S("er1"), 1)
                dve.wait_ge(S("tanh_v"), j + 1)
                dve.wait_ge(S("conv_v"), 2 * j + 2)
                dve.scalar_tensor_tensor(vT[:, :, :], th3[:, :, 2], 1.0, cv3[:, :, 2], ALU.add, ALU.mult).then_inc(S("silu_v"), 1)
                advance(U["gram"])
                dve.wait_ge(S("gram"), j + 1)
                dve.tensor_scalar(sm[:, 24:32], mx[3][:, 2 * P:2 * P + 8], 4 * EPS, None, ALU.add).then_inc(S("g_norm"), 1)
                dve.wait_ge(S("g_pow"), j + 1)
                rk = sm[:, 32:40].rearrange("p (n k) -> p n k", k=2)[:, :, 0]
                rq = sm[:, 32:40].rearrange("p (n k) -> p n k", k=2)[:, :, 1]
                nk = sm[:, 24:32].rearrange("p (n k) -> p n k", k=2)[:, :, 0]
                dve.wait_ge(S("er1"), j + 1)
                dve.tensor_tensor(ee[:, :, :], er[:, :, :], rk.unsqueeze(2).broadcast_to([P, 4, P]), ALU.mult).then_inc(S("er2"), 1)
                dve.scalar_tensor_tensor(sm[:, 40:44], nk, 0.5, rk, ALU.mult, ALU.mult).then_inc(S("g_scalars"), 1)
                dve.tensor_scalar(sm[:, 108:112], rq, SCALE, None, ALU.mult).then_inc(S("g_q"), 1)
                dve.wait_ge(S("g_q"), j + 1)
                dve.scalar_tensor_tensor(sm[:, 112:116], sm[:, 108:112], 1.0 / P, sm[:, 108:112], ALU.mult, ALU.mult).then_inc(S("g_q2"), 1)
                for h in range(2):
                    dve.tensor_tensor(sm[:, 44 + 2 * h:46 + 2 * h], rk[:, 2 * h:2 * h + 2], ab[:, A_BETA, :, 2 * j + h], ALU.mult).then_inc(S("g_b"), 1)
                    dve.tensor_tensor(sm[:, 116 + h:117 + h], rk[:, 2 * h:2 * h + 1], ab[:, A_ELAST, 0, 2 * j + h:2 * j + h + 1], ALU.mult).then_inc(S("g_el"), 1)
                dve.wait_ge(S("g_b"), 2 * j + 2)
                dve.tensor_tensor(gt[:, :, :], ident.unsqueeze(1).broadcast_to([P, 4, P]),
                                  sm[:, 44:48].unsqueeze(2).broadcast_to([P, 4, P]), ALU.mult).then_inc(S("gt"), 1)
                dve.wait_ge(S("er2"), j + 1)
                for i, dst in enumerate((mT, aT)):
                    for h in range(2):
                        dve.tensor_tensor(dst[:, 2 * h:2 * h + 2, :], mx[h][:, :].rearrange("p (c k t) -> p c k t", c=C, k=2)[:, :, i],
                                          ee[:, 2 * h:2 * h + 2, :], ALU.mult).then_inc(S("mt_at"), 1)
                for l in range(LEVELS):
                    advance(U[f"x{l}"])
                    dve.wait_ge(S("x_psum"), LEVELS * j + l + 1)
                    mask = cst[:, K_LEVEL + l * P:K_LEVEL + (l + 1) * P].unsqueeze(1).broadcast_to([P, 4, P])
                    dve.tensor_tensor(xs[:, :, :], four(mx[0][:, :]), mask, ALU.mult).then_inc(S("xs"), 1)
                    advance(U[f"y{l}"])
                    dve.wait_ge(S("y_psum"), LEVELS * j + l + 1)
                    dve.wait_ge(S("gt"), (LEVELS + 1) * j + l + 1)
                    dve.tensor_tensor(gt[:, :, :], gt[:, :, :], four(mx[1][:, :]), ALU.subtract).then_inc(S("gt"), 1)
                advance(U["v0"])
                dve.wait_ge(S("v0_psum"), j + 1)
                dve.wait_ge(S("g_el"), 2 * j + 2)
                for h in range(2):
                    dve.tensor_scalar(v0s[:, h, :], mx[3][:, h * P:(h + 1) * P], sm[:, 116 + h:117 + h], None, ALU.mult).then_inc(S("v0s"), 1)
                advance(U["ks"])
                dve.wait_ge(S("ks_psum"), j + 1)
                dve.wait_ge(S("vr"), 4 * j + 4)
                for h in range(2):
                    dve.scalar_tensor_tensor(vr[:, 2 * h + 1, :], mx[0][:, h * P:(h + 1) * P], ab[:, A_NEGC, 1, 2 * j + h:2 * j + h + 1],
                                             vr[:, 2 * h + 1, :], ALU.mult, ALU.add).then_inc(S("vr1"), 1)
                advance(U["o"])
                dve.wait_ge(S("os"), p + 1)
                for h in range(2):
                    ins = dve.scalar_tensor_tensor(os_[:, h, 1, :], mx[0][:, (2 + h) * P:(3 + h) * P], ab[:, A_EGC, 1, 2 * j + h:2 * j + h + 1],
                                                   os_[:, h, 1, :], ALU.mult, ALU.add)
                ins.then_inc(S("os_full"), 1)
                rms_factor(p, True)

            def gated_pair(p, psum, weights):
                dve.wait_ge(S("otr"), p + 1)
                dve.wait_ge(S("zg"), p + 1)
                for h in range(2):
                    ins = dve.scalar_tensor_tensor(yf[:, h, :], psum[:, h * T:(h + 1) * T], weights[h], zg[:, h, :], ALU.mult, ALU.mult)
                    if h == 1:
                        ins.then_inc(S("yf_done"), 1)

            def mix_ret(p, j, base):
                U = {k: base + v for k, v in U_RET.items()}
                advance(base + 1)
                tail(p)
                gate(p)
                advance(U["gram"])
                dve.wait_ge(S("r_gram"), j + 1)
                for h in range(2):
                    dec = cst[:, K_DECAY + (2 * j + h) * P:K_DECAY + (2 * j + h + 1) * P].unsqueeze(1).broadcast_to([P, C, P])
                    dve.tensor_tensor(aT[:, 2 * h:2 * h + 2, :], mx[0][:, h * T:(h + 1) * T].rearrange("p (c t) -> p c t", c=C), dec,
                                      ALU.mult).then_inc(S("r_at"), 1)
                advance(U["o"])
                dve.wait_ge(S("os"), p + 1)
                for h in range(2):
                    ins = dve.scalar_tensor_tensor(os_[:, h, 1, :], mx[3][:, (2 + h) * P:(3 + h) * P],
                                                   cst[:, K_QDEC + 2 * j + h:K_QDEC + 2 * j + h + 1],
                                                   os_[:, h, 1, :], ALU.mult, ALU.add)
                ins.then_inc(S("os_full"), 1)
                rms_factor(p, False)
                advance(U["tr"])
                gated_pair(p, mx[0], [sm[:, 96 + 2 * j + h:97 + 2 * j + h] for h in range(2)])

            def mix_moba(p, j, base):
                U = {k: base + v for k, v in U_MOBA.items()}
                lg = th[:, 0:6 * P].rearrange("p (h c) -> p h c", h=2)
                pr = th[:, 6 * P:12 * P].rearrange("p (h c) -> p h c", h=2)
                advance(base + 1)
                gate(p)
                advance(U["nrm"])
                dve.wait_ge(S("m_nrm"), j + 1)
                dve.tensor_scalar(sm[:, 80:88], mx[3][:, 0:8], 1.0 / P, EPS, ALU.mult, ALU.add).then_inc(S("m_norm"), 1)
                advance(U["bc"])
                dve.wait_ge(S("m_bc"), j + 1)
                for h in range(2):
                    dve.scalar_tensor_tensor(vT[:, h, :], raw[:, h, 1, PAD:], sm[:, 23:24], mx[2][:, h * T:(h + 1) * T], ALU.mult, ALU.mult).then_inc(S("knT"), 1)
                advance(U["score"])
                for h in range(2):
                    head = 2 * j + h
                    slope = 2.0 ** (-8.0 * (head + 1) / MOBA)
                    dve.wait_ge(S("m_lg"), 4 * j + 2 * h + 2)
                    dve.scalar_tensor_tensor(lg[:, h, :], cst[:, K_DIST:K_DIST + 3 * P], slope, lg[:, h, :], ALU.mult, ALU.add).then_inc(S("m_alibi"), 1)
                    dve.wait_ge(S("m_alibi"), 2 * j + h + 1)
                    for c in range(C):
                        a, b = (0, P) if c == 0 else (P, 3 * P)
                        n = 2 * h + c
                        dve.tensor_reduce(sm[:, 72 + n:73 + n], lg[:, h, a:b], AX.X, ALU.max, negate=True).then_inc(S("m_max"), 1)
                for h in range(2):
                    dve.wait_ge(S("m_exp"), 4 * j + 2 * h + 2)
                    dve.reciprocal(sm[:, 88 + 2 * h:90 + 2 * h], sm[:, 76 + 2 * h:78 + 2 * h]).then_inc(S("m_rec"), 1)
                    dve.wait_ge(S("m_rec"), 2 * j + h + 1)
                    for c in range(C):
                        a, b = (0, P) if c == 0 else (P, 3 * P)
                        n = 2 * h + c
                        dve.tensor_scalar(pr[:, h, a:b], pr[:, h, a:b], sm[:, 88 + n:89 + n], None, ALU.mult).then_inc(S("m_prob"), 1)
                advance(U["pt"])
                dve.wait_ge(S("pt_psum"), 2 * j + 2)
                dve.tensor_copy(kq[:, 1].rearrange("p c k t -> p (c k t)")[:, 0:3 * P], mx[0][:, 0:3 * P]).then_inc(S("pt_v"), 1)
                advance(U["o"])
                dve.wait_ge(S("otr"), p + 1)
                dve.wait_ge(S("zg"), p + 1)
                dve.scalar_tensor_tensor(yf[:, :, :], mx[1][:, :].rearrange("p (h t) -> p h t", h=2), 0.5, zg[:, :, :],
                                         ALU.mult, ALU.mult).then_inc(S("yf_done"), 1)

            conv_step = [0]
            advance(128)
            for p, (kind, j) in enumerate(PAIRS):
                {"gdn": mix_gdn, "ret": mix_ret, "moba": mix_moba}[kind](p, j, 128 * (p + 1))
                advance(128 * (p + 2))
            advance(64 * GROUPS)
            residual(6)
            residual(7)

        @block.tensor
        def _(pe):
            pos = [0]

            def unit(v):
                g, t = v // 64, v // UPT
                n, r = t, v % UPT
                if r == 0:
                    wait_lo(pe, n)
                hi = w_hi[:, n % NSPLIT, :].rearrange("p (k c) -> p k c", k=TK)
                lo = w_lo[:, n % NSPLIT, :].rearrange("p (k c) -> p k c", k=TK)
                if g < HEADS:
                    s, k = r // TK, r % TK
                    kc = (t % TPH) * TK + k
                    first, last = kc == 0, kc == KC - 1
                    if first and g == 0:
                        pe.wait_ge(S("h_tmp"), s + 1)
                    if g == 0 and s == 0:
                        pe.wait_ge(S("h_lo"), kc + 1)
                    if first and g:
                        pe.wait_ge(S("evac"), 4 * (g - 1) + s + 1)
                    cols = slice(s * P, (s + 1) * P)

                    def low(**kw):
                        return pe.matmul(pj[s][:, 0:T], lo[:, k, cols], hT[:, kc, 0, :], **kw)

                    def high(**kw):
                        return pe.matmul(pj[s][:, :], hi[:, k, cols], hT[:, kc].rearrange("p a t -> p (a t)"), **kw)

                    if last:
                        low(start=False, stop=False)
                        ins = high(start=False, stop=True)
                        ins.then_inc(S("proj_done"), 1)
                    else:
                        high(start=first, stop=False)
                        ins = low(start=False, stop=False)
                else:
                    k, c, half = r // 4, r // 2 % 2, r % 2
                    kc = (t % TPH) * TK + k
                    first, last = kc == 0, kc == KC - 1
                    bank = pj[(2 * (g - HEADS) + c) % 4]
                    if first and half == 0:
                        if g == HEADS:
                            pe.wait_ge(S("evac"), 4 * HEADS)
                        elif g >= HEADS + 2:
                            pe.wait_ge(S("out_ready"), 2 * (g - HEADS - 2) + c + 1)
                    if kc % 2 == 0 and half == 0 and c == 0 and g == HEADS:
                        block_ready(kc // 2)
                    tok = slice(c * P, (c + 1) * P)
                    if half == 0:
                        ins = pe.matmul(bank[:, :], yT[:, kc, 0, tok], hi[:, k, :], start=first, stop=False)
                    else:
                        pe.matmul(bank[:, :], yT[:, kc, 1, tok], hi[:, k, :], start=False, stop=False)
                        ins = pe.matmul(bank[:, :], yT[:, kc, 0, tok], lo[:, k, :], start=False, stop=last)
                        if last:
                            ins.then_inc(S("out_psum"), 1)
                if r == UPT - 1 and not last:
                    ins.then_inc(S("tile_used"), 1)

            def block_ready(b):
                order = {"ret": 3, "gdn": 0, "moba": 5}
                kind = "ret" if b < 2 else "gdn" if b < 5 else "moba"
                p = order[kind] + b - {"ret": 0, "gdn": 2, "moba": 5}[kind]
                pe.wait_ge(S("y_lo"), p + 1)

            def stream(u):
                for v in range(pos[0], min(u, 64 * GROUPS)):
                    unit(v)
                pos[0] = max(pos[0], u)

            pe.wait_ge(S("cst_in"), 16)
            for name in ("param_in", "norm_in", "param_in1", "param_in2", "param_in3", "param_in4"):
                pe.wait_ge(S(name), 16)
            pe.transpose(mx[3][:, 0:R_ROWS], prow[:, :], ident[0:R_ROWS, 0:R_ROWS]).then_inc(S("params_psum"), 1)
            def x_blocks(b, c):
                for k in range(2 * b, 2 * b + 2):
                    ins = pe.transpose((pj + mx)[b][:, k % 2 * T + c * P:k % 2 * T + (c + 1) * P],
                                       x_sb[:, c, k * P:(k + 1) * P], ident)
                return ins

            pe.wait_ge(S("x0_in"), 16)
            for b in range(7):
                x_blocks(b, 0)
            pe.wait_ge(S("x1_in"), 16)
            for b in range(7):
                x_blocks(b, 1).then_inc(S("hT_psum"), 1)
            pe.wait_ge(S("pcol_done"), 1)
            pe.wait_ge(S("rstd_done"), 1)
            for c in range(C):
                ins = pe.matmul(mx[3][:, c * P:(c + 1) * P], sm[:, 6 + c:7 + c].broadcast_to([P, P]), ident, start=True, stop=True)
            ins.then_inc(S("rstd_psum"), 1)
            pe.wait_ge(S("rstd_row"), 1)
            x_blocks(7, 0)
            x_blocks(7, 1).then_inc(S("hT_psum"), 1)

            stream(64)
            pe.wait_ge(S("h_tmp"), 8)
            pe.wait_ge(S("wab_lo_done"), 1)
            for c in range(C):
                tok = slice(c * P, (c + 1) * P)
                for k in range(KC):
                    for i, (a, w) in enumerate(((0, wab_hi), (1, wab_hi), (0, wab_lo))):
                        ins = pe.matmul(mx[0][:, c * AB:(c + 1) * AB], hT[:, k, a, tok], w[:, k, :],
                                        start=k == 0 and i == 0, stop=k == KC - 1 and i == 2)
            ins.then_inc(S("ab_psum"), 1)
            stream(88)
            pe.wait_ge(S("g_done"), 1)
            for c in range(C):
                pe.matmul(mx[1][:, c * GDN:(c + 1) * GDN], upper, ab[:, A_G, c, :], start=True, stop=True)
            pe.matmul(mx[1][:, C * GDN:(C + 1) * GDN], ones, ab[:, A_G, 0, :], start=True, stop=True).then_inc(S("cum_psum"), 1)

            def mix_gdn(p, j, base):
                U = {k: base + v for k, v in U_GDN.items()}
                stream(base + 1)
                pe.wait_ge(S("egc_done"), 2)
                if p:
                    pe.wait_ge(S("os"), p)
                for n in range(4):
                    h, c = n // 2, n % 2
                    ins = pe.matmul(mx[2][:, n * P:(n + 1) * P], ab[:, A_GC, c, 2 * j + h:2 * j + h + 1].broadcast_to([P, P]), ident,
                                    start=True, stop=True)
                ins.then_inc(S("gcb"), 1)
                tail(p, base)
                stream(U["gram"])
                if p:
                    pe.wait_ge(S("yf_done"), p)
                pe.wait_ge(S("silu_kq"), 4 * j + 4)
                for h in range(2):
                    for c in range(C):
                        pe.matmul(mx[h][:, c * T:(c + 1) * T], kq[:, h, c, 0, :], kq[:, h, c].rearrange("p k t -> p (k t)"),
                                  start=True, stop=True)
                    pe.transpose(mx[3][:, h * P:(h + 1) * P], kq[:, h, 0, 0, :], ident)
                pe.wait_ge(S("sq"), 2 * j + 2)
                for h in range(2):
                    for c in range(C):
                        for i in range(2):
                            at = 2 * P + 4 * h + 2 * c + i
                            ins = pe.matmul(mx[3][:, at:at + 1], sq[:, h, c, i, :], ones[:, 0:1], start=True, stop=True)
                ins.then_inc(S("gram"), 1)
                stream(U["vtok"])
                pe.wait_ge(S("silu_v"), j + 1)
                pe.wait_ge(S("clip_done"), 4 * j + 4)
                for n in range(4):
                    ins = pe.transpose(mx[2][:, n * P:(n + 1) * P], vT[:, n // 2, (n % 2) * P:(n % 2 + 1) * P], ident)
                ins.then_inc(S("vtok"), 1)
                for l in range(LEVELS):
                    stream(U[f"x{l}"])
                    if l == 0:
                        pe.wait_ge(S("mt_at"), 4 * j + 4)
                        pe.wait_ge(S("gt"), (LEVELS + 1) * j + 1)
                    else:
                        pe.wait_ge(S("gm"), (LEVELS - 1) * j + l)
                    g_in = gt if l == 0 else gm
                    for n in range(4):
                        ins = pe.matmul(mx[0][:, n * P:(n + 1) * P], mT[:, n, :], g_in[:, n, :], start=True, stop=True)
                    ins.then_inc(S("x_psum"), 1)
                    stream(U[f"y{l}"])
                    pe.wait_ge(S("xs"), LEVELS * j + l + 1)
                    for n in range(4):
                        ins = pe.matmul(mx[1][:, n * P:(n + 1) * P], xs[:, n, :], gt[:, n, :], start=True, stop=True)
                    ins.then_inc(S("y_psum"), 1)
                    if l < LEVELS - 1:
                        stream(U[f"t{l}"])
                        pe.wait_ge(S("gt"), (LEVELS + 1) * j + l + 2)
                        if l == 0:
                            pe.wait_ge(S("vr"), 4 * j + 4)
                        for n in range(4):
                            ins = pe.transpose(mx[2][:, n * P:(n + 1) * P], gt[:, n, :], ident)
                        ins.then_inc(S("gtr"), 1)
                stream(U["v0"])
                pe.wait_ge(S("gt"), (LEVELS + 1) * (j + 1))
                pe.wait_ge(S("ktok"), j + 1)
                for h in range(2):
                    ins = pe.matmul(mx[3][:, h * P:(h + 1) * P], gt[:, 2 * h, :], vr[:, 2 * h, :], start=True, stop=True)
                ins.then_inc(S("v0_psum"), 1)
                stream(U["s1"])
                pe.wait_ge(S("v0s"), 2 * j + 2)
                for h in range(2):
                    ins = pe.matmul(mx[1][:, h * P:(h + 1) * P], ktok[:, h, :], v0s[:, h, :], start=True, stop=True)
                ins.then_inc(S("s1_psum"), 1)
                stream(U["ks"])
                pe.wait_ge(S("st"), j + 1)
                for h in range(2):
                    pe.matmul(mx[0][:, h * P:(h + 1) * P], kq[:, h, 1, 0, :], st[:, h, :], start=True, stop=True)
                    ins = pe.matmul(mx[0][:, (2 + h) * P:(3 + h) * P], kq[:, h, 1, 1, :], st[:, h, :], start=True, stop=True)
                ins.then_inc(S("ks_psum"), 1)
                stream(U["v1"])
                pe.wait_ge(S("vr1"), 2 * j + 2)
                for h in range(2):
                    ins = pe.matmul(mx[1][:, (2 + h) * P:(3 + h) * P], gt[:, 2 * h + 1, :], vr[:, 2 * h + 1, :], start=True, stop=True)
                ins.then_inc(S("v1_psum"), 1)
                stream(U["o"])
                pe.wait_ge(S("v0"), j + 1)
                pe.wait_ge(S("v1"), j + 1)
                for h in range(2):
                    for c, v in enumerate((v0, v1)):
                        ins = pe.matmul(mx[2][:, (2 * h + c) * P:(2 * h + c + 1) * P], aT[:, 2 * h + c, :], v[:, h, :], start=True, stop=True)
                ins.then_inc(S("o_psum"), 1)

            def tail(p, base):
                if p and PAIRS[p - 1][0] == "gdn":
                    stream(base + U_TAIL)
                    out_transposes(p - 1, mx[3])

            def out_transposes(p, bank):
                pe.wait_ge(S("on"), p + 1)
                for n in range(4):
                    ins = pe.transpose(bank[:, n * P:(n + 1) * P], on[:, n // 2, n % 2, :], ident)
                ins.then_inc(S("otr"), 1)

            def mix_ret(p, j, base):
                U = {k: base + v for k, v in U_RET.items()}
                tail(p, base)
                stream(U["gram"])
                pe.wait_ge(S("evac"), 8 * p + 8)
                pe.wait_ge(S("yf_done"), p)
                for h in range(2):
                    for c in range(C):
                        n = 2 * h + c
                        ins = pe.matmul(mx[0][:, n * P:(n + 1) * P], chunk_in(h, 1, c), chunk_in(h, 0, c), start=True, stop=True)
                ins.then_inc(S("r_gram"), 1)
                for h in range(2):
                    for c in range(C):
                        n = 2 * h + c
                        pe.transpose(mx[1][:, n * P:(n + 1) * P], chunk_in(h, 2, c), ident)
                    ins = pe.transpose(mx[2][:, h * P:(h + 1) * P], chunk_in(h, 1, 0), ident)
                ins.then_inc(S("r_vtok"), 1)
                stream(U["s1"])
                pe.wait_ge(S("r_vr"), j + 1)
                pe.wait_ge(S("r_ktok"), 2 * j + 2)
                for h in range(2):
                    ins = pe.matmul(mx[3][:, h * P:(h + 1) * P], ktok[:, h, :], vr[:, 2 * h, :], start=True, stop=True)
                ins.then_inc(S("r_s1_psum"), 1)
                stream(U["qs"])
                pe.wait_ge(S("r_st"), j + 1)
                for h in range(2):
                    pe.matmul(mx[3][:, (2 + h) * P:(3 + h) * P], chunk_in(h, 0, 1), st[:, h, :], start=True, stop=True)
                pe.wait_ge(S("r_at"), 2 * j + 2)
                for n in range(4):
                    ins = pe.matmul(mx[2][:, n * P:(n + 1) * P], aT[:, n, :], vr[:, n, :], start=True, stop=True)
                ins.then_inc(S("o_psum"), 1)
                stream(U["tr"])
                out_transposes(p, mx[0])

            def mix_moba(p, j, base):
                U = {k: base + v for k, v in U_MOBA.items()}
                pr = th[:, 6 * P:12 * P].rearrange("p (h c) -> p h c", h=2)
                pt = [kq[:, h].rearrange("p c k t -> p (c k t)") for h in range(2)]
                stream(U["nrm"])
                pe.wait_ge(S("evac"), 8 * p + 8)
                pe.wait_ge(S("yf_done"), p)
                pe.wait_ge(S("m_sq"), 2 * j + 2)
                sqv = sq[:, :, :, :, :].rearrange("p h c k t -> p (h c k) t")
                for n in range(8):
                    ins = pe.matmul(mx[3][:, n:n + 1], sqv[:, n, :], ones[:, 0:1], start=True, stop=True)
                ins.then_inc(S("m_nrm"), 1)
                for n in range(4):
                    ins = pe.transpose(mx[1][:, n * P:(n + 1) * P], chunk_in(n // 2, 2, n % 2), ident)
                ins.then_inc(S("m_vtok"), 1)
                stream(U["bc"])
                pe.wait_ge(S("m_pow"), j + 1)
                for n in range(4):
                    at = 64 + 4 * (n // 2) + 2 + n % 2
                    ins = pe.matmul(mx[2][:, n * P:(n + 1) * P], sm[:, at:at + 1].broadcast_to([P, P]), ident, start=True, stop=True)
                ins.then_inc(S("m_bc"), 1)
                stream(U["score"])
                pe.wait_ge(S("knT"), 2 * j + 2)
                for h in range(2):
                    bank = mx[(0, 3)[h]]
                    pe.matmul(bank[:, 0:P], chunk_in(h, 0, 0), vT[:, h, 0:P], start=True, stop=True)
                    ins = pe.matmul(bank[:, P:3 * P], chunk_in(h, 0, 1), vT[:, h, :], start=True, stop=True)
                ins.then_inc(S("score"), 1)
                stream(U["pt"])
                for h in range(2):
                    pe.wait_ge(S("m_prob"), 4 * j + 2 * h + 2)
                    for i in range(3):
                        ins = pe.transpose(mx[(2, 0)[h]][:, i * P:(i + 1) * P], pr[:, h, i * P:(i + 1) * P], ident)
                    ins.then_inc(S("pt_psum"), 1)
                stream(U["o"])
                pe.wait_ge(S("m_vr"), j + 1)
                pe.wait_ge(S("pt_a"), j + 1)
                pe.wait_ge(S("pt_v"), j + 1)
                for h in range(2):
                    pe.matmul(mx[1][:, h * T:(h + 1) * T], vr[:, 2 * h, :], pt[h][:, 0:T], start=True, stop=False)
                    ins = pe.matmul(mx[1][:, h * T + P:(h + 1) * T], vr[:, 2 * h + 1, :], pt[h][:, T:T + P], start=False, stop=True)
                ins.then_inc(S("otr"), 1)

            stream(128)
            for p, (kind, j) in enumerate(PAIRS):
                {"gdn": mix_gdn, "ret": mix_ret, "moba": mix_moba}[kind](p, j, 128 * (p + 1))
                stream(128 * (p + 2))
            stream(64 * GROUPS)


_INS = ['x', 'norm_w', 'w_in', 'conv_w', 'a_log', 'dt_bias', 'ret_norm_w', 'gdn_norm_w', 'q_norm_w', 'k_norm_w',
        'w_out']


def kernel(**inputs):
    import numpy as _np
    import concourse.bacc as _bacc
    from concourse import mybir as _mybir
    from concourse.bass_utils import run_bass_kernel_spmd as _run

    nc = _bacc.Bacc("TRN2", target_bir_lowering=False, num_devices=1)
    arrays, args = {}, []
    for name in _INS:
        a = _np.ascontiguousarray(inputs[name])
        arrays[f"in_{name}_dram"] = a
        args.append(nc.dram_tensor(f"in_{name}_dram", a.shape, _mybir.dt.from_np(a.dtype), kind="ExternalInput").ap())
    arrays["table_dram"] = constants()
    args.append(nc.dram_tensor("table_dram", (P, K_COLS), F32, kind="ExternalInput").ap())
    args.append(nc.dram_tensor("out_0_dram", (1, T, D), F32, kind="ExternalOutput").ap())
    layer(nc, *args)
    r = _run(nc, [arrays], core_ids=[0])
    return r.results[0]["out_0_dram"]
```

```python
from contextlib import ExitStack

import numpy as np

import concourse.bass as bass
from concourse import mybir

F32 = mybir.dt.float32
F32R = mybir.dt.float32r
ALU = mybir.AluOpType
ACT = mybir.ActivationFunctionType
AX = mybir.AxisListType

P = 128
D = 2048
T = 256
C = T // P
KC = D // P
RET, GDN, MOBA = 4, 6, 6
RET_COL = 0
GDN_COL = 4 * RET * P
AB_COL = GDN_COL + 4 * GDN * P
MOBA_COL = AB_COL + 2 * GDN
AB = 2 * GDN
EPS = 1e-6
SCALE = float(P) ** -0.5
CONV = 4
PAD = CONV - 1

TK = 2
TPH = KC // TK
UPT = 4 * TK
HEADS = RET + GDN + MOBA
GROUPS = HEADS + D // 512
NRAW, NSPLIT, LEAD = 8, 4, 3
TILES = GROUPS * TPH

PAIRS = [("gdn", 0), ("gdn", 1), ("gdn", 2), ("ret", 0), ("ret", 1), ("moba", 0), ("moba", 1), ("moba", 2)]
Y_BLOCK = {"ret": 0, "gdn": RET, "moba": RET + GDN}
VEC_LO = (1, 3, 5, 7)

LOW_AT = 4

LEVELS = 7
HALF = P // 2

K_ID, K_UP, K_ONE = 0, P, 2 * P
K_POW = 3 * P
K_FIRST = K_POW + 8
K_LEVEL = K_FIRST
K_DECAY = K_LEVEL + (LEVELS - 1) * P
K_DIST = K_DECAY + RET * P
K_FIRST_T = K_DIST + 3 * P
K_STACK = K_FIRST_T + HALF
K_KDEC = K_STACK + HALF
K_QDEC = K_KDEC + RET
K_COLS = K_QDEC + RET

R_NORM = 0
R_CONV = R_NORM + KC
R_RET = R_CONV + CONV * 3 * GDN
R_GDN = R_RET + RET
R_Q = R_GDN + 1
R_K = R_Q + 1
R_ROWS = R_K + 1

U_GDN = {"gram": 15, "vtok": 22, "t5": 73}
for _l in range(1, LEVELS):
    U_GDN[f"x{_l}"] = 22 + 9 * _l
    U_GDN[f"y{_l}"] = 25 + 9 * _l
U_GDN.update(x6=77, y6=80, v0=84, s1=89, ks=93, v1=98, o=103)
U_FIRST = 90
U_TAIL = 12
U_RET = {"gram": 18, "s1": 24, "qs": 30, "o": 30, "tr": 46}
U_MOBA = {"nrm": 8, "bc": 16, "score": 22, "pt": 40, "o": 48}


def constants():
    t = np.zeros((P, K_COLS), np.float64)
    p, c = np.arange(P)[:, None], np.arange(P)[None, :]
    t[:, K_ID:K_ID + P] = p == c
    t[:, K_UP:K_UP + P] = p <= c
    t[:, K_ONE:K_ONE + P] = 1
    for l in range(1, LEVELS):
        b = 2 ** l
        t[:, K_LEVEL + (l - 1) * P:K_LEVEL + l * P] = ((p // b) % 2 == 1) & (c // b == p // b - 1)
    for h in range(RET):
        lg = np.log1p(-2.0 ** (-5.0 - h))
        t[:, K_DECAY + h * P:K_DECAY + (h + 1) * P] = np.where(c >= p, np.exp(np.maximum(c - p, 0) * lg), 0) * SCALE
        t[:, K_KDEC + h] = np.exp((P - 1 - np.arange(P)) * lg) * SCALE
        t[:, K_QDEC + h] = np.exp((np.arange(P) + 1) * lg)
    c2 = np.arange(HALF)[None, :]
    t[:, K_FIRST_T:K_FIRST_T + HALF] = np.where((c2 % 2 == 1) & (p % HALF == c2 - 1), -1, 0)
    t[:, K_STACK:K_STACK + HALF] = p % HALF == c2
    s = np.arange(2 * P)[None, :]
    t[:, K_DIST:K_DIST + P] = np.where(c <= p, c - p, -1e30)
    t[:, K_DIST + P:K_DIST + 3 * P] = np.where(s <= p + P, s - p - P, -1e30)
    t[:, K_POW:K_POW + 8] = -0.5
    return t.astype(np.float32)


def layer(nc, x, norm_w, w_in, conv_w, a_log, dt_bias, ret_norm_w, gdn_norm_w, q_norm_w, k_norm_w, w_out,
          table, out):
    ctx = ExitStack()
    with ctx:
        def sb(name, shape, dt=F32):
            return ctx.enter_context(nc.sbuf_tensor(name, shape, dt))

        sems = {}

        def S(name):
            if name not in sems:
                sems[name] = ctx.enter_context(nc.semaphore(name))
            return sems[name]

        w_raw = sb("w_raw", [P, NRAW, TK * 512])
        w_hi = sb("w_hi", [P, NSPLIT, TK * 512], F32R)
        w_lo = sb("w_lo", [P, NSPLIT, TK * 512], F32R)
        hT = sb("hT", [P, KC, 2, T], F32R)
        yT = sb("yT", [P, KC, 2, T], F32R)
        cst = sb("cst", [P, K_COLS])
        prow = sb("prow", [R_ROWS, P])
        pcol = sb("pcol", [P, R_ROWS])
        raw = sb("raw", [P, 2, 4, PAD + T])
        ev_lo = sb("ev_lo", [P, 4, T])
        cv = sb("cv", [P, 2 * 3 * T])
        th = sb("th", [P, 2 * 3 * T])
        kq = sb("kq", [P, 2, C, 2, P])
        sq = sb("sq", [P, 2, C, 2, P])
        vT = sb("vT", [P, 2, T])
        zg = sb("zg", [P, 2, T])
        dd = sb("dd", [P, 4, P])
        ee = sb("ee", [P, 4, P])
        er = sb("er", [P, 4, P])
        mT = sb("mT", [P, 4, P])
        aT = sb("aT", [P, 4, P])
        vr = sb("vr", [P, 4, P])
        ktok = sb("ktok", [P, 2, P])
        mB = sb("mB", [P, 4, P])
        gm = sb("gm", [P, 4, HALF])
        gs = sb("gs", [P, 4, HALF])
        gt = sb("gt", [P, 4, P])
        xs = sb("xs", [P, 4, P])
        v0 = sb("v0", [P, 2, P])
        v0s = sb("v0s", [P, 2, P])
        v1 = sb("v1", [P, 2, P])
        st = sb("st", [P, 2, P])
        os_ = sb("os", [P, 2, C, P])
        on = sb("on", [P, 2, C, P])
        yf = sb("yf", [P, 2, T])
        ab = sb("ab", [P, 16, C, GDN])
        wab_hi = sb("wab_hi", [P, KC, AB], F32R)
        wab_lo = sb("wab_lo", [P, KC, AB], F32R)
        bias = sb("bias", [P, 2, GDN])
        sm = sb("sm", [P, 128])

        pj = [ctx.enter_context(nc.psum_tensor(f"pj{s}", [P, 512], F32)) for s in range(4)]
        mx = [ctx.enter_context(nc.psum_tensor(f"mx{s}", [P, 512], F32)) for s in range(4)]

        ident = cst[:, K_ID:K_ID + P]
        upper = cst[:, K_UP:K_UP + P]
        ones = cst[:, K_ONE:K_ONE + P]
        x_sb = w_raw[:, NRAW // 2:, :].rearrange("p a n -> p (a n)").rearrange("p (c n) -> p c n", c=C)

        wab = dd[:, :, :].rearrange("p n c -> p (n c)")[:, 0:KC * AB].rearrange("p (k c) -> p k c", k=KC)
        abT = vT[:, :, :].rearrange("p a t -> p (a t)")[0:AB]
        junk_a, junk_v = kq[:, :].rearrange("p h c k t -> p (h c k t)"), sq[:, :].rearrange("p h c k t -> p (h c k t)")
        rstd_row = yf[:, 0, :]

        def h_tmp(k, n=1):
            buf = (cv, th)[k // 2 % 6 // 3]
            at = k // 2 % 3 * 512 + k % 2 * T
            return buf[:, at:at + n * T]

        def four(ap):
            return ap.rearrange("p (n c) -> p n c", c=P)

        def stacked(bank):
            return bank[:, 0:4 * HALF].rearrange("p (n c) -> p n c", n=4)

        A_G, A_BETA, A_GC, A_NGC, A_EGC, A_NEGC, A_GL, A_Z, A_E, A_U, A_L, A_T1, A_T2, A_T3, A_ELAST, A_TB = range(16)

        def chunk_in(h, s, c):
            return raw[:, h, s, PAD + c * P:PAD + (c + 1) * P]

        def lo_count(n, vec):
            v = n // TPH * len(VEC_LO) + sum(q < n % TPH for q in VEC_LO)
            return v if vec else n - v

        def wait_lo(eng, n):
            if n % TPH in VEC_LO:
                eng.wait_ge(S("lo_vec"), lo_count(n + 1, True))
            else:
                eng.wait_ge(S("lo_pool"), lo_count(n + 1, False))

        def wait_used(eng, n):
            g, q = n // TPH, n % TPH
            if q < TPH - 1:
                eng.wait_ge(S("tile_used"), (TPH - 1) * g + q + 1)
            elif g < HEADS:
                eng.wait_ge(S("proj_done"), 4 * (g + 1))
            else:
                eng.wait_ge(S("out_psum"), 2 * (g + 1 - HEADS))

        def evacuated(v):
            head, rest = divmod(v + 6, 64)
            return (head - 1, rest // 2) if 0 < head <= HEADS and rest < 8 and rest % 2 == 0 else None

        def low_part(eng, n, name):
            eng.wait_ge(S("hi_done"), n + 1)
            eng.tensor_tensor(w_lo[:, n % NSPLIT, :], w_raw[:, n % NRAW, :],
                              w_hi[:, n % NSPLIT, :].bitcast(F32), ALU.subtract).then_inc(S(name), 1)

        block = ctx.enter_context(nc.Block())

        @block.sync
        def _(sp):
            sp.dma_start(x_sb[:, 0, :], x[0, 0:P, :]).then_inc(S("x0_in"), 16)
            sp.dma_start(cst[:, 0:K_FIRST], table[:, 0:K_FIRST]).then_inc(S("cst_in"), 16)
            sp.dma_start(x_sb[:, 1, :], x[0, P:T, :]).then_inc(S("x1_in"), 16)

            def load(n):
                group, q = n // TPH, n % TPH
                rows = slice(q * TK * P, (q + 1) * TK * P)
                if n >= NRAW:
                    wait_lo(sp, n - NRAW)
                elif n >= NRAW // 2:
                    sp.wait_ge(S("hT_psum"), 8)
                dst = w_raw[:, n % NRAW, :].rearrange("p (k n) -> p k n", k=TK)
                if group < HEADS:
                    kind, j = PAIRS[group // 2]
                    heads = {"gdn": GDN, "ret": RET, "moba": MOBA}[kind]
                    col = {"gdn": GDN_COL, "ret": RET_COL, "moba": MOBA_COL}[kind]
                    h = 2 * j + group % 2
                    src = w_in[0, rows, col:col + 4 * heads * P].rearrange(
                        "(k p) (s c) -> p k s c", p=P, s=4)[:, :, :, h * P:(h + 1) * P]
                    dst = dst.rearrange("p k (s c) -> p k s c", s=4)
                    for k in range(TK):
                        sp.dma_start(dst[:, k], src[:, k]).then_inc(S(f"w_in{n % NRAW}"), 16)
                else:
                    g = group - HEADS
                    src = w_out[0, rows, g * 512:(g + 1) * 512].rearrange("(k p) c -> p k c", p=P)
                    for k in range(TK):
                        sp.dma_start(dst[:, k], src[:, k]).then_inc(S(f"w_in{n % NRAW}"), 16)

            def load_x(n):
                g, c = n // 2, n % 2
                if n >= 3:
                    sp.wait_ge(S("out_ready"), n - 2)
                sp.dma_start(cv[:, (n % 3) * 512:(n % 3 + 1) * 512],
                             x[0, c * P:(c + 1) * P, g * 512:(g + 1) * 512]).then_inc(S(f"xr_in{n % 3}"), 16)

            for n in range(TILES):
                load(n)
                group = n // TPH - 1 - HEADS
                if group >= 0 and n % TPH == 3:
                    load_x(2 * group)
                    load_x(2 * group + 1)
                if n == NRAW // 2 - 1:
                    sp.dma_start(wab[:, :, :], w_in[0, :, AB_COL:AB_COL + AB].rearrange("(k p) c -> p k c", p=P)).then_inc(S("wab_in"), 16)
                    sp.dma_start(prow[R_CONV:R_RET, :], conv_w[0].rearrange("j (t c) -> (j t) c", c=P)).then_inc(S("param_in"), 16)
                    sp.dma_start(prow[R_RET:R_GDN, :], ret_norm_w[0]).then_inc(S("param_in"), 16)
                    sp.dma_start(prow[R_GDN:R_Q, :], gdn_norm_w).then_inc(S("param_in"), 16)
                    sp.dma_start(prow[R_Q:R_K, :], q_norm_w).then_inc(S("param_in"), 16)
                    sp.dma_start(prow[R_K:R_ROWS, :], k_norm_w).then_inc(S("param_in"), 16)
                if n == NRAW - 1:
                    sp.dma_start(bias[:, 0, :], a_log[0:1, :].broadcast_to([P, GDN])).then_inc(S("bias_in"), 16)
                    sp.dma_start(bias[:, 1, :], dt_bias[0:1, :].broadcast_to([P, GDN])).then_inc(S("bias_in"), 16)
                    sp.dma_start(cst[:, K_FIRST:], table[:, K_FIRST:]).then_inc(S("cst_in2"), 16)
            load_x(6)
            load_x(7)

        @block.scalar
        def _(act):
            act.dma_start(prow[R_NORM:R_CONV, :], norm_w[0].rearrange("(k p) -> k p", p=P)).then_inc(S("norm_in"), 16)

            def high_part(n):
                act.wait_ge(S(f"w_in{n % NRAW}"), 16 * TK * (n // NRAW + 1))
                if n >= NSPLIT:
                    wait_used(act, n - NSPLIT)
                act.activation(w_hi[:, n % NSPLIT, :], w_raw[:, n % NRAW, :], ACT.Copy).then_inc(S("hi_done"), 1)

            def evacuate_low(g, s):
                act.wait_ge(S("proj_done"), 4 * g + s + 1)
                act.activation(ev_lo[:, s, :], pj[s][:, T:2 * T], ACT.Copy).then_inc(S("ev_lo_done"), 1)

            def send(n):
                g, c = n // 2, n % 2
                act.wait_ge(S("out_ready"), n + 1)
                act.dma_start(out[0, c * P:(c + 1) * P, g * 512:(g + 1) * 512],
                              sq[:, n % 2].rearrange("p c k t -> p (c k t)")).then_inc(S(f"out_sent{n % 2}"), 16)

            pos = [0]

            def advance(u):
                for v in range(pos[0], min(u, 64 * GROUPS)):
                    if evacuated(v):
                        evacuate_low(*evacuated(v))
                    if v % UPT == 0 and v // UPT + LEAD < TILES:
                        high_part(v // UPT + LEAD)
                    if v > 64 * HEADS and v % 64 == 0:
                        send(2 * (v // 64 - HEADS) - 2)
                        send(2 * (v // 64 - HEADS) - 1)
                pos[0] = max(pos[0], u)

            act.wait_ge(S("x0_in"), 16)
            act.activation(junk_a,
                           x_sb[:, 0, 0:1024], ACT.Square, accum_out=sm[:, 0:1]).then_inc(S("ss_act"), 1)
            act.wait_ge(S("x1_in"), 16)
            act.wait_ge(S("ss_act"), 1)
            act.activation(junk_a, x_sb[:, 1, 0:1024], ACT.Square, accum_out=sm[:, 2:3]).then_inc(S("ss_act"), 1)
            high_part(0)
            for k in range(KC):
                act.wait_ge(S("h_tmp"), k // 2 + 1)
                act.activation(hT[:, k, 0, :], h_tmp(k), ACT.Copy,
                               scale=pcol[:, R_NORM + k:R_NORM + k + 1]).then_inc(S("h_hi"), 1)
                if k == 1 or k == 3:
                    high_part(k // 2 + 1)
                if k % 2 and k >= 5:
                    advance(UPT * (k // 2 - 1))
            act.wait_ge(S("wab_in"), 16)
            act.activation(wab_hi[:, :, :], wab[:, :, :], ACT.Copy).then_inc(S("wab_hi_done"), 1)
            advance(64)

            act.wait_ge(S("bias_in"), 2 * 16)
            act.activation(sm[:, 16:16 + GDN], bias[:, 0, :], ACT.Exp).then_inc(S("expa_done"), 1)
            advance(65)
            act.wait_ge(S("abt_psum"), 1)
            act.activation(abT, mx[0][0:AB, :], ACT.Copy).then_inc(S("abt_done"), 1)
            act.wait_ge(S("ab_psum"), 1)
            act.activation(ab[:, A_TB], mx[1][:, 0:2 * AB].rearrange("p (c h) -> p c h", c=C)[:, :, GDN:], ACT.Tanh,
                           scale=0.5).then_inc(S("tanh_b"), 1)
            act.wait_ge(S("negabs_z"), 1)
            act.activation(ab[:, A_E], ab[:, A_T1], ACT.Exp).then_inc(S("exp_z"), 1)
            act.wait_ge(S("one_plus"), 1)
            act.activation(ab[:, A_L], ab[:, A_U], ACT.Ln).then_inc(S("ln_u"), 1)
            advance(90)
            act.wait_ge(S("gc_done"), 1)
            act.activation(ab[:, A_EGC], ab[:, A_GC], ACT.Exp).then_inc(S("egc_done"), 1)
            act.activation(ab[:, A_ELAST, 0, :], ab[:, A_T2, 0, :], ACT.Exp).then_inc(S("egc_done"), 1)

            def gate_tanh(p):
                act.wait_ge(S("evac"), 8 * (p + 1))
                if p:
                    act.wait_ge(S("yf_done"), p)
                act.activation(zg[:, :, :], raw[:, :, 3, PAD:], ACT.Tanh, scale=0.5).then_inc(S("tanh_z"), 1)

            def split_y(p, y0):
                act.wait_ge(S("yf_done"), p + 1)
                act.activation(yT[:, y0:y0 + 2, 0, :], yf[:, :, :], ACT.Copy).then_inc(S("y_hi"), 1)

            def tail(p):
                if p and PAIRS[p - 1][0] == "gdn":
                    split_y(p - 1, Y_BLOCK["gdn"] + 2 * PAIRS[p - 1][1])

            def decay_exp(j):
                act.wait_ge(S("clip_done"), 4 * (j + 1))
                act.activation(ee[:, :, :], dd[:, :, :], ACT.Exp).then_inc(S("exp_decay"), 1)

            def tanh_first(j):
                act.wait_ge(S("conv_v"), 2 * j + 1)
                th3, cv3 = (b[:, :].rearrange("p (h s t) -> p h s t", h=2, s=3) for b in (th, cv))
                act.activation(th3[:, 0], cv3[:, 0], ACT.Tanh, scale=0.5).then_inc(S("tanh_kq"), 1)

            def mix_gdn(p, j, base):
                U = {k: base + v for k, v in U_GDN.items()}
                advance(base + 1)
                th3, cv3 = (b[:, :].rearrange("p (h s t) -> p h s t", h=2, s=3) for b in (th, cv))
                act.wait_ge(S("silu_kq"), 4 * j + 2)
                act.activation(sq[:, 0], kq[:, 0], ACT.Square).then_inc(S("sq"), 1)
                act.wait_ge(S("conv_kq"), 2 * j + 2)
                act.activation(th3[:, 1, 0:2], cv3[:, 1, 0:2], ACT.Tanh, scale=0.5).then_inc(S("tanh_kq"), 1)
                act.wait_ge(S("silu_kq"), 4 * j + 4)
                act.activation(sq[:, 1], kq[:, 1], ACT.Square).then_inc(S("sq"), 1)
                advance(base + 9)
                act.wait_ge(S("conv_v"), 2 * j + 2)
                act.activation(th3[:, 1, 2], cv3[:, 1, 2], ACT.Tanh, scale=0.5).then_inc(S("tanh_v"), 1)
                advance(U["gram"])
                act.wait_ge(S("g_norm"), j + 1)
                act.activation(ktok[:, :, :], mx[3][:, 0:2 * P].rearrange("p (h c) -> p h c", h=2), ACT.Copy).then_inc(S("ktok"), 1)
                tail(p)
                gate_tanh(p)
                advance(U["vtok"])
                act.wait_ge(S("vtok"), j + 1)
                act.wait_ge(S("g_scalars"), j + 1)
                for n in range(4):
                    act.activation(vr[:, n, :], mx[2][:, n * P:(n + 1) * P], ACT.Copy,
                                   scale=sm[:, 40 + n:41 + n]).then_inc(S("vr"), 1)
                def widen(dst, src, wide, name):
                    for a in (0, HALF):
                        part = src[a:a + HALF, :, a:a + HALF] if wide else src[a:a + HALF, :, :]
                        act.activation(dst[a:a + HALF, :, a:a + HALF], part, ACT.Copy).then_inc(S(name), 1)

                if j == 0:
                    act.wait_ge(S("wide_zero"), 2)
                act.wait_ge(S("mt"), 4 * j + 4)
                widen(mB, mT, True, "mb")
                if j + 1 < GDN // 2:
                    advance(U["y2"])
                    decay_exp(j + 1)
                advance(U["y5"])
                act.wait_ge(S("gs"), 6 * (j + 1))
                advance(U["t5"])
                act.wait_ge(S("gtr"), j + 1)
                act.activation(gm[0:HALF, :, :], stacked(mx[2])[0:HALF], ACT.Copy).then_inc(S("gm_last"), 1)
                widen(gt, gs, False, "gt_wide")
                advance(U["v0"])
                act.wait_ge(S("v0s"), 2 * j + 2)
                for h in range(2):
                    act.activation(v0[:, h, :], mx[3][:, h * P:(h + 1) * P], ACT.Copy,
                                   scale=sm[:, 44 + 2 * h:45 + 2 * h]).then_inc(S("v0"), 1)
                advance(U["s1"])
                act.wait_ge(S("s1_psum"), j + 1)
                act.activation(st[:, :, :], mx[1][:, 0:2 * P].rearrange("p (h c) -> p h c", h=2), ACT.Copy).then_inc(S("st"), 1)
                advance(U["v1"])
                act.wait_ge(S("v1_psum"), j + 1)
                for h in range(2):
                    act.activation(v1[:, h, :], mx[1][:, (2 + h) * P:(3 + h) * P], ACT.Copy,
                                   scale=sm[:, 45 + 2 * h:46 + 2 * h]).then_inc(S("v1"), 1)
                advance(U["o"])
                act.wait_ge(S("o_psum"), p + 1)
                act.activation(os_[:, :, :, :], mx[2][:, :].rearrange("p (h c e) -> p h c e", h=2, c=C), ACT.Copy).then_inc(S("os"), 1)
                if j + 1 < GDN // 2:
                    tanh_first(j + 1)
                squares(p)

            def squares(p):
                act.wait_ge(S("os_full"), p + 1)
                for n in range(4):
                    act.wait_ge(S("os_sq"), 4 * p + n) if 4 * p + n else None
                    act.activation(xs[:, 0, :], os_[:, n // 2, n % 2, :], ACT.Square,
                                   accum_out=sm[:, 48 + n:49 + n]).then_inc(S("os_sq"), 1)

            def mix_ret(p, j, base):
                U = {k: base + v for k, v in U_RET.items()}
                advance(base + 1)
                tail(p)
                gate_tanh(p)
                advance(U["gram"])
                act.wait_ge(S("r_vtok"), j + 1)
                act.activation(vr[:, :, :], four(mx[1][:, :]), ACT.Copy).then_inc(S("r_vr"), 1)
                for h in range(2):
                    act.activation(ktok[:, h, :], mx[2][:, h * P:(h + 1) * P], ACT.Copy,
                                   scale=cst[:, K_KDEC + 2 * j + h:K_KDEC + 2 * j + h + 1]).then_inc(S("r_ktok"), 1)
                advance(U["s1"])
                act.wait_ge(S("r_s1_psum"), j + 1)
                act.activation(st[:, :, :], mx[3][:, 0:2 * P].rearrange("p (h c) -> p h c", h=2), ACT.Copy).then_inc(S("r_st"), 1)
                advance(U["o"])
                act.wait_ge(S("o_psum"), p + 1)
                act.activation(os_[:, :, :, :], mx[2][:, :].rearrange("p (h c e) -> p h c e", h=2, c=C), ACT.Copy).then_inc(S("os"), 1)
                squares(p)
                advance(U["tr"])
                split_y(p, Y_BLOCK["ret"] + 2 * j)

            def mix_moba(p, j, base):
                U = {k: base + v for k, v in U_MOBA.items()}
                lg = th[:, 0:6 * P].rearrange("p (h c) -> p h c", h=2)
                pr = th[:, 6 * P:12 * P].rearrange("p (h c) -> p h c", h=2)
                advance(base + 1)
                for h in range(2):
                    act.wait_ge(S("evac"), 8 * p + 4 * h + 2)
                    act.activation(sq[:, h].rearrange("p c k t -> p (c k t)").rearrange("p (s t) -> p s t", s=2),
                                   raw[:, h, 0:2, PAD:], ACT.Square).then_inc(S("m_sq"), 1)
                gate_tanh(p)
                advance(U["nrm"])
                act.wait_ge(S("m_vtok"), j + 1)
                act.activation(vr[:, :, :], four(mx[1][:, :]), ACT.Copy).then_inc(S("m_vr"), 1)
                advance(U["score"])
                act.wait_ge(S("score"), j + 1)
                for h in range(2):
                    for c in range(C):
                        a, b = (0, P) if c == 0 else (P, 3 * P)
                        act.activation(lg[:, h, a:b], mx[(0, 3)[h]][:, a:b], ACT.Copy,
                                       scale=sm[:, 64 + 4 * h + c:65 + 4 * h + c]).then_inc(S("m_lg"), 1)
                for n in range(4):
                    h, c = n // 2, n % 2
                    a, b = (0, P) if c == 0 else (P, 3 * P)
                    act.wait_ge(S("m_max"), 4 * j + n + 1)
                    act.activation(pr[:, h, a:b], lg[:, h, a:b], ACT.Exp, bias=sm[:, 72 + n:73 + n],
                                   accum_out=sm[:, 76 + n:77 + n]).then_inc(S("m_exp"), 1)
                advance(U["pt"])
                act.wait_ge(S("pt_psum"), 2 * j + 1)
                act.activation(kq[:, 0].rearrange("p c k t -> p (c k t)")[:, 0:3 * P], mx[2][:, 0:3 * P], ACT.Copy).then_inc(S("pt_a"), 1)
                advance(U["o"])
                split_y(p, Y_BLOCK["moba"] + 2 * j)

            advance(U_FIRST)
            decay_exp(0)
            tanh_first(0)
            advance(128)
            for p, (kind, j) in enumerate(PAIRS):
                {"gdn": mix_gdn, "ret": mix_ret, "moba": mix_moba}[kind](p, j, 128 * (p + 1))
                advance(128 * (p + 2))
            advance(64 * GROUPS)

            send(6)
            send(7)
            act.wait_ge(S("out_sent0"), 64)
            act.wait_ge(S("out_sent1"), 64)

        @block.gpsimd
        def _(pool):
            pos = [0]

            def advance(u):
                for v in range(pos[0], min(u, 64 * GROUPS)):
                    n = v // UPT + LEAD
                    if v % UPT == 0 and n < TILES and n % TPH not in VEC_LO:
                        low_part(pool, n, "lo_pool")
                pos[0] = max(pos[0], u)

            def power(dst, src, n):
                return pool.tensor_tensor(sm[:, dst:dst + n], sm[:, src:src + n], cst[:, K_POW:K_POW + n], ALU.pow)

            pool.memset(raw[:, :, :, 0:PAD], 0.0).then_inc(S("pad_zero"), 1)
            pool.memset(mB[:, :, :], 0.0).then_inc(S("wide_zero"), 1)
            pool.memset(gt[:, :, :], 0.0).then_inc(S("wide_zero"), 1)
            pool.wait_ge(S("cst_in"), 16)
            pool.wait_ge(S("ms_done"), 1)
            power(6, 4, 2).then_inc(S("rstd_done"), 1)
            for n in range(LEAD):
                if n not in VEC_LO:
                    low_part(pool, n, "lo_pool")
            advance(56)

            def split_y(p, y0):
                pool.wait_ge(S("y_hi"), p + 1)
                pool.tensor_tensor(yT[:, y0:y0 + 2, 1, :], yf[:, :, :], yT[:, y0:y0 + 2, 0, :].bitcast(F32),
                                   ALU.subtract).then_inc(S("y_lo"), 1)

            def tail(p):
                if p and PAIRS[p - 1][0] == "gdn":
                    split_y(p - 1, Y_BLOCK["gdn"] + 2 * PAIRS[p - 1][1])

            def rms_power(p):
                pool.wait_ge(S("o_ms"), p + 1)
                power(56, 52, 4).then_inc(S("o_pow"), 1)

            def mix_gdn(p, j, base):
                U = {k: base + v for k, v in U_GDN.items()}
                advance(base + 1)
                advance(U["gram"])
                pool.wait_ge(S("g_norm"), j + 1)
                power(32, 24, 8).then_inc(S("g_pow"), 1)
                tail(p)
                advance(U["o"])
                rms_power(p)

            def mix_ret(p, j, base):
                U = {k: base + v for k, v in U_RET.items()}
                advance(base + 1)
                tail(p)
                advance(U["o"])
                rms_power(p)
                advance(U["tr"])
                split_y(p, Y_BLOCK["ret"] + 2 * j)

            def mix_moba(p, j, base):
                U = {k: base + v for k, v in U_MOBA.items()}
                advance(U["nrm"])
                pool.wait_ge(S("m_norm"), j + 1)
                power(64, 80, 8).then_inc(S("m_pow"), 1)
                advance(U["o"])
                split_y(p, Y_BLOCK["moba"] + 2 * j)

            advance(128)
            for p, (kind, j) in enumerate(PAIRS):
                {"gdn": mix_gdn, "ret": mix_ret, "moba": mix_moba}[kind](p, j, 128 * (p + 1))
                advance(128 * (p + 2))
            advance(64 * GROUPS)

        @block.vector
        def _(dve):
            pos = [0]

            def evacuate(g, s):
                dve.wait_ge(S("ev_lo_done"), 4 * g + s + 1)
                if g == 0 and s == 0:
                    dve.wait_ge(S("pad_zero"), 1)
                dve.tensor_tensor(raw[:, g % 2, s, PAD:], pj[s][:, 0:T], ev_lo[:, s, :], ALU.add).then_inc(S("evac"), 1)

            def residual(n):
                g, c = n // 2, n % 2
                dve.wait_ge(S("out_psum"), n + 1)
                dve.wait_ge(S(f"xr_in{n % 3}"), 16 * (n // 3 + 1))
                if n >= 2:
                    dve.wait_ge(S(f"out_sent{n % 2}"), 16 * (n // 2))
                dve.tensor_tensor(sq[:, n % 2].rearrange("p c k t -> p (c k t)"), pj[n % 4][:, :],
                                  cv[:, (n % 3) * 512:(n % 3 + 1) * 512], ALU.add).then_inc(S("out_ready"), 1)

            def advance(u):
                for v in range(pos[0], min(u, 64 * GROUPS)):
                    if evacuated(v):
                        evacuate(*evacuated(v))
                    n = v // UPT + LEAD
                    if v % UPT == LOW_AT and n < TILES and n % TPH in VEC_LO:
                        low_part(dve, n, "lo_vec")
                    if v > 64 * HEADS and v % 64 == 0:
                        residual(2 * (v // 64 - HEADS) - 2)
                        residual(2 * (v // 64 - HEADS) - 1)
                pos[0] = max(pos[0], u)

            for c in range(C):
                dve.wait_ge(S(f"x{c}_in"), 16)
                if c:
                    dve.wait_ge(S("ss_vec"), c)
                dve.scalar_tensor_tensor(junk_v, x_sb[:, c, 1024:], 1.0, x_sb[:, c, 1024:], ALU.mult, ALU.mult,
                                         accum_out=sm[:, 2 * c + 1:2 * c + 2]).then_inc(S("ss_vec"), 1)
            dve.wait_ge(S("ss_vec"), C)
            dve.wait_ge(S("ss_act"), C)
            halves = sm[:, 0:4].rearrange("p (c h) -> p c h", h=2)
            dve.tensor_tensor(sm[:, 8:10], halves[:, :, 0], halves[:, :, 1], ALU.add).then_inc(S("ss2"), 1)
            dve.wait_ge(S("ss2"), 1)
            dve.tensor_scalar(sm[:, 4:6], sm[:, 8:10], 1.0 / D, EPS, ALU.mult, ALU.add).then_inc(S("ms_done"), 1)
            dve.wait_ge(S("norm_psum"), 1)
            dve.tensor_copy(pcol[:, 0:KC], mx[3][:, 0:KC]).then_inc(S("norm_cols"), 1)
            dve.wait_ge(S("rstd_psum"), 1)
            dve.tensor_copy(rstd_row, mx[3][:, 0:T]).then_inc(S("rstd_row"), 1)
            dve.wait_ge(S("rstd_row"), 1)

            def norm_two(b):
                dve.wait_ge(S("hT_psum"), b + 1)
                if b >= 6:
                    dve.wait_ge(S("h_hi"), 2 * (b - 6) + 2)
                    dve.wait_ge(S("h_lo"), 2 * (b - 6) + 2)
                dve.tensor_tensor(h_tmp(2 * b, 2).rearrange("p (k t) -> p k t", k=2),
                                  (pj + mx)[b][:, :].rearrange("p (k t) -> p k t", k=2),
                                  rstd_row.unsqueeze(1).broadcast_to([P, 2, T]), ALU.mult).then_inc(S("h_tmp"), 1)

            norm_two(0)
            norm_two(1)
            for k in range(KC):
                dve.wait_ge(S("h_hi"), k + 1)
                dve.scalar_tensor_tensor(hT[:, k, 1, :], h_tmp(k), pcol[:, R_NORM + k:R_NORM + k + 1],
                                         hT[:, k, 0, :].bitcast(F32), ALU.mult, ALU.subtract).then_inc(S("h_lo"), 1)
                if k == 1:
                    low_part(dve, 1, "lo_vec")
                if k % 2 and k // 2 + 2 < KC // 2:
                    norm_two(k // 2 + 2)
                if k % 2:
                    advance(UPT * (k // 2))
            dve.wait_ge(S("wab_hi_done"), 1)
            dve.tensor_tensor(wab_lo[:, :, :], wab[:, :, :], wab_hi[:, :, :].bitcast(F32), ALU.subtract).then_inc(S("wab_lo_done"), 1)
            advance(66)

            dve.wait_ge(S("params_psum"), 1)
            dve.tensor_copy(pcol[:, KC:], mx[2][:, KC:R_ROWS]).then_inc(S("param_cols"), 1)
            dve.wait_ge(S("param_cols"), 1)
            dve.wait_ge(S("cst_in"), 16)
            dve.wait_ge(S("cst_in2"), 16)
            steps = [0]

            def link(ins):
                steps[0] += 1
                ins.then_inc(S("ab_step"), 1)
                dve.wait_ge(S("ab_step"), steps[0])

            def over_chunks(ap):
                return ap.unsqueeze(1).broadcast_to([P, C, GDN])

            dve.wait_ge(S("bias_in"), 2 * 16)
            dve.wait_ge(S("tanh_b"), 1)
            link(dve.tensor_tensor(ab[:, A_Z], mx[1][:, 0:2 * AB].rearrange("p (c h) -> p c h", c=C)[:, :, 0:GDN],
                                   over_chunks(bias[:, 1, :]), ALU.add))
            link(dve.tensor_scalar(ab[:, A_T1], ab[:, A_Z], -1.0, None, ALU.mult))
            dve.tensor_tensor(ab[:, A_T1], ab[:, A_Z], ab[:, A_T1], ALU.min).then_inc(S("negabs_z"), 1)
            dve.wait_ge(S("exp_z"), 1)
            dve.tensor_scalar(ab[:, A_U], ab[:, A_E], 1.0, None, ALU.add).then_inc(S("one_plus"), 1)
            dve.wait_ge(S("one_plus"), 1)
            link(dve.tensor_scalar(ab[:, A_T2], ab[:, A_U], 1.0, None, ALU.subtract))
            link(dve.tensor_tensor(ab[:, A_T2], ab[:, A_E], ab[:, A_T2], ALU.subtract))
            link(dve.reciprocal(ab[:, A_T3], ab[:, A_U]))
            link(dve.tensor_tensor(ab[:, A_T2], ab[:, A_T2], ab[:, A_T3], ALU.mult))
            dve.wait_ge(S("ln_u"), 1)
            link(dve.tensor_tensor(ab[:, A_T2], ab[:, A_T2], ab[:, A_L], ALU.add))
            link(dve.scalar_tensor_tensor(ab[:, A_T2], ab[:, A_Z], 0.0, ab[:, A_T2], ALU.max, ALU.add))
            dve.wait_ge(S("expa_done"), 1)
            link(dve.tensor_tensor(ab[:, A_T2], ab[:, A_T2], over_chunks(sm[:, 16:16 + GDN]), ALU.mult))
            dve.tensor_scalar(ab[:, A_G], ab[:, A_T2], -1.0, None, ALU.mult).then_inc(S("g_done"), 1)
            dve.wait_ge(S("tanh_b"), 1)
            dve.tensor_scalar(ab[:, A_BETA], ab[:, A_TB], 0.5, 0.5, ALU.mult, ALU.add).then_inc(S("beta_done"), 1)
            advance(90)
            dve.wait_ge(S("cum_psum"), 1)
            link(dve.tensor_copy(ab[:, A_GC], mx[1][:, 0:C * GDN].rearrange("p (c h) -> p c h", c=C)))
            link(dve.tensor_scalar(ab[:, A_NGC], ab[:, A_GC], -1.0, None, ALU.mult))
            dve.tensor_tensor(ab[:, A_T2, 0, :], mx[1][:, C * GDN:(C + 1) * GDN], ab[:, A_GC, 0, :], ALU.subtract).then_inc(S("gc_done"), 1)
            dve.wait_ge(S("egc_done"), 2)
            link(dve.tensor_scalar(ab[:, A_NEGC], ab[:, A_EGC], -1.0, None, ALU.mult))
            dve.tensor_tensor(sm[:, 22:23], pcol[:, R_Q:R_Q + 1], pcol[:, R_K:R_K + 1], ALU.mult).then_inc(S("wqk0"), 1)
            dve.wait_ge(S("wqk0"), 1)
            dve.tensor_scalar(sm[:, 23:24], sm[:, 22:23], SCALE, None, ALU.mult).then_inc(S("wqk"), 1)
            dve.tensor_scalar(sm[:, 96:96 + RET + 1], pcol[:, R_RET:R_GDN + 1], 0.5, None, ALU.mult).then_inc(S("halfw"), 1)

            def gate(p):
                dve.wait_ge(S("tanh_z"), p + 1)
                dve.scalar_tensor_tensor(zg[:, :, :], zg[:, :, :], 1.0, raw[:, :, 3, PAD:], ALU.add, ALU.mult).then_inc(S("zg"), 1)

            def mean_square(p, gdn):
                dve.wait_ge(S("os_sq"), 4 * p + 4)
                if gdn:
                    dve.tensor_tensor(sm[:, 104:108], sm[:, 48:52], sm[:, 112:116], ALU.mult).then_inc(S("o_ms0"), 1)
                    dve.wait_ge(S("o_ms0"), p + 1)
                    dve.tensor_scalar(sm[:, 52:56], sm[:, 104:108], EPS, None, ALU.add).then_inc(S("o_ms"), 1)
                else:
                    dve.tensor_scalar(sm[:, 52:56], sm[:, 48:52], 1.0 / P, EPS, ALU.mult, ALU.add).then_inc(S("o_ms"), 1)

            def norm_out(p, gdn):
                dve.wait_ge(S("o_pow"), p + 1)
                if gdn:
                    dve.tensor_tensor(sm[:, 60:64], sm[:, 56:60], sm[:, 108:112], ALU.mult).then_inc(S("o_fac"), 1)
                else:
                    dve.tensor_copy(sm[:, 60:64], sm[:, 56:60]).then_inc(S("o_fac"), 1)
                dve.wait_ge(S("o_fac"), p + 1)
                dve.tensor_tensor(on[:, :, :, :].rearrange("p h c e -> p (h c) e"), os_[:, :, :, :].rearrange("p h c e -> p (h c) e"),
                                  sm[:, 60:64].unsqueeze(2).broadcast_to([P, 4, P]), ALU.mult).then_inc(S("on"), 1)

            def tail(p):
                if p and PAIRS[p - 1][0] == "gdn":
                    gated_pair(p - 1, mx[2], [sm[:, 96 + RET:97 + RET]] * 2)

            def tail_norm(p):
                if p and PAIRS[p - 1][0] == "gdn":
                    norm_out(p - 1, True)

            th3, cv3 = (b[:, :].rearrange("p (h s t) -> p h s t", h=2, s=3) for b in (th, cv))

            def conv(p, j, h, s):
                dst = cv3[:, h, {0: 1, 1: 0, 2: 2}[s]]
                dve.wait_ge(S("evac"), 8 * p + 4 * h + s + 1)
                for k in range(CONV):
                    tap = pcol[:, R_CONV + k * 3 * GDN + s * GDN + 2 * j + h:][:, 0:1]
                    if k == 0:
                        ins = dve.tensor_scalar(dst, raw[:, h, s, 0:T], tap, None, ALU.mult)
                    else:
                        conv_step[0] += 1
                        ins.then_inc(S("conv_step"), 1)
                        dve.wait_ge(S("conv_step"), conv_step[0])
                        ins = dve.scalar_tensor_tensor(dst, raw[:, h, s, k:k + T], tap, dst, ALU.mult, ALU.add)
                return ins

            def conv_kq(p, j, h):
                conv(p, j, h, 1).then_inc(S("conv_one"), 1)
                conv(p, j, h, 0).then_inc(S("conv_kq"), 1)

            def silu_kq(j, h):
                dve.wait_ge(S("tanh_kq"), 2 * j + h + 1)
                for i in range(2):
                    dve.scalar_tensor_tensor(kq[:, h, :, i, :], th3[:, h, i].rearrange("p (c t) -> p c t", c=C), 1.0,
                                             cv3[:, h, i].rearrange("p (c t) -> p c t", c=C), ALU.add, ALU.mult).then_inc(S("silu_kq"), 1)

            def decay_clip(j):
                dve.wait_ge(S("gcb"), j + 1)
                for n in range(4):
                    h, c = n // 2, n % 2
                    dve.tensor_scalar(dd[:, n, :], mx[3][:, n * P:(n + 1) * P], ab[:, A_NGC, c, 2 * j + h:2 * j + h + 1], 0.0,
                                      ALU.add, ALU.min).then_inc(S("clip_done"), 1)

            def decay_mask(j):
                dve.wait_ge(S("exp_decay"), j + 1)
                dve.tensor_tensor(er[:, :, :], ee[:, :, :], upper.unsqueeze(1).broadcast_to([P, 4, P]), ALU.mult).then_inc(S("er1"), 1)

            def mix_gdn(p, j, base):
                U = {k: base + v for k, v in U_GDN.items()}

                advance(base + 1)
                conv(p, j, 1, 1).then_inc(S("conv_one"), 1)
                conv(p, j, 1, 0).then_inc(S("conv_kq"), 1)
                tail_norm(p)
                silu_kq(j, 1)
                conv(p, j, 1, 2).then_inc(S("conv_v"), 1)
                advance(base + 9)
                dve.wait_ge(S("tanh_v"), j + 1)
                dve.scalar_tensor_tensor(vT[:, :, :], th3[:, :, 2], 1.0, cv3[:, :, 2], ALU.add, ALU.mult).then_inc(S("silu_v"), 1)
                advance(U["gram"])
                dve.wait_ge(S("gram"), j + 1)
                dve.tensor_scalar(sm[:, 24:32], mx[3][:, 2 * P:2 * P + 8], 4 * EPS, None, ALU.add).then_inc(S("g_norm"), 1)
                tail(p)
                dve.wait_ge(S("g_pow"), j + 1)
                rk = sm[:, 32:40].rearrange("p (n k) -> p n k", k=2)[:, :, 0]
                rq = sm[:, 32:40].rearrange("p (n k) -> p n k", k=2)[:, :, 1]
                nk = sm[:, 24:32].rearrange("p (n k) -> p n k", k=2)[:, :, 0]
                dve.wait_ge(S("er1"), j + 1)
                dve.tensor_tensor(ee[:, :, :], er[:, :, :], rk.unsqueeze(2).broadcast_to([P, 4, P]), ALU.mult).then_inc(S("er2"), 1)
                dve.scalar_tensor_tensor(sm[:, 40:44], nk, 0.5, rk, ALU.mult, ALU.mult).then_inc(S("g_scalars"), 1)
                dve.tensor_scalar(sm[:, 108:112], rq, SCALE, None, ALU.mult).then_inc(S("g_q"), 1)
                dve.wait_ge(S("g_q"), j + 1)
                dve.scalar_tensor_tensor(sm[:, 112:116], sm[:, 108:112], 1.0 / P, sm[:, 108:112], ALU.mult, ALU.mult).then_inc(S("g_q2"), 1)
                for h in range(2):
                    dve.tensor_tensor(sm[:, 44 + 2 * h:46 + 2 * h], rk[:, 2 * h:2 * h + 2], ab[:, A_BETA, :, 2 * j + h], ALU.mult).then_inc(S("g_b"), 1)
                dve.wait_ge(S("g_b"), 2 * j + 2)
                dve.wait_ge(S("er2"), j + 1)
                for n in range(4):
                    at = (n % 2) * T
                    dve.scalar_tensor_tensor(mT[:, n, :], mx[n // 2][:, at:at + P], sm[:, 44 + n:45 + n], ee[:, n, :],
                                             ALU.mult, ALU.mult).then_inc(S("mt"), 1)
                dve.wait_ge(S("mt"), 4 * j + 4)
                for a in (0, HALF):
                    first = cst[a:a + HALF, K_FIRST_T:K_FIRST_T + HALF].unsqueeze(1).broadcast_to([HALF, 4, HALF])
                    dve.tensor_tensor(gs[a:a + HALF, :, :], mT[a:a + HALF, :, a:a + HALF], first, ALU.mult).then_inc(S("gs_pairs"), 1)
                dve.wait_ge(S("gs_pairs"), 2 * j + 2)
                stack = cst[:, K_STACK:K_STACK + HALF].unsqueeze(1).broadcast_to([P, 4, HALF])
                dve.tensor_tensor(gs[:, :, :], gs[:, :, :], stack, ALU.add).then_inc(S("gs"), 1)

                def turn(l):
                    dve.wait_ge(S("gs"), 6 * j + l + 1)
                    dve.transpose(gm[:, :, :].rearrange("p n c -> p (n c)"), gs[:, :, :].rearrange("p n c -> p (n c)")).then_inc(S("gm"), 1)

                turn(0)
                for h in range(2):
                    dve.tensor_tensor(aT[:, 2 * h:2 * h + 2, :], mx[h][:, :].rearrange("p (c k t) -> p c k t", c=C, k=2)[:, :, 1],
                                      ee[:, 2 * h:2 * h + 2, :], ALU.mult).then_inc(S("at"), 1)
                for h in range(2):
                    dve.scalar_tensor_tensor(sm[:, 116 + h:117 + h], rk[:, 2 * h:2 * h + 1], ab[:, A_ELAST, 0, 2 * j + h:2 * j + h + 1],
                                             sm[:, 44 + 2 * h:45 + 2 * h], ALU.mult, ALU.mult).then_inc(S("g_el"), 1)
                gate(p)
                for l in range(1, LEVELS):
                    advance(U[f"x{l}"])
                    dve.wait_ge(S("x_psum"), (LEVELS - 1) * j + l)
                    mask = cst[:, K_LEVEL + (l - 1) * P:K_LEVEL + l * P].rearrange("p (a c) -> p a c", a=2)
                    dve.tensor_tensor(xs[:, :, :].rearrange("p n (a c) -> p n a c", a=2),
                                      stacked(mx[0]).unsqueeze(2).broadcast_to([P, 4, 2, HALF]),
                                      mask.unsqueeze(1).broadcast_to([P, 4, 2, HALF]), ALU.mult).then_inc(S("xs"), 1)
                    advance(U[f"y{l}"])
                    dve.wait_ge(S("y_psum"), (LEVELS - 1) * j + l)
                    if l < LEVELS - 1:
                        dve.tensor_tensor(gs[:, :, :], gs[:, :, :], stacked(mx[1]), ALU.subtract).then_inc(S("gs"), 1)
                        if l < 5:
                            turn(l)
                        if j + 1 < GDN // 2:
                            if l == 1:
                                decay_clip(j + 1)
                            elif l == 2:
                                decay_mask(j + 1)
                            elif l == 5:
                                conv(p + 1, j + 1, 0, 1).then_inc(S("conv_one"), 1)
                    else:
                        dve.tensor_scalar(gt[0:HALF, :, HALF:P], stacked(mx[1])[0:HALF], -1.0, None, ALU.mult).then_inc(S("gt_done"), 1)
                        if j + 1 < GDN // 2:
                            conv(p + 1, j + 1, 0, 0).then_inc(S("conv_kq"), 1)
                advance(U["v0"])
                dve.wait_ge(S("v0_psum"), j + 1)
                dve.wait_ge(S("g_el"), 2 * j + 2)
                for h in range(2):
                    dve.tensor_scalar(v0s[:, h, :], mx[3][:, h * P:(h + 1) * P], sm[:, 116 + h:117 + h], None, ALU.mult).then_inc(S("v0s"), 1)
                advance(U["ks"])
                dve.wait_ge(S("ks_psum"), j + 1)
                dve.wait_ge(S("vr"), 4 * j + 4)
                for h in range(2):
                    dve.scalar_tensor_tensor(vr[:, 2 * h + 1, :], mx[0][:, h * P:(h + 1) * P], ab[:, A_NEGC, 1, 2 * j + h:2 * j + h + 1],
                                             vr[:, 2 * h + 1, :], ALU.mult, ALU.add).then_inc(S("vr1"), 1)
                if j + 1 < GDN // 2:
                    conv(p + 1, j + 1, 0, 2).then_inc(S("conv_v"), 1)
                advance(U["o"])
                dve.wait_ge(S("os"), p + 1)
                for h in range(2):
                    ins = dve.scalar_tensor_tensor(os_[:, h, 1, :], mx[0][:, (2 + h) * P:(3 + h) * P], ab[:, A_EGC, 1, 2 * j + h:2 * j + h + 1],
                                                   os_[:, h, 1, :], ALU.mult, ALU.add)
                ins.then_inc(S("os_full"), 1)
                if j + 1 < GDN // 2:
                    silu_kq(j + 1, 0)
                mean_square(p, True)

            def gated_pair(p, psum, weights):
                dve.wait_ge(S("otr"), p + 1)
                dve.wait_ge(S("zg"), p + 1)
                for h in range(2):
                    ins = dve.scalar_tensor_tensor(yf[:, h, :], psum[:, h * T:(h + 1) * T], weights[h], zg[:, h, :], ALU.mult, ALU.mult)
                    if h == 1:
                        ins.then_inc(S("yf_done"), 1)

            def mix_ret(p, j, base):
                U = {k: base + v for k, v in U_RET.items()}
                advance(base + 1)
                tail_norm(p)
                tail(p)
                gate(p)
                advance(U["gram"])
                dve.wait_ge(S("r_gram"), j + 1)
                for h in range(2):
                    dec = cst[:, K_DECAY + (2 * j + h) * P:K_DECAY + (2 * j + h + 1) * P].unsqueeze(1).broadcast_to([P, C, P])
                    dve.tensor_tensor(aT[:, 2 * h:2 * h + 2, :], mx[0][:, h * T:(h + 1) * T].rearrange("p (c t) -> p c t", c=C), dec,
                                      ALU.mult).then_inc(S("r_at"), 1)
                advance(U["o"])
                dve.wait_ge(S("os"), p + 1)
                for h in range(2):
                    ins = dve.scalar_tensor_tensor(os_[:, h, 1, :], mx[3][:, (2 + h) * P:(3 + h) * P],
                                                   cst[:, K_QDEC + 2 * j + h:K_QDEC + 2 * j + h + 1],
                                                   os_[:, h, 1, :], ALU.mult, ALU.add)
                ins.then_inc(S("os_full"), 1)
                mean_square(p, False)
                norm_out(p, False)
                advance(U["tr"])
                gated_pair(p, mx[0], [sm[:, 96 + 2 * j + h:97 + 2 * j + h] for h in range(2)])

            def mix_moba(p, j, base):
                U = {k: base + v for k, v in U_MOBA.items()}
                lg = th[:, 0:6 * P].rearrange("p (h c) -> p h c", h=2)
                pr = th[:, 6 * P:12 * P].rearrange("p (h c) -> p h c", h=2)
                advance(base + 1)
                gate(p)
                advance(U["nrm"])
                dve.wait_ge(S("m_nrm"), j + 1)
                dve.tensor_scalar(sm[:, 80:88], mx[3][:, 0:8], 1.0 / P, EPS, ALU.mult, ALU.add).then_inc(S("m_norm"), 1)
                advance(U["bc"])
                dve.wait_ge(S("m_bc"), j + 1)
                for h in range(2):
                    dve.scalar_tensor_tensor(vT[:, h, :], raw[:, h, 1, PAD:], sm[:, 23:24], mx[2][:, h * T:(h + 1) * T], ALU.mult, ALU.mult).then_inc(S("knT"), 1)
                advance(U["score"])
                for h in range(2):
                    head = 2 * j + h
                    slope = 2.0 ** (-8.0 * (head + 1) / MOBA)
                    dve.wait_ge(S("m_lg"), 4 * j + 2 * h + 2)
                    dve.scalar_tensor_tensor(lg[:, h, :], cst[:, K_DIST:K_DIST + 3 * P], slope, lg[:, h, :], ALU.mult, ALU.add).then_inc(S("m_alibi"), 1)
                    dve.wait_ge(S("m_alibi"), 2 * j + h + 1)
                    for c in range(C):
                        a, b = (0, P) if c == 0 else (P, 3 * P)
                        n = 2 * h + c
                        dve.tensor_reduce(sm[:, 72 + n:73 + n], lg[:, h, a:b], AX.X, ALU.max, negate=True).then_inc(S("m_max"), 1)
                for h in range(2):
                    dve.wait_ge(S("m_exp"), 4 * j + 2 * h + 2)
                    dve.reciprocal(sm[:, 88 + 2 * h:90 + 2 * h], sm[:, 76 + 2 * h:78 + 2 * h]).then_inc(S("m_rec"), 1)
                    dve.wait_ge(S("m_rec"), 2 * j + h + 1)
                    for c in range(C):
                        a, b = (0, P) if c == 0 else (P, 3 * P)
                        n = 2 * h + c
                        dve.tensor_scalar(pr[:, h, a:b], pr[:, h, a:b], sm[:, 88 + n:89 + n], None, ALU.mult).then_inc(S("m_prob"), 1)
                advance(U["pt"])
                dve.wait_ge(S("pt_psum"), 2 * j + 2)
                dve.tensor_copy(kq[:, 1].rearrange("p c k t -> p (c k t)")[:, 0:3 * P], mx[0][:, 0:3 * P]).then_inc(S("pt_v"), 1)
                advance(U["o"])
                dve.wait_ge(S("otr"), p + 1)
                dve.wait_ge(S("zg"), p + 1)
                dve.scalar_tensor_tensor(yf[:, :, :], mx[1][:, :].rearrange("p (h t) -> p h t", h=2), 0.5, zg[:, :, :],
                                         ALU.mult, ALU.mult).then_inc(S("yf_done"), 1)

            conv_step = [0]
            conv_kq(0, 0, 0)
            conv(0, 0, 0, 2).then_inc(S("conv_v"), 1)
            advance(U_FIRST)
            decay_clip(0)
            decay_mask(0)
            silu_kq(0, 0)
            advance(128)
            for p, (kind, j) in enumerate(PAIRS):
                {"gdn": mix_gdn, "ret": mix_ret, "moba": mix_moba}[kind](p, j, 128 * (p + 1))
                advance(128 * (p + 2))
            advance(64 * GROUPS)
            residual(6)
            residual(7)

        @block.tensor
        def _(pe):
            pos = [0]

            def unit(v):
                g, t = v // 64, v // UPT
                n, r = t, v % UPT
                if r == 0:
                    wait_lo(pe, n)
                hi = w_hi[:, n % NSPLIT, :].rearrange("p (k c) -> p k c", k=TK)
                lo = w_lo[:, n % NSPLIT, :].rearrange("p (k c) -> p k c", k=TK)
                if g < HEADS:
                    s, k = r // TK, r % TK
                    kc = (t % TPH) * TK + k
                    first, last = kc == 0, kc == KC - 1
                    if first and g == 0:
                        pe.wait_ge(S("h_tmp"), s + 1)
                    if g == 0 and s == 0:
                        pe.wait_ge(S("h_lo"), kc + 1)
                    if first and g:
                        pe.wait_ge(S("evac"), 4 * (g - 1) + s + 1)
                    cols = slice(s * P, (s + 1) * P)

                    def low(**kw):
                        return pe.matmul(pj[s][:, 0:T], lo[:, k, cols], hT[:, kc, 0, :], **kw)

                    def high(**kw):
                        return pe.matmul(pj[s][:, :], hi[:, k, cols], hT[:, kc].rearrange("p a t -> p (a t)"), **kw)

                    if last:
                        low(start=False, stop=False)
                        ins = high(start=False, stop=True)
                        ins.then_inc(S("proj_done"), 1)
                    else:
                        high(start=first, stop=False)
                        ins = low(start=False, stop=False)
                else:
                    k, c, half = r // 4, r // 2 % 2, r % 2
                    kc = (t % TPH) * TK + k
                    first, last = kc == 0, kc == KC - 1
                    bank = pj[(2 * (g - HEADS) + c) % 4]
                    if first and half == 0:
                        if g == HEADS:
                            pe.wait_ge(S("evac"), 4 * HEADS)
                        elif g >= HEADS + 2:
                            pe.wait_ge(S("out_ready"), 2 * (g - HEADS - 2) + c + 1)
                    if kc % 2 == 0 and half == 0 and c == 0 and g == HEADS:
                        block_ready(kc // 2)
                    tok = slice(c * P, (c + 1) * P)
                    if half == 0:
                        ins = pe.matmul(bank[:, :], yT[:, kc, 0, tok], hi[:, k, :], start=first, stop=False)
                    else:
                        pe.matmul(bank[:, :], yT[:, kc, 1, tok], hi[:, k, :], start=False, stop=False)
                        ins = pe.matmul(bank[:, :], yT[:, kc, 0, tok], lo[:, k, :], start=False, stop=last)
                        if last:
                            ins.then_inc(S("out_psum"), 1)
                if r == UPT - 1 and not last:
                    ins.then_inc(S("tile_used"), 1)

            def block_ready(b):
                order = {"ret": 3, "gdn": 0, "moba": 5}
                kind = "ret" if b < 2 else "gdn" if b < 5 else "moba"
                p = order[kind] + b - {"ret": 0, "gdn": 2, "moba": 5}[kind]
                pe.wait_ge(S("y_lo"), p + 1)

            def stream(u):
                for v in range(pos[0], min(u, 64 * GROUPS)):
                    unit(v)
                pos[0] = max(pos[0], u)

            def x_blocks(b, c):
                for k in range(2 * b, 2 * b + 2):
                    ins = pe.transpose((pj + mx)[b][:, k % 2 * T + c * P:k % 2 * T + (c + 1) * P],
                                       x_sb[:, c, k * P:(k + 1) * P], ident)
                return ins

            pe.wait_ge(S("cst_in"), 16)
            pe.wait_ge(S("x0_in"), 16)
            for b in range(7):
                x_blocks(b, 0)
            pe.wait_ge(S("x1_in"), 16)
            for b in range(7):
                x_blocks(b, 1).then_inc(S("hT_psum"), 1)
            pe.wait_ge(S("norm_in"), 16)
            pe.transpose(mx[3][:, 0:KC], prow[0:KC, :], ident[0:KC, 0:KC]).then_inc(S("norm_psum"), 1)
            pe.wait_ge(S("norm_cols"), 1)
            pe.wait_ge(S("rstd_done"), 1)
            for c in range(C):
                ins = pe.matmul(mx[3][:, c * P:(c + 1) * P], sm[:, 6 + c:7 + c].broadcast_to([P, P]), ident, start=True, stop=True)
            ins.then_inc(S("rstd_psum"), 1)
            pe.wait_ge(S("rstd_row"), 1)
            x_blocks(7, 0)
            x_blocks(7, 1).then_inc(S("hT_psum"), 1)

            stream(64)
            pe.wait_ge(S("h_tmp"), 8)
            pe.wait_ge(S("wab_lo_done"), 1)
            for k in range(KC):
                pe.matmul(mx[0][0:AB, :], wab_hi[:, k, :], hT[:, k].rearrange("p a t -> p (a t)"), start=k == 0, stop=False)
                ins = pe.matmul(mx[0][0:AB, 0:T], wab_lo[:, k, :], hT[:, k, 0, :], start=False, stop=k == KC - 1)
            ins.then_inc(S("abt_psum"), 1)
            pe.wait_ge(S("param_in"), 5 * 16)
            pe.transpose(mx[2][:, 0:R_ROWS], prow[:, :], ident[0:R_ROWS, 0:R_ROWS]).then_inc(S("params_psum"), 1)
            stream(68)
            pe.wait_ge(S("abt_done"), 1)
            for c in range(C):
                for a in range(2):
                    ins = pe.matmul(mx[1][:, c * AB:(c + 1) * AB], abT[:, a * T + c * P:a * T + (c + 1) * P], ident[0:AB, 0:AB],
                                    start=a == 0, stop=a == 1)
            ins.then_inc(S("ab_psum"), 1)
            stream(88)
            pe.wait_ge(S("g_done"), 1)
            for c in range(C):
                pe.matmul(mx[1][:, c * GDN:(c + 1) * GDN], upper, ab[:, A_G, c, :], start=True, stop=True)
            pe.matmul(mx[1][:, C * GDN:(C + 1) * GDN], ones, ab[:, A_G, 0, :], start=True, stop=True).then_inc(S("cum_psum"), 1)

            def decay_rows(j):
                if j:
                    pe.wait_ge(S("ktok"), j)
                for n in range(4):
                    h, c = n // 2, n % 2
                    ins = pe.matmul(mx[3][:, n * P:(n + 1) * P], ab[:, A_GC, c, 2 * j + h:2 * j + h + 1].broadcast_to([P, P]), ident,
                                    start=True, stop=True)
                ins.then_inc(S("gcb"), 1)

            def mix_gdn(p, j, base):
                U = {k: base + v for k, v in U_GDN.items()}
                tail(p, base)
                stream(U["gram"])
                if j == 0:
                    pe.wait_ge(S("clip_done"), 4)
                pe.wait_ge(S("silu_kq"), 4 * j + 4)
                for h in range(2):
                    for c in range(C):
                        pe.matmul(mx[h][:, c * T:(c + 1) * T], kq[:, h, c, 0, :], kq[:, h, c].rearrange("p k t -> p (k t)"),
                                  start=True, stop=True)
                    pe.transpose(mx[3][:, h * P:(h + 1) * P], kq[:, h, 0, 0, :], ident)
                pe.wait_ge(S("sq"), 2 * j + 2)
                for h in range(2):
                    for c in range(C):
                        for i in range(2):
                            at = 2 * P + 4 * h + 2 * c + i
                            ins = pe.matmul(mx[3][:, at:at + 1], sq[:, h, c, i, :], ones[:, 0:1], start=True, stop=True)
                ins.then_inc(S("gram"), 1)
                stream(U["vtok"])
                pe.wait_ge(S("silu_v"), j + 1)
                if p:
                    pe.wait_ge(S("yf_done"), p)
                for n in range(4):
                    ins = pe.transpose(mx[2][:, n * P:(n + 1) * P], vT[:, n // 2, (n % 2) * P:(n % 2 + 1) * P], ident)
                ins.then_inc(S("vtok"), 1)
                def col(bank, n):
                    return bank[:, n * HALF:(n + 1) * HALF]

                for l in range(1, LEVELS):
                    stream(U[f"x{l}"])
                    if l < LEVELS - 1:
                        pe.wait_ge(S("gm"), 5 * j + l)
                    else:
                        pe.wait_ge(S("gm_last"), j + 1)
                    if l == 1:
                        pe.wait_ge(S("mb"), 2 * j + 2)
                        pe.wait_ge(S("at"), 2 * j + 2)
                    for n in range(4):
                        if l < LEVELS - 1:
                            ins = pe.matmul(col(mx[0], n), mB[:, n, :], gm[:, n, :], start=True, stop=True)
                        else:
                            ins = pe.matmul(col(mx[0], n), mT[0:HALF, n, :], gm[0:HALF, n, :], start=True, stop=True)
                    ins.then_inc(S("x_psum"), 1)
                    stream(U[f"y{l}"])
                    pe.wait_ge(S("xs"), (LEVELS - 1) * j + l)
                    pe.wait_ge(S("gs"), 6 * j + l)
                    for n in range(4):
                        ins = pe.matmul(col(mx[1], n), xs[:, n, :], gs[:, n, :], start=True, stop=True)
                    ins.then_inc(S("y_psum"), 1)
                    if l == 1 and j + 1 < GDN // 2:
                        decay_rows(j + 1)
                    if l == LEVELS - 2:
                        stream(U[f"t{l}"])
                        pe.wait_ge(S("vr"), 4 * j + 4)
                        pe.wait_ge(S("gs"), 6 * (j + 1))
                        for n in range(4):
                            ins = pe.matmul(col(mx[2], n)[0:HALF], gs[0:HALF, n, :], ident[0:HALF, 0:HALF], start=True, stop=True)
                        ins.then_inc(S("gtr"), 1)
                stream(U["v0"])
                pe.wait_ge(S("gt_wide"), 2 * j + 2)
                pe.wait_ge(S("gt_done"), j + 1)
                pe.wait_ge(S("clip_done"), 4 * min(j + 2, GDN // 2))
                pe.wait_ge(S("ktok"), j + 1)
                for h in range(2):
                    ins = pe.matmul(mx[3][:, h * P:(h + 1) * P], gt[:, 2 * h, :], vr[:, 2 * h, :], start=True, stop=True)
                ins.then_inc(S("v0_psum"), 1)
                stream(U["s1"])
                pe.wait_ge(S("v0s"), 2 * j + 2)
                for h in range(2):
                    ins = pe.matmul(mx[1][:, h * P:(h + 1) * P], ktok[:, h, :], v0s[:, h, :], start=True, stop=True)
                ins.then_inc(S("s1_psum"), 1)
                stream(U["ks"])
                pe.wait_ge(S("st"), j + 1)
                for h in range(2):
                    pe.matmul(mx[0][:, h * P:(h + 1) * P], kq[:, h, 1, 0, :], st[:, h, :], start=True, stop=True)
                    ins = pe.matmul(mx[0][:, (2 + h) * P:(3 + h) * P], kq[:, h, 1, 1, :], st[:, h, :], start=True, stop=True)
                ins.then_inc(S("ks_psum"), 1)
                stream(U["v1"])
                pe.wait_ge(S("vr1"), 2 * j + 2)
                for h in range(2):
                    ins = pe.matmul(mx[1][:, (2 + h) * P:(3 + h) * P], gt[:, 2 * h + 1, :], vr[:, 2 * h + 1, :], start=True, stop=True)
                ins.then_inc(S("v1_psum"), 1)
                stream(U["o"])
                pe.wait_ge(S("v0"), 2 * j + 2)
                pe.wait_ge(S("v1"), 2 * j + 2)
                for h in range(2):
                    for c, v in enumerate((v0, v1)):
                        ins = pe.matmul(mx[2][:, (2 * h + c) * P:(2 * h + c + 1) * P], aT[:, 2 * h + c, :], v[:, h, :], start=True, stop=True)
                ins.then_inc(S("o_psum"), 1)

            def tail(p, base):
                if p and PAIRS[p - 1][0] == "gdn":
                    stream(base + U_TAIL)
                    out_transposes(p - 1, mx[2])

            def out_transposes(p, bank):
                pe.wait_ge(S("on"), p + 1)
                for n in range(4):
                    ins = pe.transpose(bank[:, n * P:(n + 1) * P], on[:, n // 2, n % 2, :], ident)
                ins.then_inc(S("otr"), 1)

            def mix_ret(p, j, base):
                U = {k: base + v for k, v in U_RET.items()}
                tail(p, base)
                stream(U["gram"])
                pe.wait_ge(S("evac"), 8 * p + 8)
                pe.wait_ge(S("yf_done"), p)
                for h in range(2):
                    for c in range(C):
                        n = 2 * h + c
                        ins = pe.matmul(mx[0][:, n * P:(n + 1) * P], chunk_in(h, 1, c), chunk_in(h, 0, c), start=True, stop=True)
                ins.then_inc(S("r_gram"), 1)
                for h in range(2):
                    for c in range(C):
                        n = 2 * h + c
                        pe.transpose(mx[1][:, n * P:(n + 1) * P], chunk_in(h, 2, c), ident)
                    ins = pe.transpose(mx[2][:, h * P:(h + 1) * P], chunk_in(h, 1, 0), ident)
                ins.then_inc(S("r_vtok"), 1)
                stream(U["s1"])
                pe.wait_ge(S("r_vr"), j + 1)
                pe.wait_ge(S("r_ktok"), 2 * j + 2)
                for h in range(2):
                    ins = pe.matmul(mx[3][:, h * P:(h + 1) * P], ktok[:, h, :], vr[:, 2 * h, :], start=True, stop=True)
                ins.then_inc(S("r_s1_psum"), 1)
                stream(U["qs"])
                pe.wait_ge(S("r_st"), j + 1)
                for h in range(2):
                    pe.matmul(mx[3][:, (2 + h) * P:(3 + h) * P], chunk_in(h, 0, 1), st[:, h, :], start=True, stop=True)
                pe.wait_ge(S("r_at"), 2 * j + 2)
                for n in range(4):
                    ins = pe.matmul(mx[2][:, n * P:(n + 1) * P], aT[:, n, :], vr[:, n, :], start=True, stop=True)
                ins.then_inc(S("o_psum"), 1)
                stream(U["tr"])
                out_transposes(p, mx[0])

            def mix_moba(p, j, base):
                U = {k: base + v for k, v in U_MOBA.items()}
                pr = th[:, 6 * P:12 * P].rearrange("p (h c) -> p h c", h=2)
                pt = [kq[:, h].rearrange("p c k t -> p (c k t)") for h in range(2)]
                stream(U["nrm"])
                pe.wait_ge(S("evac"), 8 * p + 8)
                pe.wait_ge(S("yf_done"), p)
                pe.wait_ge(S("m_sq"), 2 * j + 2)
                sqv = sq[:, :, :, :, :].rearrange("p h c k t -> p (h c k) t")
                for n in range(8):
                    ins = pe.matmul(mx[3][:, n:n + 1], sqv[:, n, :], ones[:, 0:1], start=True, stop=True)
                ins.then_inc(S("m_nrm"), 1)
                for n in range(4):
                    ins = pe.transpose(mx[1][:, n * P:(n + 1) * P], chunk_in(n // 2, 2, n % 2), ident)
                ins.then_inc(S("m_vtok"), 1)
                stream(U["bc"])
                pe.wait_ge(S("m_pow"), j + 1)
                for n in range(4):
                    at = 64 + 4 * (n // 2) + 2 + n % 2
                    ins = pe.matmul(mx[2][:, n * P:(n + 1) * P], sm[:, at:at + 1].broadcast_to([P, P]), ident, start=True, stop=True)
                ins.then_inc(S("m_bc"), 1)
                stream(U["score"])
                pe.wait_ge(S("knT"), 2 * j + 2)
                for h in range(2):
                    bank = mx[(0, 3)[h]]
                    pe.matmul(bank[:, 0:P], chunk_in(h, 0, 0), vT[:, h, 0:P], start=True, stop=True)
                    ins = pe.matmul(bank[:, P:3 * P], chunk_in(h, 0, 1), vT[:, h, :], start=True, stop=True)
                ins.then_inc(S("score"), 1)
                stream(U["pt"])
                for h in range(2):
                    pe.wait_ge(S("m_prob"), 4 * j + 2 * h + 2)
                    for i in range(3):
                        ins = pe.transpose(mx[(2, 0)[h]][:, i * P:(i + 1) * P], pr[:, h, i * P:(i + 1) * P], ident)
                    ins.then_inc(S("pt_psum"), 1)
                stream(U["o"])
                pe.wait_ge(S("m_vr"), j + 1)
                pe.wait_ge(S("pt_a"), j + 1)
                pe.wait_ge(S("pt_v"), j + 1)
                for h in range(2):
                    pe.matmul(mx[1][:, h * T:(h + 1) * T], vr[:, 2 * h, :], pt[h][:, 0:T], start=True, stop=False)
                    ins = pe.matmul(mx[1][:, h * T + P:(h + 1) * T], vr[:, 2 * h + 1, :], pt[h][:, T:T + P], start=False, stop=True)
                ins.then_inc(S("otr"), 1)

            stream(U_FIRST)
            pe.wait_ge(S("gc_done"), 1)
            decay_rows(0)
            stream(128)
            for p, (kind, j) in enumerate(PAIRS):
                {"gdn": mix_gdn, "ret": mix_ret, "moba": mix_moba}[kind](p, j, 128 * (p + 1))
                stream(128 * (p + 2))
            stream(64 * GROUPS)


_INS = ['x', 'norm_w', 'w_in', 'conv_w', 'a_log', 'dt_bias', 'ret_norm_w', 'gdn_norm_w', 'q_norm_w', 'k_norm_w',
        'w_out']


def kernel(**inputs):
    import numpy as _np
    import concourse.bacc as _bacc
    from concourse import mybir as _mybir
    from concourse.bass_utils import run_bass_kernel_spmd as _run

    nc = _bacc.Bacc("TRN2", target_bir_lowering=False, num_devices=1)
    arrays, args = {}, []
    for name in _INS:
        a = _np.ascontiguousarray(inputs[name])
        arrays[f"in_{name}_dram"] = a
        args.append(nc.dram_tensor(f"in_{name}_dram", a.shape, _mybir.dt.from_np(a.dtype), kind="ExternalInput").ap())
    arrays["table_dram"] = constants()
    args.append(nc.dram_tensor("table_dram", (P, K_COLS), F32, kind="ExternalInput").ap())
    args.append(nc.dram_tensor("out_0_dram", (1, T, D), F32, kind="ExternalOutput").ap())
    layer(nc, *args)
    r = _run(nc, [arrays], core_ids=[0])
    return r.results[0]["out_0_dram"]
```
